# Optimizing a Trainium2 kernel written in Bass

```python
import numpy as np
import jax
import jax.numpy as jnp
from jax import lax
import math

D_MODEL = 1024
BATCH = 1
SEQ = 256
DEPTH = 1

D_RNN = 1344
RNN_BLOCKS = 16
RNN_BLOCK_W = D_RNN // RNN_BLOCKS
RNN_CONV_W = 4
LRU_C = 8.0
N_HEADS = 16
N_KV = 4
HEAD_DIM = 64
GROUP = N_HEADS // N_KV
CMP_LEN = 32
CMP_STRIDE = 16
CMP_HIDDEN = 128
SEL_LEN = 64
N_SELECT = 16
WINDOW = 512
Q_BLOCK = 64
D_FF = 3 * D_MODEL
FFN_CONV_W = 3
EPS = 1e-6
NEG = -1e30
FORCE = 1e6


def rms_norm(x, g):
    x32 = x.astype(jnp.float32)
    y = x32 * lax.rsqrt(jnp.mean(x32 * x32, axis=-1, keepdims=True) + EPS)
    return (y * g.astype(jnp.float32)).astype(x.dtype)

def causal_dwconv(x, w, b):
    k = w.shape[0]
    y = lax.conv_general_dilated(x, w[:, None, :].astype(x.dtype), window_strides=(1,),
                                 padding=[(k - 1, 0)], dimension_numbers=('NWC', 'WIO', 'NWC'),
                                 feature_group_count=x.shape[-1])
    return y + b.astype(x.dtype)

def masked_softmax(s, mask):
    p = jax.nn.softmax(jnp.where(mask, s, NEG), axis=-1)
    return p * mask

def rg_lru(x, w_a, b_a, w_x, b_x, lam):
    bsz, s, _ = x.shape
    xb = x.reshape(bsz, s, RNN_BLOCKS, RNN_BLOCK_W)
    r = jax.nn.sigmoid(jnp.einsum('bsnc,ncd->bsnd', xb, w_a).reshape(bsz, s, D_RNN) + b_a)
    i = jax.nn.sigmoid(jnp.einsum('bsnc,ncd->bsnd', xb, w_x).reshape(bsz, s, D_RNN) + b_x)
    log_a = LRU_C * r.astype(jnp.float32) * jax.nn.log_sigmoid(lam.astype(jnp.float32))
    a = jnp.exp(log_a)
    u = jnp.sqrt(-jnp.expm1(2.0 * log_a)) * (i * x).astype(jnp.float32)

    def combine(lhs, rhs):
        a1, b1 = lhs
        a2, b2 = rhs
        return a1 * a2, a2 * b1 + b2

    _, h = lax.associative_scan(combine, (a, u), axis=1)
    return h.astype(x.dtype)

def compress(kv, pe, w1, w2):
    bsz, s, g, hd = kv.shape
    nc = (s - CMP_LEN) // CMP_STRIDE + 1
    pos = np.arange(nc)[:, None] * CMP_STRIDE + np.arange(CMP_LEN)[None, :]
    blocks = kv[:, pos] + pe[None, None, :, None, :]
    blocks = blocks.transpose(0, 3, 1, 2, 4).reshape(bsz, g, nc, CMP_LEN * hd)
    return jax.nn.gelu(blocks @ w1) @ w2

def overlap_matrix(nc, ns):
    i = np.arange(nc)[:, None]
    j = np.arange(ns)[None, :]
    lo = np.maximum(i * CMP_STRIDE, j * SEL_LEN)
    hi = np.minimum(i * CMP_STRIDE + CMP_LEN, (j + 1) * SEL_LEN)
    return jnp.asarray(np.maximum(hi - lo, 0) / CMP_STRIDE, dtype=jnp.float32)

def nsa(q, kc, vc, ks, vs, kw, vw, gates, q_norm_g, k_cmp_norm_g, k_slc_norm_g, k_win_norm_g,
        cmp_pe_k, cmp_w1_k, cmp_w2_k, cmp_pe_v, cmp_w1_v, cmp_w2_v):
    bsz, s, _ = q.shape
    f32 = jnp.float32
    scale = HEAD_DIM ** -0.5

    def heads(t, n):
        return t.reshape(bsz, s, n, HEAD_DIM)

    qh = rms_norm(heads(q, N_HEADS), q_norm_g)
    qh = qh.reshape(bsz, s, N_KV, GROUP, HEAD_DIM).transpose(0, 2, 3, 1, 4)
    k_cmp = rms_norm(compress(heads(kc, N_KV), cmp_pe_k, cmp_w1_k, cmp_w2_k), k_cmp_norm_g)
    v_cmp = compress(heads(vc, N_KV), cmp_pe_v, cmp_w1_v, cmp_w2_v)
    nc = k_cmp.shape[2]
    ns = s // SEL_LEN
    k_slc = rms_norm(heads(ks, N_KV), k_slc_norm_g).transpose(0, 2, 1, 3).reshape(bsz, N_KV, ns, SEL_LEN, HEAD_DIM)
    v_slc = heads(vs, N_KV).transpose(0, 2, 1, 3).reshape(bsz, N_KV, ns, SEL_LEN, HEAD_DIM)
    pad = ((0, 0), (0, 0), (WINDOW, 0), (0, 0))
    k_win = jnp.pad(rms_norm(heads(kw, N_KV), k_win_norm_g).transpose(0, 2, 1, 3), pad)
    v_win = jnp.pad(heads(vw, N_KV).transpose(0, 2, 1, 3), pad)
    g = jax.nn.sigmoid(gates).reshape(bsz, s, N_KV, GROUP, 3).transpose(0, 2, 3, 1, 4)
    overlap = overlap_matrix(nc, ns)
    cmp_end = np.arange(nc) * CMP_STRIDE + CMP_LEN - 1
    n_top = min(N_SELECT, ns)
    gather = jax.vmap(jax.vmap(lambda blk, ix: blk[ix]))
    jb = jnp.arange(ns)

    def block(qi):
        st = qi * Q_BLOCK
        t = st + jnp.arange(Q_BLOCK)
        qb = lax.dynamic_slice_in_dim(qh, st, Q_BLOCK, axis=3)
        gb = lax.dynamic_slice_in_dim(g, st, Q_BLOCK, axis=3)
        sc = jnp.einsum('bgrqd,bgcd->bgrqc', qb, k_cmp).astype(f32) * scale
        p_cmp = masked_softmax(sc, cmp_end[None, :] <= t[:, None])
        o_cmp = jnp.einsum('bgrqc,bgcd->bgrqd', p_cmp.astype(v_cmp.dtype), v_cmp)
        imp = jnp.einsum('bgrqc,cn->bgqn', p_cmp, overlap)
        cur = t // SEL_LEN
        causal_b = jb[None, :] <= cur[:, None]
        forced = (jb[None, :] == 0) | (jb[None, :] == cur[:, None]) | (jb[None, :] == cur[:, None] - 1)
        rank = jnp.where(causal_b, jnp.where(forced, FORCE, imp), -FORCE)
        _, idx = lax.top_k(rank, n_top)
        kg = gather(k_slc, idx)
        vg = gather(v_slc, idx)
        kpos = idx[..., None] * SEL_LEN + jnp.arange(SEL_LEN)
        ok = (idx <= cur[:, None])[..., None] & (kpos <= t[:, None, None])
        sc = jnp.einsum('bgrqd,bgqnld->bgrqnl', qb, kg).astype(f32) * scale
        p = masked_softmax(sc.reshape(bsz, N_KV, GROUP, Q_BLOCK, n_top * SEL_LEN),
                           ok.reshape(bsz, N_KV, 1, Q_BLOCK, n_top * SEL_LEN))
        o_slc = jnp.einsum('bgrqm,bgqmd->bgrqd', p.astype(vg.dtype),
                           vg.reshape(bsz, N_KV, Q_BLOCK, n_top * SEL_LEN, HEAD_DIM))
        kwb = lax.dynamic_slice_in_dim(k_win, st, WINDOW + Q_BLOCK, axis=2)
        vwb = lax.dynamic_slice_in_dim(v_win, st, WINDOW + Q_BLOCK, axis=2)
        kp = st - WINDOW + jnp.arange(WINDOW + Q_BLOCK)
        okw = (kp[None, :] <= t[:, None]) & (kp[None, :] > t[:, None] - WINDOW) & (kp[None, :] >= 0)
        sc = jnp.einsum('bgrqd,bgkd->bgrqk', qb, kwb).astype(f32) * scale
        pw = masked_softmax(sc, okw)
        o_win = jnp.einsum('bgrqk,bgkd->bgrqd', pw.astype(vwb.dtype), vwb)
        return gb[..., 0:1] * o_cmp + gb[..., 1:2] * o_slc + gb[..., 2:3] * o_win

    out = lax.map(block, jnp.arange(s // Q_BLOCK))
    return out.transpose(1, 0, 4, 2, 3, 5).reshape(bsz, s, N_HEADS * HEAD_DIM)

def first_inputs(seed: int = 0) -> dict:
    key = jax.random.key(seed)
    k = jax.random.split(key, 28)

    def nrm(kk, shape, scale):
        return jax.random.normal(kk, shape, jnp.float32) * scale

    d, hd = D_MODEL, HEAD_DIM
    n_in = 2 * D_RNN + N_HEADS * hd + 6 * N_KV * hd + 3 * N_HEADS + 2 * d
    u = jax.random.uniform(k[9], (D_RNN,), jnp.float32, 0.9, 0.999)
    sg = u ** (1.0 / LRU_C)
    lam = jnp.log(sg) - jnp.log1p(-sg)
    return {
        'x': nrm(k[0], (BATCH, SEQ, d), 1.0),
        'norm1_g': 1.0 + nrm(k[1], (d,), 0.02),
        'w_in': nrm(k[2], (d, n_in), d ** -0.5),
        'rnn_conv_w': nrm(k[3], (RNN_CONV_W, D_RNN), RNN_CONV_W ** -0.5),
        'rnn_conv_b': nrm(k[4], (D_RNN,), 0.02),
        'rg_w_a': nrm(k[5], (RNN_BLOCKS, RNN_BLOCK_W, RNN_BLOCK_W), RNN_BLOCK_W ** -0.5),
        'rg_b_a': nrm(k[6], (D_RNN,), 0.02),
        'rg_w_x': nrm(k[7], (RNN_BLOCKS, RNN_BLOCK_W, RNN_BLOCK_W), RNN_BLOCK_W ** -0.5),
        'rg_b_x': nrm(k[8], (D_RNN,), 0.02),
        'lru_lambda': lam,
        'w_rnn_out': nrm(k[10], (D_RNN, d), D_RNN ** -0.5),
        'q_norm_g': 1.0 + nrm(k[11], (hd,), 0.02),
        'k_cmp_norm_g': 1.0 + nrm(k[12], (hd,), 0.02),
        'k_slc_norm_g': 1.0 + nrm(k[13], (hd,), 0.02),
        'k_win_norm_g': 1.0 + nrm(k[14], (hd,), 0.02),
        'cmp_pe_k': nrm(k[15], (CMP_LEN, hd), 0.1),
        'cmp_w1_k': nrm(k[16], (CMP_LEN * hd, CMP_HIDDEN), (CMP_LEN * hd) ** -0.5),
        'cmp_w2_k': nrm(k[17], (CMP_HIDDEN, hd), CMP_HIDDEN ** -0.5),
        'cmp_pe_v': nrm(k[18], (CMP_LEN, hd), 0.1),
        'cmp_w1_v': nrm(k[19], (CMP_LEN * hd, CMP_HIDDEN), (CMP_LEN * hd) ** -0.5),
        'cmp_w2_v': nrm(k[20], (CMP_HIDDEN, hd), CMP_HIDDEN ** -0.5),
        'w_attn_out': nrm(k[21], (N_HEADS * hd, d), (N_HEADS * hd) ** -0.5),
        'w_out': nrm(k[22], (d, d), d ** -0.5),
        'norm2_g': 1.0 + nrm(k[23], (d,), 0.02),
        'w_up': nrm(k[24], (d, 2 * D_FF), d ** -0.5),
        'ffn_conv_w': nrm(k[25], (FFN_CONV_W, 2 * D_FF), FFN_CONV_W ** -0.5),
        'ffn_conv_b': nrm(k[26], (2 * D_FF,), 0.02),
        'w_down': nrm(k[27], (D_FF, d), D_FF ** -0.5),
    }

def first_block(x, norm1_g, w_in, rnn_conv_w, rnn_conv_b, rg_w_a, rg_b_a, rg_w_x, rg_b_x, lru_lambda,
              w_rnn_out, q_norm_g, k_cmp_norm_g, k_slc_norm_g, k_win_norm_g, cmp_pe_k, cmp_w1_k, cmp_w2_k,
              cmp_pe_v, cmp_w1_v, cmp_w2_v, w_attn_out, w_out, norm2_g, w_up, ffn_conv_w, ffn_conv_b, w_down):
    kvw = N_KV * HEAD_DIM
    sizes = [D_RNN, D_RNN, N_HEADS * HEAD_DIM] + [kvw] * 6 + [3 * N_HEADS, D_MODEL, D_MODEL]
    splits = np.cumsum(sizes)[:-1].tolist()
    for _ in range(DEPTH):
        h = rms_norm(x, norm1_g)
        proj = h @ w_in
        (rx, rgate, q, kc, vc, ks, vs, kw, vw, nsa_g, mg_rnn, mg_attn) = jnp.split(proj, splits, axis=-1)
        hr = rg_lru(causal_dwconv(rx, rnn_conv_w, rnn_conv_b), rg_w_a, rg_b_a, rg_w_x, rg_b_x, lru_lambda)
        y_rnn = (hr * jax.nn.gelu(rgate)) @ w_rnn_out
        o = nsa(q, kc, vc, ks, vs, kw, vw, nsa_g, q_norm_g, k_cmp_norm_g, k_slc_norm_g, k_win_norm_g,
                cmp_pe_k, cmp_w1_k, cmp_w2_k, cmp_pe_v, cmp_w1_v, cmp_w2_v)
        y_attn = o @ w_attn_out
        x = x + (jax.nn.sigmoid(mg_rnn) * y_rnn + jax.nn.sigmoid(mg_attn) * y_attn) @ w_out
        up = causal_dwconv(rms_norm(x, norm2_g) @ w_up, ffn_conv_w, ffn_conv_b)
        gate, val = jnp.split(up, 2, axis=-1)
        x = x + (jax.nn.gelu(gate) * val) @ w_down
    return x


DEPTH_2 = 2

N_MIXERS = 4
N_HEADS_2 = D_MODEL // HEAD_DIM
ROPE_THETA = 10000.0
RMS_EPS = 1e-6
NEG_INF = -1e30
ATTN_QBLOCK = 128
MOBA_BLOCK = 256
MOBA_TOPK = 3
MOBA_QCHUNK = 32
MLA_HEADS = N_HEADS_2
MLA_Q_LORA = 3 * D_MODEL // 8
MLA_KV_LORA = D_MODEL // 4
MLA_NOPE = HEAD_DIM
MLA_ROPE = HEAD_DIM // 2
MLA_V = HEAD_DIM
DIL_GROUPS = ((128, 1), (512, 4), (2048, 16))
DIL_HEADS = N_HEADS_2
DIL_BLOCK = 128
SB_HEADS = N_HEADS_2
SB_QBLOCK = 128
D_FF_2 = ((8 * D_MODEL // 3 + 255) // 256) * 256
CONV_WIDTH = 3


def rms_norm_2(x, g):
    xf = x.astype(jnp.float32)
    y = xf * lax.rsqrt(jnp.mean(xf * xf, axis=-1, keepdims=True) + RMS_EPS)
    return (y * g.astype(jnp.float32)).astype(x.dtype)

def rope_tables(pos, dim):
    inv = ROPE_THETA ** (-jnp.arange(0, dim, 2, dtype=jnp.float32) / dim)
    ang = pos[:, None] * inv[None, :]
    return jnp.cos(ang), jnp.sin(ang)

def apply_rope(x, cos, sin):
    half = x.shape[-1] // 2
    x1, x2 = x[..., :half], x[..., half:]
    c = cos[None, :, None, :].astype(x.dtype)
    s = sin[None, :, None, :].astype(x.dtype)
    return jnp.concatenate([x1 * c - x2 * s, x2 * c + x1 * s], axis=-1)

def moba_attention(q, k, v):
    B, S, H, dh = q.shape
    scale = dh ** -0.5
    nb = -(-S // MOBA_BLOCK)
    sp = nb * MOBA_BLOCK
    padw = ((0, 0), (0, sp - S), (0, 0), (0, 0))
    qh = jnp.pad(q, padw).transpose(0, 2, 1, 3)
    kh = jnp.pad(k, padw).transpose(0, 2, 1, 3)
    vh = jnp.pad(v, padw).transpose(0, 2, 1, 3)
    kblk = kh.reshape(B, H, nb, MOBA_BLOCK, dh)
    vblk = vh.reshape(B, H, nb, MOBA_BLOCK, dh)
    kmean = jnp.mean(kblk.astype(jnp.float32), axis=3)
    topk = min(MOBA_TOPK, nb)
    bi = jnp.arange(B)[:, None, None, None]
    hi = jnp.arange(H)[None, :, None, None]
    blk_ids = jnp.arange(nb)

    def step(c):
        start = c * MOBA_QCHUNK
        blk = start // MOBA_BLOCK
        qc = lax.dynamic_slice_in_dim(qh, start, MOBA_QCHUNK, axis=2)
        qpos = start + jnp.arange(MOBA_QCHUNK)
        gate = jnp.einsum("bhqd,bhnd->bhqn", qc.astype(jnp.float32), kmean)
        gate = jnp.where(blk_ids < blk, gate, NEG_INF)
        _, gidx = lax.top_k(gate, topk)
        valid = gidx < blk
        ksel = kblk[bi, hi, gidx]
        vsel = vblk[bi, hi, gidx]
        s_sel = jnp.einsum("bhqd,bhqnkd->bhqnk", qc, ksel, preferred_element_type=jnp.float32) * scale
        s_sel = jnp.where(valid[..., None], s_sel, NEG_INF)
        s_sel = s_sel.reshape(B, H, MOBA_QCHUNK, topk * MOBA_BLOCK)
        kown = lax.dynamic_slice_in_dim(kh, blk * MOBA_BLOCK, MOBA_BLOCK, axis=2)
        vown = lax.dynamic_slice_in_dim(vh, blk * MOBA_BLOCK, MOBA_BLOCK, axis=2)
        s_own = jnp.einsum("bhqd,bhkd->bhqk", qc, kown, preferred_element_type=jnp.float32) * scale
        kpos = blk * MOBA_BLOCK + jnp.arange(MOBA_BLOCK)
        s_own = jnp.where(kpos[None, :] <= qpos[:, None], s_own, NEG_INF)
        p = jax.nn.softmax(jnp.concatenate([s_own, s_sel], axis=-1), axis=-1).astype(vh.dtype)
        p_own = p[..., :MOBA_BLOCK]
        p_sel = p[..., MOBA_BLOCK:].reshape(B, H, MOBA_QCHUNK, topk, MOBA_BLOCK)
        return (jnp.einsum("bhqk,bhkd->bhqd", p_own, vown)
                + jnp.einsum("bhqnk,bhqnkd->bhqd", p_sel, vsel))

    out = lax.map(step, jnp.arange(sp // MOBA_QCHUNK))
    out = out.transpose(1, 0, 3, 2, 4).reshape(B, sp, H, dh)
    return out[:, :S]

def moba_mixer(xn, w_qkv, w_o, cos, sin):
    B, S, _ = xn.shape
    qkv = (xn @ w_qkv).reshape(B, S, 3, N_HEADS_2, HEAD_DIM)
    q = apply_rope(qkv[:, :, 0], cos, sin)
    k = apply_rope(qkv[:, :, 1], cos, sin)
    o = moba_attention(q, k, qkv[:, :, 2])
    return o.reshape(B, S, N_HEADS_2 * HEAD_DIM) @ w_o

def causal_attention_blocked(q, k, v, scale):
    B, S, H, dk = q.shape
    dv = v.shape[-1]
    nq = S // ATTN_QBLOCK
    qb = q.reshape(B, nq, ATTN_QBLOCK, H, dk).transpose(1, 0, 2, 3, 4)
    key_pos = jnp.arange(S)

    def step(args):
        i, qi = args
        s = jnp.einsum("bqhd,bkhd->bhqk", qi, k, preferred_element_type=jnp.float32) * scale
        qpos = i * ATTN_QBLOCK + jnp.arange(ATTN_QBLOCK)
        s = jnp.where(key_pos[None, :] <= qpos[:, None], s, NEG_INF)
        p = jax.nn.softmax(s, axis=-1).astype(v.dtype)
        return jnp.einsum("bhqk,bkhd->bqhd", p, v)

    out = lax.map(step, (jnp.arange(nq), qb))
    return out.transpose(1, 0, 2, 3, 4).reshape(B, S, H, dv)

def mla_mixer(xn, w_in, q_norm, w_uq, kv_norm, w_ukv, w_o, cos_r, sin_r):
    B, S, _ = xn.shape
    c = xn @ w_in
    cq = rms_norm_2(c[..., :MLA_Q_LORA], q_norm)
    ckv = rms_norm_2(c[..., MLA_Q_LORA:MLA_Q_LORA + MLA_KV_LORA], kv_norm)
    kr = c[..., MLA_Q_LORA + MLA_KV_LORA:]
    qf = (cq @ w_uq).reshape(B, S, MLA_HEADS, MLA_NOPE + MLA_ROPE)
    q_rope = apply_rope(qf[..., MLA_NOPE:], cos_r, sin_r)
    kv = (ckv @ w_ukv).reshape(B, S, MLA_HEADS, MLA_NOPE + MLA_V)
    k_rope = jnp.broadcast_to(apply_rope(kr[:, :, None, :], cos_r, sin_r), (B, S, MLA_HEADS, MLA_ROPE))
    q = jnp.concatenate([qf[..., :MLA_NOPE], q_rope], axis=-1)
    k = jnp.concatenate([kv[..., :MLA_NOPE], k_rope], axis=-1)
    v = kv[..., MLA_NOPE:]
    o = causal_attention_blocked(q, k, v, (MLA_NOPE + MLA_ROPE) ** -0.5)
    return o.reshape(B, S, MLA_HEADS * MLA_V) @ w_o

def dilated_group_attention(q, k, v, window, dilation):
    B, S, H, dh = q.shape
    scale = dh ** -0.5
    span = window // dilation
    unit = DIL_BLOCK * dilation
    sp = -(-S // unit) * unit
    L = sp // dilation
    nb = L // DIL_BLOCK
    padw = ((0, 0), (0, sp - S), (0, 0), (0, 0))

    def to_blocks(t):
        t = jnp.pad(t, padw).reshape(B, L, dilation, H, dh).transpose(0, 3, 2, 1, 4)
        return t.reshape(B, H, dilation, nb, DIL_BLOCK, dh)

    def with_prev(t):
        prev = jnp.pad(t, ((0, 0), (0, 0), (0, 0), (1, 0), (0, 0), (0, 0)))[:, :, :, :-1]
        return jnp.concatenate([prev, t], axis=4)

    qb = to_blocks(q)
    kk = with_prev(to_blocks(k))
    vv = with_prev(to_blocks(v))
    s = jnp.einsum("bhrnqd,bhrnkd->bhrnqk", qb, kk, preferred_element_type=jnp.float32) * scale
    qi = jnp.arange(DIL_BLOCK)[:, None]
    kj = jnp.arange(2 * DIL_BLOCK)[None, :]
    dist = qi + DIL_BLOCK - kj
    key_sub = jnp.arange(nb)[:, None, None] * DIL_BLOCK - DIL_BLOCK + kj[None]
    mask = (dist >= 0)[None] & (dist <= span)[None] & (key_sub >= 0)
    s = jnp.where(mask, s, NEG_INF)
    lse = jax.nn.logsumexp(s, axis=-1)
    p = jnp.exp(s - lse[..., None]).astype(v.dtype)
    o = jnp.einsum("bhrnqk,bhrnkd->bhrnqd", p, vv)
    o = o.reshape(B, H, dilation, L, dh).transpose(0, 3, 2, 1, 4).reshape(B, sp, H, dh)[:, :S]
    lse = lse.reshape(B, H, dilation, L).transpose(0, 3, 2, 1).reshape(B, sp, H)[:, :S]
    return o, lse

def dilated_mixer(xn, w_qkv, w_o, cos, sin):
    B, S, _ = xn.shape
    G = len(DIL_GROUPS)
    qkv = (xn @ w_qkv).reshape(B, S, G, 3, DIL_HEADS, HEAD_DIM)
    outs, lses = [], []
    for g, (window, dilation) in enumerate(DIL_GROUPS):
        q = apply_rope(qkv[:, :, g, 0], cos, sin)
        k = apply_rope(qkv[:, :, g, 1], cos, sin)
        o, lse = dilated_group_attention(q, k, qkv[:, :, g, 2], window, dilation)
        outs.append(o)
        lses.append(lse)
    wts = jax.nn.softmax(jnp.stack(lses, axis=0), axis=0)
    o = jnp.einsum("gbsh,gbshd->bshd", wts, jnp.stack(outs, axis=0).astype(jnp.float32))
    return o.reshape(B, S, DIL_HEADS * HEAD_DIM).astype(xn.dtype) @ w_o

def stick_breaking_attention(q, k, v):
    B, S, H, dh = q.shape
    scale = dh ** -0.5
    nq = S // SB_QBLOCK
    qb = q.reshape(B, nq, SB_QBLOCK, H, dh).transpose(1, 0, 2, 3, 4)
    key_pos = jnp.arange(S)

    def step(args):
        i, qi = args
        z = jnp.einsum("bqhd,bkhd->bhqk", qi, k, preferred_element_type=jnp.float32) * scale
        qpos = i * SB_QBLOCK + jnp.arange(SB_QBLOCK)
        past = key_pos[None, :] < qpos[:, None]
        log_beta = jnp.where(past, jax.nn.log_sigmoid(z), NEG_INF)
        log_stay = jnp.where(past, jax.nn.log_sigmoid(-z), 0.0)
        after = jnp.concatenate([log_stay[..., 1:], jnp.zeros_like(log_stay[..., :1])], axis=-1)
        stay = lax.cumsum(after, axis=3, reverse=True)
        a = jnp.exp(log_beta + stay).astype(v.dtype)
        return jnp.einsum("bhqk,bkhd->bqhd", a, v)

    out = lax.map(step, (jnp.arange(nq), qb))
    return out.transpose(1, 0, 2, 3, 4).reshape(B, S, H, dh)

def stick_breaking_mixer(xn, w_qkv, w_o):
    B, S, _ = xn.shape
    qkv = (xn @ w_qkv).reshape(B, S, 3, SB_HEADS, HEAD_DIM)
    o = stick_breaking_attention(qkv[:, :, 0], qkv[:, :, 1], qkv[:, :, 2])
    return o.reshape(B, S, SB_HEADS * HEAD_DIM) @ w_o

def conv_ffn(xn, w_gate, conv_w, conv_b, w_up, w_down):
    S = xn.shape[1]
    g = xn @ w_gate
    gp = jnp.pad(g, ((0, 0), (CONV_WIDTH - 1, 0), (0, 0)))
    gc = conv_b + sum(conv_w[j] * gp[:, j:j + S] for j in range(CONV_WIDTH))
    h = jax.nn.gelu(gc, approximate=False) * (xn @ w_up)
    return h @ w_down

def _n_layers_of(kind):
    return len(range(kind, DEPTH_2, N_MIXERS))

def second_inputs(seed: int = 0) -> dict:
    key = jax.random.key(seed)
    ks = jax.random.split(key, 24)
    f32 = jnp.float32
    nA, nB, nC, nD = (_n_layers_of(m) for m in range(N_MIXERS))
    hd = N_HEADS_2 * HEAD_DIM

    def dense(k, shape, fan_in):
        return jax.random.normal(k, shape, f32) * (fan_in ** -0.5)

    def gain(k, shape):
        return 1.0 + 0.02 * jax.random.normal(k, shape, f32)

    return {
        "x": jax.random.normal(ks[0], (BATCH, SEQ, D_MODEL), f32),
        "norm_mix": gain(ks[1], (DEPTH_2, D_MODEL)),
        "norm_ffn": gain(ks[2], (DEPTH_2, D_MODEL)),
        "norm_final": gain(ks[3], (D_MODEL,)),
        "a_w_qkv": dense(ks[4], (nA, D_MODEL, 3 * hd), D_MODEL),
        "a_w_o": dense(ks[5], (nA, hd, D_MODEL), hd),
        "b_w_in": dense(ks[6], (nB, D_MODEL, MLA_Q_LORA + MLA_KV_LORA + MLA_ROPE), D_MODEL),
        "b_q_norm": gain(ks[7], (nB, MLA_Q_LORA)),
        "b_w_uq": dense(ks[8], (nB, MLA_Q_LORA, MLA_HEADS * (MLA_NOPE + MLA_ROPE)), MLA_Q_LORA),
        "b_kv_norm": gain(ks[9], (nB, MLA_KV_LORA)),
        "b_w_ukv": dense(ks[10], (nB, MLA_KV_LORA, MLA_HEADS * (MLA_NOPE + MLA_V)), MLA_KV_LORA),
        "b_w_o": dense(ks[11], (nB, MLA_HEADS * MLA_V, D_MODEL), MLA_HEADS * MLA_V),
        "c_w_qkv": dense(ks[12], (nC, D_MODEL, len(DIL_GROUPS) * 3 * DIL_HEADS * HEAD_DIM), D_MODEL),
        "c_w_o": dense(ks[13], (nC, DIL_HEADS * HEAD_DIM, D_MODEL), DIL_HEADS * HEAD_DIM),
        "d_w_qkv": dense(ks[14], (nD, D_MODEL, 3 * SB_HEADS * HEAD_DIM), D_MODEL),
        "d_w_o": dense(ks[15], (nD, SB_HEADS * HEAD_DIM, D_MODEL), SB_HEADS * HEAD_DIM),
        "ffn_w_gate": dense(ks[16], (DEPTH_2, D_MODEL, D_FF_2), D_MODEL),
        "ffn_conv_w": dense(ks[17], (DEPTH_2, CONV_WIDTH, D_FF_2), CONV_WIDTH),
        "ffn_conv_b": 0.02 * jax.random.normal(ks[18], (DEPTH_2, D_FF_2), f32),
        "ffn_w_up": dense(ks[19], (DEPTH_2, D_MODEL, D_FF_2), D_MODEL),
        "ffn_w_down": dense(ks[20], (DEPTH_2, D_FF_2, D_MODEL), D_FF_2),
    }

def second_block(x, norm_mix, norm_ffn, norm_final,
              a_w_qkv, a_w_o,
              b_w_in, b_q_norm, b_w_uq, b_kv_norm, b_w_ukv, b_w_o,
              c_w_qkv, c_w_o,
              d_w_qkv, d_w_o,
              ffn_w_gate, ffn_conv_w, ffn_conv_b, ffn_w_up, ffn_w_down):
    S = x.shape[1]
    pos = jnp.arange(S, dtype=jnp.float32)
    cos_h, sin_h = rope_tables(pos, HEAD_DIM)
    cos_r, sin_r = rope_tables(pos, MLA_ROPE)
    h = x
    for i in range(DEPTH_2):
        kind, j = i % N_MIXERS, i // N_MIXERS
        hn = rms_norm_2(h, norm_mix[i])
        if kind == 0:
            mix = moba_mixer(hn, a_w_qkv[j], a_w_o[j], cos_h, sin_h)
        elif kind == 1:
            mix = mla_mixer(hn, b_w_in[j], b_q_norm[j], b_w_uq[j], b_kv_norm[j], b_w_ukv[j], b_w_o[j], cos_r, sin_r)
        elif kind == 2:
            mix = dilated_mixer(hn, c_w_qkv[j], c_w_o[j], cos_h, sin_h)
        else:
            mix = stick_breaking_mixer(hn, d_w_qkv[j], d_w_o[j])
        h = h + mix.astype(h.dtype)
        f = conv_ffn(rms_norm_2(h, norm_ffn[i]), ffn_w_gate[i], ffn_conv_w[i], ffn_conv_b[i], ffn_w_up[i], ffn_w_down[i])
        h = h + f.astype(h.dtype)
    return rms_norm_2(h, norm_final)


def setup_inputs(seed=0):
    out = dict(first_inputs(seed))
    for name, value in second_inputs(seed + 1).items():
        if name != "x":
            out[name + "_2"] = value
    return out


def reference(
    x, norm1_g, w_in, rnn_conv_w, rnn_conv_b, rg_w_a, rg_b_a, rg_w_x, rg_b_x, lru_lambda,
    w_rnn_out, q_norm_g, k_cmp_norm_g, k_slc_norm_g, k_win_norm_g, cmp_pe_k, cmp_w1_k, cmp_w2_k,
    cmp_pe_v, cmp_w1_v, cmp_w2_v, w_attn_out, w_out, norm2_g, w_up, ffn_conv_w, ffn_conv_b,
    w_down, norm_mix_2, norm_ffn_2, norm_final_2, a_w_qkv_2, a_w_o_2, b_w_in_2, b_q_norm_2,
    b_w_uq_2, b_kv_norm_2, b_w_ukv_2, b_w_o_2, c_w_qkv_2, c_w_o_2, d_w_qkv_2, d_w_o_2,
    ffn_w_gate_2, ffn_conv_w_2, ffn_conv_b_2, ffn_w_up_2, ffn_w_down_2,
):
    x = first_block(
        x, norm1_g, w_in, rnn_conv_w, rnn_conv_b, rg_w_a, rg_b_a, rg_w_x, rg_b_x, lru_lambda,
        w_rnn_out, q_norm_g, k_cmp_norm_g, k_slc_norm_g, k_win_norm_g, cmp_pe_k, cmp_w1_k,
        cmp_w2_k, cmp_pe_v, cmp_w1_v, cmp_w2_v, w_attn_out, w_out, norm2_g, w_up, ffn_conv_w,
        ffn_conv_b, w_down,
    )
    return second_block(
        x, norm_mix_2, norm_ffn_2, norm_final_2, a_w_qkv_2, a_w_o_2, b_w_in_2, b_q_norm_2,
        b_w_uq_2, b_kv_norm_2, b_w_ukv_2, b_w_o_2, c_w_qkv_2, c_w_o_2, d_w_qkv_2, d_w_o_2,
        ffn_w_gate_2, ffn_conv_w_2, ffn_conv_b_2, ffn_w_up_2, ffn_w_down_2,
    )


_drawn_inputs = setup_inputs


def setup_inputs(seed=0):
    import zlib

    import numpy as np

    out = dict(_drawn_inputs(seed))
    spreads = {}
    factors = {'norm1_g': 5.21,
     'rg_b_a': 8.0,
     'rg_b_x': 8.0,
     'q_norm_g': 8.0,
     'k_cmp_norm_g': 8.0,
     'k_slc_norm_g': 8.0,
     'k_win_norm_g': 8.0,
     'cmp_pe_k': 8.0,
     'norm2_g': 3.007,
     'ffn_conv_b': 2.933,
     'norm_mix_2': 6.633,
     'norm_ffn_2': 3.029,
     'norm_final_2': 2.842,
     'b_q_norm_2': 8.0,
     'b_kv_norm_2': 8.0,
     'ffn_conv_b_2': 4.299}
    for name, (base, spread) in spreads.items():
        noise = np.random.default_rng([zlib.crc32(name.encode()), seed]).standard_normal(out[name].shape)
        drawn = base * np.exp(spread * noise) if base else spread * noise
        out[name] = jnp.asarray(drawn.astype(out[name].dtype))
    for name, factor in factors.items():
        out[name] = (out[name] * factor).astype(out[name].dtype)
    return out
```

```python
from contextlib import ExitStack

import numpy as np

import concourse.bass as bass
from concourse import mybir

F32 = mybir.dt.float32
F32R = mybir.dt.float32r
BF16 = mybir.dt.bfloat16
ALU = mybir.AluOpType
ACT = mybir.ActivationFunctionType
AX = mybir.AxisListType

P = 128
S = 256
TT = S // P
D = 1024
DT = D // P
D_RNN, RNN_BLOCKS = 1344, 16
BW = D_RNN // RNN_BLOCKS
RT = -(-D_RNN // P)
LRU_C = 8.0
NH, NKV, HD = 16, 4, 64
KVW = NKV * HD
CL, CS = 32, 16
NC = (S - CL) // CS + 1
FF0, FF2 = 3072, 2816
QL, KVL, ROPE = 384, 256, 32
EPS = 1e-6
NEG = -1e30

RAW = 3
RING = 6
BODY = 6


def gate_blocks():
    out = []
    for m in range(RT):
        lo = BW * (P * m // BW)
        hi = BW * (min(P * m + P - 1, D_RNN - 1) // BW + 1) - 1
        for gate in range(2):
            out += [(gate, m, k) for k in range(lo // P, hi // P + 1)]
    return out


GATES = gate_blocks()
FFN_BLOCKS = {0: FF0 // P, 1: FF2 // P, 2: FF2 // P}

STAGES = [("rgate", RT), ("kvc", 4), ("w1", 4), ("rx", RT), ("lru", -(-len(GATES) // 8)), ("v", 4),
          ("g", 1), ("k", 4), ("q", 8), ("yr", RT), ("mg", 16), ("ao", 8), ("wo", 8),
          ("ffn0", 3 * FFN_BLOCKS[0]),
          ("q1", 8), ("k1", 8), ("v1", 8), ("wo1", 8), ("ffn1", 3 * FFN_BLOCKS[1]),
          ("c2", 6), ("uq", 6), ("uk", 2), ("uv", 2), ("wo2", 8), ("ffn2", 3 * FFN_BLOCKS[2])]
BASE, N_CHUNKS = {}, 0
for _name, _n in STAGES:
    BASE[_name] = N_CHUNKS
    N_CHUNKS += _n
SIZE = dict(STAGES)



SMALL = [("ident", 128), ("mask", 128), ("cmpmask", TT * NC), ("rowok", TT), ("blk2", 2), ("ones", 2),
         ("eps", 2), ("c64", S), ("s64", S), ("rot64", P), ("c32", S), ("s32", S), ("rot32", P),
         ("norm", 7 * DT), ("rcw", 4 * RT), ("rcb", RT), ("rba", RT), ("rbx", RT), ("lam", RT),
         ("hg", 4), ("pek", 32), ("pev", 32), ("w2k", P), ("w2v", HD),
         ("fcw0", 6 * FFN_BLOCKS[0]), ("fcb0", 2 * FFN_BLOCKS[0]), ("fcw1", 3 * FFN_BLOCKS[1]),
         ("fcb1", FFN_BLOCKS[1]), ("fcw2", 3 * FFN_BLOCKS[2]), ("fcb2", FFN_BLOCKS[2]),
         ("ln2", 5)]
AT, N_SMALL = {}, 0
for _name, _n in SMALL:
    AT[_name] = (N_SMALL, _n)
    N_SMALL += _n

TILE_STAGES = [("rgate", RT, "act"), ("kvc", 4, "act"), ("rx", RT, "dve"), ("lru", 2 * RT, "act"),
               ("k", 4, "act"), ("q", 8, "act"), ("mg", 16, "act"), ("ao", 8, "dve"),
               ("q1", 8, "act"), ("k1", 8, "act"), ("c2", 6, "act"), ("uq", NH, "act"), ("uk", 8, "act")]
TILE0, TILE_OWNER = {}, []
for _name, _n, _who in TILE_STAGES:
    TILE0[_name] = len(TILE_OWNER)
    for _ in range(_n):
        TILE_OWNER.append((_who, sum(w == _who for w, _ in TILE_OWNER) + 1))
TILE_BANKS = 4


def lru_groups():
    out = []
    for n, (gate, m, k) in enumerate(GATES):
        if not out or out[-1][:2] != (gate, m):
            out.append((gate, m, []))
        out[-1][2].append((n, k))
    return out


LRU_GROUPS = lru_groups()


def build(nc, weight_stream, small_in, x_in, out):
    with ExitStack() as ctx:
        def sb(name, shape, dt=F32):
            return ctx.enter_context(nc.sbuf_tensor(name, shape, dt))

        def sem(name):
            return ctx.enter_context(nc.semaphore(name))

        w_raw = sb("w_raw", [P, RAW, D])
        w_high = sb("w_high", [P, RING, D], F32R)
        w_low = sb("w_low", [P, RING, D], F32R)
        small = sb("small", [P, N_SMALL])
        x = sb("x", [P, DT, S])
        h_high = sb("h_high", [P, DT, S], F32R)
        h_low = sb("h_low", [P, DT, S], F32R)
        r_high = sb("r_high", [P, RT, S], F32R)
        r_low = sb("r_low", [P, RT, S], F32R)
        pe_high = sb("pe_high", [P, 64], F32R)
        pe_low = sb("pe_low", [P, 64], F32R)
        ident_b = sb("ident_b", [P, P], BF16)
        mask_b = sb("mask_b", [P, P], BF16)
        stats = sb("stats", [P, 480])
        arena = sb("arena", [P, 22912])
        bank = [ctx.enter_context(nc.psum_tensor(f"bank{i}", [P, 512], F32)) for i in range(8)]
        acc = bank[4:8]

        def par(name, a=0, n=None):
            at, size = AT[name]
            return small[:, at + a:at + (size if n is None else a + n)]

        def tiles(at, n, w=S):
            return arena[:, at:at + n * w].rearrange("p (k t) -> p k t", t=w)

        ident = par("ident")
        blk2 = par("blk2")
        ones = par("ones", 0, 1)
        eps_col = par("eps", 0, 1)
        eps64_col = par("eps", 1, 1)

        squares = tiles(0, DT)
        x_gain = tiles(2048, DT)
        x_norm = tiles(4096, DT)
        gelu_gate = tiles(0, RT)
        conv = tiles(2816, RT)
        r_gate = tiles(5632, RT)
        i_gate = tiles(8448, RT)
        decay = tiles(11264, RT)
        kv2 = tiles(2816, 8)
        cmp_hid = arena[:, 11264:11384]
        cmp_kraw = arena[:, 11384:11444]
        cmp_ksq = arena[:, 11444:11504]
        cmp_hv = arena[:, 11520:12032].rearrange("p (g r c) -> p g r c", g=NKV, r=4)
        q0 = tiles(14080, DT)
        k0 = arena[:, 16128:20224].rearrange("p (b v g t) -> p b v g t", b=2, v=2, g=NKV)
        v0 = arena[:, 20224:21248].rearrange("p (b t c) -> p b t c", b=2, t=TT)
        cmp_v = arena[:, 21248:22272].rearrange("p (g c) -> p g c", g=NKV)
        cmp_k = arena[:, 22272:22392].rearrange("p (v n) -> p v n", v=2)
        head_sq = tiles(22400, 2)
        y_rnn = tiles(0, DT)
        o0 = arena[:, 2048:4096].rearrange("p (t h d) -> p t h d", t=TT, h=NH)
        merge = tiles(4096, 16)
        cmp_p = arena[:, 8192:9216].rearrange("p (t h c) -> p t h c", t=TT, h=NH)
        probs0 = tiles(9216, 3, 384)
        probs_t0 = tiles(10368, 2, 384)
        o_part = arena[:, 11136:11648].rearrange("p (t h d) -> p t h d", t=TT, h=4)
        cmp_s = arena[:, 11648:12128].rearrange("p (t h c) -> p t h c", t=TT, h=NH)
        cmp_pt = tiles(12288, 8, P)
        q1 = tiles(0, 8)
        k1 = arena[:, 2048:6144].rearrange("p (v k t) -> p v k t", v=2, k=8)
        v1 = arena[:, 6144:8192].rearrange("p (t c) -> p t c", t=TT)
        o1 = arena[:, 8192:10240].rearrange("p (t h d) -> p t h d", t=TT, h=NH)
        probs1 = tiles(10240, 3, 384)
        probs_t1 = tiles(11392, 2, 384)
        rope_in = tiles(12288, 2)
        rope_a = tiles(12800, 2)
        rope_b = tiles(13312, 2)
        q2 = tiles(0, NH)
        k2 = tiles(4096, NH)
        v2 = arena[:, 8192:10240].rearrange("p (t c) -> p t c", t=TT)
        o2 = arena[:, 10240:12288].rearrange("p (t h d) -> p t h d", t=TT, h=NH)
        probs2 = tiles(12288, 3, 384)
        probs_t2 = tiles(13440, 2, 384)
        c_raw = tiles(14336, 6)
        c_sq = tiles(15872, 5)
        c_norm = tiles(17152, 5)
        rope_a2 = tiles(18432, 2, 512)
        rope_b2 = tiles(19456, 2, 512)
        taps_g = tiles(20480, 2)
        taps_v = tiles(20992, 2)
        gelu_g = tiles(21504, 2)
        hidden = tiles(22016, 2)

        st_std = stats[:, 0:2]
        st_rstd = stats[:, 2:4]
        lru_k = stats[:, 16:16 + RT]
        lru_kn = stats[:, 32:32 + RT]
        lru_t = [stats[:, 48 + 12 * i:48 + 12 * i + RT] for i in range(4)]
        cmp_bias = stats[:, 96:98]
        cmp_std = stats[:, 98:99]
        cmp_rstd = stats[:, 99:100]
        head_std = stats[:, 100:148].rearrange("p (t e j) -> p t e j", t=TT, j=2)
        head_rstd = stats[:, 148:196].rearrange("p (t e j) -> p t e j", t=TT, j=2)
        nsa_gate = stats[:, 200:296].rearrange("p (t h b) -> p t h b", t=TT, b=3)
        neg_max = stats[:, 296:328].rearrange("p (h t) -> p h t", t=TT)
        sums = stats[:, 328:360].rearrange("p (t h) -> p t h", t=TT)
        weights_o = stats[:, 360:392].rearrange("p (t h) -> p t h", t=TT)
        cmp_max = stats[:, 392:424].rearrange("p (t h) -> p t h", t=TT)
        cmp_sum = stats[:, 424:456].rearrange("p (t h) -> p t h", t=TT)
        c_std = stats[:, 456:460]
        c_rstd = stats[:, 460:464]

        chunk_loaded = [sem(f"chunk_loaded{i}") for i in range(RAW)]
        high_ready = sem("high_ready")
        low_ready = sem("low_ready")
        chunk_used = sem("chunk_used")
        small_loaded = sem("small_loaded")
        x_loaded = sem("x_loaded")
        out_stored = sem("out_stored")
        consts_ready = sem("consts_ready")
        zeros_ready = sem("zeros_ready")
        fill_done = sem("fill_done")
        dve_step = sem("dve_step")
        act_step = sem("act_step")
        tile_free = {"act": sem("tile_read_act"), "dve": sem("tile_read_dve")}
        acc_read = sem("accumulator_banks_read")
        squares_ready = sem("squares_ready")
        sumsq_ready = sem("sumsq_ready")
        std_ready = sem("std_ready")
        rstd_ready = sem("rstd_ready")
        rstd_spread = sem("rstd_spread")
        norm_ready = sem("norm_ready")
        h_high_ready = sem("h_high_ready")
        h_low_ready = sem("h_low_ready")
        kv2_ready = sem("kv2_ready")
        r_high_ready = sem("r_high_ready")
        r_low_ready = sem("r_low_ready")
        pe_high_ready = sem("pe_high_ready")
        cmp_hid_ready = sem("cmp_hid_ready")
        cmp_hv_ready = sem("cmp_hv_ready")
        cmp_kv_ready = sem("cmp_kv_ready")
        cmp_sq_ready = sem("cmp_sq_ready")
        cmp_sumsq_ready = sem("cmp_sumsq_ready")
        cmp_std_ready = sem("cmp_std_ready")
        cmp_rstd_ready = sem("cmp_rstd_ready")
        cmp_spread = sem("cmp_spread")
        tap_ready = sem("first_tap_ready")
        decay_ready = sem("decay_ready")
        var_ready = sem("input_scale_squared_ready")
        scale_ready = sem("input_scale_ready")
        scan_ready = sem("scan_ready")
        gated_ready = sem("gated_scan_ready")
        head_sq_ready = sem("head_squares_ready")
        head_sumsq_done = sem("head_sumsq_done")
        head_std_ready = sem("head_std_ready")
        head_rstd_ready = sem("head_rstd_ready")
        head_spread = sem("head_spread")
        head_normed = sem("head_normed")
        scores_ready = sem("scores_ready")
        max_ready = sem("max_ready")
        probs_ready = sem("probs_ready")
        probs_turned = sem("probs_turned")
        probs_copied = sem("probs_copied")
        pv_done = sem("pv_done")
        o_read = sem("o_read")
        cmp_scores = sem("cmp_scores")
        cmp_shifted = sem("cmp_shifted")
        cmp_probs = sem("cmp_probs")
        cmp_turned = sem("cmp_turned")
        cmp_copied = sem("cmp_copied")
        cmp_pv = sem("cmp_pv")
        cmp_done = sem("cmp_done")
        o_turned = sem("o_turned")
        z_ready = sem("merged_ready")
        rope_turned = sem("rope_turned")
        rope_done = sem("rope_done")
        c_sq_ready = sem("latent_squares_ready")
        c_sumsq = sem("latent_sumsq_ready")
        c_std_ready = sem("latent_std_ready")
        c_rstd_ready = sem("latent_rstd_ready")
        c_spread = sem("latent_rstd_spread")
        c_normed = sem("latent_normed")
        k2_ready = sem("mla_keys_ready")
        tap_g = sem("ffn_first_tap_gate")
        tap_g2 = sem("ffn_second_tap_gate")
        conv_g = sem("ffn_conv_gate")
        tap_v = sem("ffn_first_tap_value")
        tap_v2 = sem("ffn_second_tap_value")
        conv_v = sem("ffn_conv_value")
        gelu_ready = sem("ffn_gelu")
        hidden_ready = sem("ffn_hidden")
        hid_high = sem("ffn_hidden_high")
        hid_low = sem("ffn_hidden_low")

        FFN_STEP0 = {0: 0, 1: FFN_BLOCKS[0], 2: FFN_BLOCKS[0] + FFN_BLOCKS[1]}
        CONV_V0 = FFN_BLOCKS[0]
        ACC_V, ACC_YR, ACC_WO, ACC_FFN0, ACC_V1, ACC_WO1, ACC_FFN1, ACC_V2, ACC_WO2, ACC_FFN2 = range(10)
        R_CMP, R_CONV, R_SCAN = 0, 1, 1 + RT
        R_O = [1 + 2 * RT + DT * n for n in range(3)]
        H_N = {0: 0, 1: 4 + 8, 2: 16, 3: 20, 4: 24, 5: 28 + 5}
        H_Z, H_C = 4, 28

        def f(ap):
            return ap.bitcast(F32)

        block = ctx.enter_context(nc.Block())

        def par2(name, n):
            return small[:, AT[name][0]:AT[name][0] + n]

        def tile_read(eng, stage, i):
            who, n = TILE_OWNER[TILE0[stage] + i]
            eng.wait_ge(tile_free[who], n)

        def pieces(ap, p):
            return ap[:, 2 * p:2 * p + 2, :]

        def lru_posts(eng, split, post):
            at = 0
            for q in range(SIZE["lru"]):
                c = BASE["lru"] + q
                eng.wait_ge(chunk_used, c + 1)
                while at < len(LRU_GROUPS) and LRU_GROUPS[at][2][-1][0] // 8 <= q:
                    post(at, *LRU_GROUPS[at][:2])
                    at += 1
                split(c + RING)

        @block.sync
        def _(sp):
            def load(c, turn=0, wait=True):
                if wait:
                    sp.wait_ge(low_ready, turn + c - RAW + 1)
                sp.dma_start(w_raw[:, c % RAW, :], weight_stream[turn + c]).then_inc(chunk_loaded[c % RAW], 16)

            for c in range(BODY):
                load(c, wait=c >= RAW)
            turns = N_CHUNKS // BODY
            with sp.Fori(1, turns) as i:
                for c in range(BODY):
                    load(c, BODY * i)
            for c in range(turns * BODY, N_CHUNKS):
                load(c)
            sp.wait_ge(norm_ready, 4 * 7)
            sp.dma_start(out, x_norm[:, :, :]).then_inc(out_stored, 16)
            sp.wait_ge(out_stored, 16)

        @block.gpsimd
        def _(pool):
            nc.gpsimd.memset(k0[HD:P, :, 0, :, :], 0.0).then_inc(fill_done, 1)
            pool.wait_ge(fill_done, 1)
            nc.gpsimd.memset(k0[0:HD, :, 1, :, :], 0.0).then_inc(fill_done, 1)
            pool.wait_ge(fill_done, 2)
            nc.gpsimd.memset(cmp_k[HD:P, 0, :], 0.0).then_inc(fill_done, 1)
            pool.wait_ge(fill_done, 3)
            nc.gpsimd.memset(cmp_k[0:HD, 1, :], 0.0).then_inc(fill_done, 1)
            pool.wait_ge(fill_done, 4)
            nc.gpsimd.memset(cmp_hv[:, :, :, :], 0.0).then_inc(fill_done, 1)
            pool.wait_ge(fill_done, 5)
            nc.gpsimd.memset(cmp_v[:, :, :], 0.0).then_inc(zeros_ready, 1)
            pool.wait_ge(zeros_ready, 1)
            pool.wait_ge(acc_read, 4 * ACC_FFN0 + 4)
            pool.wait_ge(norm_ready, 4 * 3)
            pool.wait_ge(h_low_ready, H_N[2] + 4)
            pool.wait_ge(h_high_ready, H_N[2] + 4)
            nc.gpsimd.memset(k1[HD:P, 0, :, :], 0.0).then_inc(fill_done, 1)
            pool.wait_ge(fill_done, 6)
            nc.gpsimd.memset(k1[0:HD, 1, :, :], 0.0).then_inc(zeros_ready, 1)
            pool.wait_ge(zeros_ready, 2)
            pool.wait_ge(acc_read, 4 * ACC_FFN1 + 4)
            pool.wait_ge(h_low_ready, H_N[4] + 4)
            pool.wait_ge(h_high_ready, H_N[4] + 4)
            nc.gpsimd.memset(k2[96:P, :, :], 0.0).then_inc(zeros_ready, 1)

        @block.tensor
        def _(pe):
            mm = nc.tensor.matmul

            def split_product(out_ap, c, col, high, low, start, stop):
                wh = w_high[:, c % RING, col:col + P]
                wl = w_low[:, c % RING, col:col + P]
                mm(out_ap, wh, high, start=start, stop=False, skip_group_check=True)
                mm(out_ap, wh, low, start=False, stop=False, skip_group_check=True)
                return mm(out_ap, wl, high, start=False, stop=stop, skip_group_check=True)

            def moving_product(out_ap, c, col, n, high, low, start, stop):
                wh = w_high[:, c % RING, col:col + n]
                wl = w_low[:, c % RING, col:col + n]
                mm(out_ap, high, wh, start=start, stop=False, skip_group_check=True)
                mm(out_ap, high, wl, start=False, stop=False, skip_group_check=True)
                return mm(out_ap, low, wh, start=False, stop=stop, skip_group_check=True)

            def chunk_here(c, turn=0):
                pe.wait_ge(low_ready, turn + c + 1)

            def tile_bank(t):
                if t >= TILE_BANKS:
                    who, n = TILE_OWNER[t - TILE_BANKS]
                    pe.wait_ge(tile_free[who], n)
                return bank[t % TILE_BANKS]

            def column_tiles(stage, high, low, h_wait=None, after=None):
                for i in range(SIZE[stage]):
                    c = BASE[stage] + i
                    chunk_here(c)
                    b = tile_bank(TILE0[stage] + i)
                    for k in range(DT):
                        if i == 0 and h_wait:
                            h_wait(k)
                        last = split_product(b[:, 0:S], c, k * P, high[:, k, :], low[:, k, :],
                                             k == 0, k == DT - 1)
                    last.then_inc(chunk_used, 1)
                    if after:
                        after(i)

            def row_chunk(c, high, low, first=False, last=False, turn=0):
                for m in range(DT):
                    ins = split_product(acc[m // 2][:, (m % 2) * S:(m % 2 + 1) * S], c, m * P, high, low,
                                        first and m % 2 == 0, last)
                ins.then_inc(chunk_used, 1)

            def residual():
                for m in range(DT):
                    mm(acc[m // 2][:, (m % 2) * S:(m % 2 + 1) * S], ident, x[:, m, :],
                       start=m % 2 == 0, stop=False, skip_group_check=True)

            def norm_sums(n):
                for k in range(DT):
                    if k % 2 == 0:
                        pe.wait_ge(squares_ready, 4 * n + k // 2 + 1)
                    for t in range(TT):
                        ins = mm(bank[t][:, 0:1], squares[:, k, t * P:(t + 1) * P], ones,
                                 start=k == 0, stop=k == DT - 1)
                ins.then_inc(sumsq_ready, 1)
                pe.wait_ge(rstd_ready, n + 1)
                for t in range(TT):
                    ins = mm(bank[2][:, t * P:(t + 1) * P], st_rstd[:, t:t + 1].to_broadcast([P, P]), ident,
                             start=True, stop=True)
                ins.then_inc(rstd_spread, 1)

            def attention(n, q, kpad, v, probs, probs_t):
                def scores(h):
                    if h >= 3:
                        pe.wait_ge(probs_ready, NH * n + h - 2)
                    b = bank[h % 3]
                    mm(b[:, 0:P], q(h, 0), kpad(h)[:, 0:P], start=True, stop=False, skip_group_check=True)
                    mm(b[:, 0:P], ident_b[:, :], mask_b[:, :], start=False, stop=True, skip_group_check=True)
                    mm(b[:, P:3 * P], q(h, 1), kpad(h), start=True, stop=False, skip_group_check=True)
                    mm(b[:, 2 * P:3 * P], ident_b[:, :], mask_b[:, :], start=False, stop=True,
                       skip_group_check=True).then_inc(scores_ready, 1)

                def turn(h):
                    pe.wait_ge(probs_ready, NH * n + h + 1)
                    if h >= 2:
                        pe.wait_ge(probs_copied, NH * n + h - 1)
                    for j in range(3):
                        ins = nc.tensor.transpose(bank[3 + h % 2][:, j * P:(j + 1) * P],
                                                  probs[:, h % 3, j * P:(j + 1) * P], ident)
                    ins.then_inc(probs_turned, 1)

                def values(h):
                    pe.wait_ge(probs_copied, NH * n + h + 1)
                    g = h // 4
                    if h % 4 == 0 and g >= 2:
                        pe.wait_ge(o_read, 4 * n + g - 1)
                    b = bank[5 + g % 2]
                    pt = probs_t[:, h % 2, :]
                    at = (h % 4) * HD
                    mm(b[:, at:at + HD], pt[:, 0:P], v(h, 0), start=True, stop=True)
                    mm(b[:, S + at:S + at + HD], pt[:, P:2 * P], v(h, 0), start=True, stop=False)
                    mm(b[:, S + at:S + at + HD], pt[:, 2 * P:3 * P], v(h, 1), start=False,
                       stop=True).then_inc(pv_done, 1)

                for h in range(NH + 2):
                    if h < NH:
                        scores(h)
                    if 1 <= h <= NH:
                        turn(h - 1)
                    if h >= 2:
                        values(h - 2)
                pe.wait_ge(o_read, 4 * n + 4)

            def turn_output(n, o):
                flat = o.rearrange("p t h d -> p t (h d)")
                for m in range(DT):
                    for t in range(TT):
                        ins = nc.tensor.transpose(bank[m][:, t * P:(t + 1) * P],
                                                  flat[:, t, m * P:(m + 1) * P], ident)
                    ins.then_inc(o_turned, 1)
                pe.wait_ge(r_low_ready, R_O[n] + DT)

            def feed_forward(n, acc_use):
                base, s0, blocks = BASE[f"ffn{n}"], FFN_STEP0[n], FFN_BLOCKS[n]

                def gate_and_up(j, c, turn=0, first=False):
                    for which in range(2):
                        chunk_here(c + which, turn)
                        for k in range(DT):
                            if first and which == 0 and k % 2 == 0:
                                pe.wait_ge(h_low_ready, H_N[2 * n + 1] + k // 2 + 1)
                            last = split_product(bank[2 * which + j % 2][:, 0:S], c + which, k * P,
                                                 h_high[:, k, :], h_low[:, k, :], k == 0, k == DT - 1)
                        last.then_inc(chunk_used, 1)

                def down(j, c, turn=0, more=0, last=False):
                    pe.wait_ge(hid_low, s0 + j + more + 1)
                    chunk_here(c, turn)
                    row_chunk(c, r_high[:, j % 2, :], r_low[:, j % 2, :], last=last)

                residual()
                norm_sums(2 * n + 1)
                gate_and_up(0, base, first=True)
                with pe.Fori(0, (blocks - 2) // 2) as i:
                    for q in range(2):
                        c = base + 2 + 3 * q
                        gate_and_up(1 + q, c, BODY * i)
                        down(q, c + 2, BODY * i, more=2 * i)
                c = base + 2 + 3 * (blocks - 2)
                gate_and_up(blocks - 1, c)
                down(blocks - 2, c + 2)
                down(blocks - 1, c + 3, last=True)

            pe.wait_ge(small_loaded, 16)
            norm_sums(0)
            column_tiles("rgate", h_high, h_low,
                         lambda k: pe.wait_ge(h_low_ready, H_N[0] + k // 2 + 1) if k % 2 == 0 else None)
            column_tiles("kvc", h_high, h_low)
            pe.wait_ge(r_low_ready, R_CMP + 1)
            for which in range(2):
                for j in range(16):
                    c = BASE["w1"] + 2 * which + j // 8
                    if j % 8 == 0:
                        chunk_here(c)
                    at = 4 * which
                    moving = [r[:, at:at + 4, 2 * j:2 * j + CS * (NC - 1) + 1:CS].rearrange("p g c -> p c g")
                              for r in (r_high, r_low)]
                    split_product(acc[2 * which][:, 0:NC * NKV].rearrange("p (c g) -> p c g", g=NKV), c,
                                  (j % 8) * P, *moving, j == 0, j == 15)
                    at = 32 * which + 2 * j
                    ins = split_product(acc[2 * which + 1][:, 0:2], c, (j % 8) * P, pe_high[:, at:at + 2],
                                        pe_low[:, at:at + 2], j == 0, j == 15)
                    if j % 8 == 7:
                        ins.then_inc(chunk_used, 1)

            def compression(i):
                if i == 1:
                    pe.wait_ge(cmp_hv_ready, 1)
                    mm(acc[0][:, 0:60], par("w2k"), cmp_hid[:, 0:60], start=True, stop=True)
                    for g in range(NKV):
                        ins = mm(acc[1][:, g * HD:(g + 1) * HD], cmp_hv[:, g, :, :].rearrange("p r c -> p (r c)"),
                                 par("w2v"), start=True, stop=True)
                    ins.then_inc(cmp_kv_ready, 1)
                if i == 3:
                    pe.wait_ge(cmp_sq_ready, 1)
                    mm(acc[2][0:60, 0:1], cmp_ksq, blk2[:, 0:1], start=True, stop=True).then_inc(cmp_sumsq_ready, 1)
                if i == 6:
                    pe.wait_ge(cmp_rstd_ready, 1)
                    mm(acc[3][:, 0:60], cmp_rstd[0:60, :].to_broadcast([60, P]), ident[0:60, 0:60],
                       start=True, stop=True).then_inc(cmp_spread, 1)

            column_tiles("rx", h_high, h_low, after=compression)
            for t, (gate, m, blocks) in enumerate(LRU_GROUPS):
                b = tile_bank(TILE0["lru"] + t)
                pe.wait_ge(r_low_ready, R_CONV + blocks[-1][1] + 1)
                for n, (at, k) in enumerate(blocks):
                    c = BASE["lru"] + at // 8
                    if at % 8 == 0:
                        chunk_here(c)
                    ins = split_product(b[:, 0:S], c, at % 8 * P, r_high[:, k, :], r_low[:, k, :],
                                        n == 0, n == len(blocks) - 1)
                    if at % 8 == 7 or at == len(GATES) - 1:
                        ins.then_inc(chunk_used, 1)
            pe.wait_ge(cmp_spread, 1)
            pe.wait_ge(head_normed, 1)
            for i in range(4):
                c = BASE["v"] + i
                chunk_here(c)
                for k in (2 * i, 2 * i + 1):
                    for t in range(TT):
                        ins = moving_product(acc[t][:, :], c, (k % 2) * 512, 512, h_high[:, k, t * P:(t + 1) * P],
                                             h_low[:, k, t * P:(t + 1) * P], k == 0, k == DT - 1)
                ins.then_inc(chunk_used, 1)
            c = BASE["g"]
            chunk_here(c)
            for k in range(DT):
                for t in range(TT):
                    ins = moving_product(acc[2 + t][:, 0:3 * NH], c, k * P, 3 * NH, h_high[:, k, t * P:(t + 1) * P],
                                         h_low[:, k, t * P:(t + 1) * P], k == 0, k == DT - 1)
            ins.then_inc(chunk_used, 1)

            def head_sums(e):
                pe.wait_ge(head_sq_ready, e + 1)
                if e == 0:
                    pe.wait_ge(acc_read, 4 * ACC_V + 4)
                for t in range(TT):
                    at = (t * 12 + e) * 2
                    ins = mm(acc[0][:, at:at + 2], head_sq[:, e % 2, t * P:(t + 1) * P], blk2,
                             start=True, stop=True)
                ins.then_inc(head_sumsq_done, 1)

            column_tiles("k", h_high, h_low, after=lambda i: head_sums(i - 1) if i else None)
            column_tiles("q", h_high, h_low, after=lambda i: head_sums(i + 3))
            head_sums(11)

            def spread_heads(e):
                if e == 0:
                    pe.wait_ge(head_rstd_ready, 1)
                if e >= TILE_BANKS:
                    pe.wait_ge(head_normed, 1 + e - TILE_BANKS + 1)
                for t in range(TT):
                    for j in range(2):
                        ins = mm(bank[e % TILE_BANKS][HD * j:HD * (j + 1), t * P:(t + 1) * P],
                                 head_rstd[:, t, e, j:j + 1].to_broadcast([P, HD]), ident, start=True, stop=True)
                ins.then_inc(head_spread, 1)

            tile_read(pe, "q", 7)
            pe.wait_ge(head_std_ready, 2)
            for k in range(RT):
                chunk_here(BASE["yr"] + k)
                pe.wait_ge(r_low_ready, R_SCAN + k + 1)
                row_chunk(BASE["yr"] + k, r_high[:, k, :], r_low[:, k, :], first=k == 0, last=k == RT - 1)
                spread_heads(k)
            spread_heads(RT)
            pe.wait_ge(head_normed, 1 + 12)

            pe.wait_ge(consts_ready, 1)
            for t in range(TT):
                for h in range(NH):
                    at = (t * NH + h) * 16
                    ins = mm(bank[0][:, at:at + NC], q0[:, h // 2, t * P:(t + 1) * P],
                             cmp_k[:, h % 2, h // 4:h // 4 + NKV * (NC - 1) + 1:NKV], start=True, stop=True)
            ins.then_inc(cmp_scores, 1)
            pe.wait_ge(cmp_probs, 1)
            pe.wait_ge(acc_read, 4 * ACC_YR + 4)
            for i in range(8):
                ins = nc.tensor.transpose(bank[1 + i // 4][:, (i % 4) * P:(i % 4 + 1) * P],
                                          cmp_p[:, i // 4, 4 * (i % 4):4 * (i % 4) + 4, :]
                                          .rearrange("p h c -> p (h c)"), ident)
            ins.then_inc(cmp_turned, 1)
            pe.wait_ge(cmp_copied, 2)
            for t in range(TT):
                for g in range(NKV):
                    ins = mm(bank[3 + 2 * t + g // 2][:, (g % 2) * 256:(g % 2 + 1) * 256],
                             cmp_pt[:, 4 * t + g, :], cmp_v[:, g, :], start=True, stop=True)
                ins.then_inc(cmp_pv, 1)
            pe.wait_ge(cmp_done, 4)
            for n in range(2):
                attention(n, lambda h, t: q0[:, h // 2, t * P:(t + 1) * P],
                          lambda h: k0[:, n, h % 2, h // 4, :],
                          lambda h, t: v0[:, n, t, (h // 4) * HD:(h // 4 + 1) * HD], probs0, probs_t0)
            turn_output(0, o0)
            column_tiles("mg", h_high, h_low)
            column_tiles("ao", r_high, r_low)
            pe.wait_ge(acc_read, 4 * ACC_YR + 4)
            residual()
            for k in range(DT):
                chunk_here(BASE["wo"] + k)
                pe.wait_ge(h_low_ready, H_Z + k + 1)
                row_chunk(BASE["wo"] + k, h_high[:, k, :], h_low[:, k, :], last=k == DT - 1)
            pe.wait_ge(acc_read, 4 * ACC_WO + 4)
            feed_forward(0, ACC_FFN0)

            pe.wait_ge(acc_read, 4 * ACC_FFN0 + 4)
            norm_sums(2)

            def turn_rope(e):
                tile_read(pe, "q1" if e < 8 else "k1", e % 8)
                if e >= 2:
                    pe.wait_ge(rope_done, e - 1)
                mm(acc[e % 2][:, 0:S], par("rot64"), rope_in[:, e % 2, :], start=True,
                   stop=True).then_inc(rope_turned, 1)

            column_tiles("q1", h_high, h_low,
                         lambda k: pe.wait_ge(h_low_ready, H_N[2] + k // 2 + 1) if k % 2 == 0 else None,
                         after=lambda i: turn_rope(i - 1) if i else None)
            column_tiles("k1", h_high, h_low, after=lambda i: turn_rope(i + 7))
            turn_rope(15)
            pe.wait_ge(rope_done, 16)

            def values_all(stage, n_k):
                for k in range(n_k):
                    c = BASE[stage] + k
                    chunk_here(c)
                    for t in range(TT):
                        for half in range(2):
                            ins = moving_product(acc[2 * t + half][:, :], c, half * 512, 512,
                                                 h_high[:, k, t * P:(t + 1) * P], h_low[:, k, t * P:(t + 1) * P],
                                                 k == 0, k == n_k - 1)
                    ins.then_inc(chunk_used, 1)

            values_all("v1", DT)
            pe.wait_ge(zeros_ready, 2)
            tile_read(pe, "k1", 7)
            pe.wait_ge(acc_read, 4 * ACC_V1 + 4)
            attention(2, lambda h, t: q1[:, h // 2, t * P:(t + 1) * P], lambda h: k1[:, h % 2, h // 2, :],
                      lambda h, t: v1[:, t, h * HD:(h + 1) * HD], probs1, probs_t1)
            turn_output(1, o1)
            residual()
            for k in range(DT):
                chunk_here(BASE["wo1"] + k)
                row_chunk(BASE["wo1"] + k, r_high[:, k, :], r_low[:, k, :], last=k == DT - 1)
            pe.wait_ge(acc_read, 4 * ACC_WO1 + 4)
            feed_forward(1, ACC_FFN1)

            pe.wait_ge(acc_read, 4 * ACC_FFN1 + 4)
            norm_sums(4)
            column_tiles("c2", h_high, h_low,
                         lambda k: pe.wait_ge(h_low_ready, H_N[4] + k // 2 + 1) if k % 2 == 0 else None)
            pe.wait_ge(c_sq_ready, 1)
            for which, (a, b) in enumerate(((0, 3), (3, 5))):
                for t in range(TT):
                    for e in range(a, b):
                        ins = mm(acc[0][:, 2 * which + t:2 * which + t + 1], c_sq[:, e, t * P:(t + 1) * P], ones,
                                 start=e == a, stop=e == b - 1)
            ins.then_inc(c_sumsq, 1)
            tile_read(pe, "c2", 5)
            mm(acc[3][:, 0:S], par("rot32"), c_raw[:, 5, :], start=True, stop=True).then_inc(rope_turned, 1)
            pe.wait_ge(c_rstd_ready, 1)
            for which in range(2):
                for t in range(TT):
                    ins = mm(acc[1 + which][:, t * P:(t + 1) * P],
                             c_rstd[:, 2 * which + t:2 * which + t + 1].to_broadcast([P, P]), ident,
                             start=True, stop=True)
            ins.then_inc(c_spread, 1)
            for h in range(NH):
                b = tile_bank(TILE0["uq"] + h)
                for k in range(3):
                    n = 3 * h + k
                    c = BASE["uq"] + n // 8
                    if n % 8 == 0:
                        chunk_here(c)
                    if h == 0:
                        pe.wait_ge(h_low_ready, H_C + k + 1)
                    ins = split_product(b[:, 0:S], c, n % 8 * P, h_high[:, k, :], h_low[:, k, :], k == 0, k == 2)
                    if n % 8 == 7:
                        ins.then_inc(chunk_used, 1)
            pe.wait_ge(h_low_ready, H_C + 5)
            for m in range(8):
                b = tile_bank(TILE0["uk"] + m)
                for k in range(2):
                    n = 2 * m + k
                    c = BASE["uk"] + n // 8
                    if n % 8 == 0:
                        chunk_here(c)
                    ins = split_product(b[:, 0:S], c, n % 8 * P, h_high[:, 3 + k, :], h_low[:, 3 + k, :],
                                        k == 0, k == 1)
                    if n % 8 == 7:
                        ins.then_inc(chunk_used, 1)
            for e in range(8):
                tile_read(pe, "uq", 2 * e + 1)
                if e >= 2:
                    pe.wait_ge(rope_done, 17 + e - 1)
                mm(acc[e % 2][:, :], par("rot32"), q2[:, 2 * e:2 * e + 2, :].rearrange("p h t -> p (h t)"),
                   start=True, stop=True).then_inc(rope_turned, 1)
            pe.wait_ge(rope_done, 16 + 1 + 8)
            for k in range(2):
                c = BASE["uv"] + k
                chunk_here(c)
                for t in range(TT):
                    for half in range(2):
                        ins = moving_product(acc[2 * t + half][:, :], c, half * 512, 512,
                                             h_high[:, 3 + k, t * P:(t + 1) * P],
                                             h_low[:, 3 + k, t * P:(t + 1) * P], k == 0, k == 1)
                ins.then_inc(chunk_used, 1)
            tile_read(pe, "uk", 7)
            pe.wait_ge(k2_ready, 1)
            pe.wait_ge(zeros_ready, 3)
            pe.wait_ge(acc_read, 4 * ACC_V2 + 4)
            attention(3, lambda h, t: q2[:, h, t * P:(t + 1) * P], lambda h: k2[:, h, :],
                      lambda h, t: v2[:, t, h * HD:(h + 1) * HD], probs2, probs_t2)
            turn_output(2, o2)
            residual()
            for k in range(DT):
                chunk_here(BASE["wo2"] + k)
                row_chunk(BASE["wo2"] + k, r_high[:, k, :], r_low[:, k, :], last=k == DT - 1)
            pe.wait_ge(acc_read, 4 * ACC_WO2 + 4)
            feed_forward(2, ACC_FFN2)
            norm_sums(6)

        @block.scalar
        def _(act):
            fn = nc.scalar.activation

            def split_high(c, i=None):
                if c >= N_CHUNKS:
                    return
                turn, turn_dma = (0, 0) if i is None else (BODY * i, 16 * (BODY // RAW) * i)
                act.wait_ge(chunk_loaded[c % RAW], turn_dma + 16 * (c // RAW + 1))
                if c >= RING:
                    act.wait_ge(chunk_used, turn + c - RING + 1)
                fn(w_high[:, c % RING, :], w_raw[:, c % RAW, :], ACT.Copy).then_inc(high_ready, 1)

            def stage(name, post):
                for i in range(SIZE[name]):
                    c = BASE[name] + i
                    act.wait_ge(chunk_used, c + 1)
                    post(i)
                    split_high(c + RING)

            def tile(name, i):
                return bank[(TILE0[name] + i) % TILE_BANKS][:, 0:S]

            def freed(ins):
                ins.then_inc(tile_free["act"], 1)

            def read_acc(p, ap):
                fn(ap, acc[p][:, :], ACT.Copy).then_inc(acc_read, 1)

            def norm(n, from_acc=None):
                if from_acc is not None:
                    act.wait_ge(chunk_used, from_acc)
                    for p in range(4):
                        read_acc(p, pieces(x, p).rearrange("p k t -> p (k t)"))
                act.wait_ge(sumsq_ready, n + 1)
                for t in range(TT):
                    ins = fn(st_std[:, t:t + 1], bank[t][:, 0:1], ACT.Sqrt, bias=eps_col, scale=1.0 / D)
                ins.then_inc(std_ready, 1)
                if n < 6:
                    for p in range(4):
                        act.wait_ge(norm_ready, 4 * n + p + 1)
                        fn(pieces(h_high, p), pieces(x_norm, p), ACT.Copy).then_inc(h_high_ready, 1)

            def attention(n, probs):
                for h in range(NH):
                    act.wait_ge(max_ready, NH * n + h + 1)
                    if h >= 3:
                        act.wait_ge(probs_turned, NH * n + h - 2)
                    b = bank[h % 3]
                    fn(probs[:, h % 3, 0:P], b[:, 0:P], ACT.Exp, bias=neg_max[:, h, 0:1],
                       accum_out=sums[:, 0, h:h + 1])
                    fn(probs[:, h % 3, P:3 * P], b[:, P:3 * P], ACT.Exp, bias=neg_max[:, h, 1:2],
                       accum_out=sums[:, 1, h:h + 1]).then_inc(probs_ready, 1)

            def output_high(n):
                for m in range(DT):
                    act.wait_ge(o_turned, DT * n + m + 1)
                    fn(r_high[:, m, :], bank[m][:, 0:S], ACT.Copy).then_inc(r_high_ready, 1)

            def feed_forward(n):
                base, s0, blocks, both = BASE[f"ffn{n}"], FFN_STEP0[n], FFN_BLOCKS[n], n == 0
                func = ACT.Gelu_apprx_tanh if both else ACT.Gelu

                def tap(name, row, j):
                    at = AT[name][0] + row * blocks
                    return small[:, at + j:at + j + 1] if isinstance(j, int) else small[:, bass.ds(j + at, 1)]

                def step(j, c, i=None):
                    turn, k = (0, 0) if i is None else (BODY * i, 2 * i)
                    act.wait_ge(chunk_used, turn + c + 1)
                    fn(taps_g[:, j % 2, :], bank[j % 2][:, 0:S], ACT.Identity, scale=tap(f"fcw{n}", 2, k + j),
                       bias=tap(f"fcb{n}", 0, k + j)).then_inc(tap_g, 1)
                    split_high(c + RING, i)
                    act.wait_ge(chunk_used, turn + c + 2)
                    if both:
                        fn(taps_v[:, j % 2, :], bank[2 + j % 2][:, 0:S], ACT.Identity,
                           scale=tap("fcw0", 5, k + j), bias=tap("fcb0", 1, k + j)).then_inc(tap_v, 1)
                    split_high(c + 1 + RING, i)
                    act.wait_ge(conv_g, k + (s0 + j + 1))
                    fn(gelu_g[:, j % 2, :], taps_g[:, j % 2, :], func).then_inc(gelu_ready, 1)
                    if j:
                        split_high(c + 2 + RING, i)
                    act.wait_ge(hidden_ready, k + (s0 + j + 1))
                    fn(r_high[:, j % 2, :], hidden[:, j % 2, :], ACT.Copy).then_inc(hid_high, 1)

                step(0, base)
                turns = (blocks - 2) // 2 - (n == 2)
                with act.Fori(0, turns) as i:
                    for q in range(2):
                        step(1 + q, base + 2 + 3 * q, i)
                for j in range(1 + 2 * turns, blocks):
                    step(j, base + 3 * j - 1)
                split_high(base + 3 * blocks - 1 + RING)

            act.dma_start(x[:, :, :], x_in).then_inc(x_loaded, 16)
            act.dma_start(small[:, :], small_in).then_inc(small_loaded, 16)
            act.wait_ge(small_loaded, 16)
            fn(ident_b[:, :], ident, ACT.Copy)
            fn(mask_b[:, :], par("mask"), ACT.Copy).then_inc(consts_ready, 1)
            fn(pe_high[:, :], par2("pek", 64), ACT.Copy).then_inc(pe_high_ready, 1)
            fn(lru_t[0], par("lam"), ACT.Abs).then_inc(act_step, 1)
            act.wait_ge(act_step, 1)
            fn(lru_t[1], lru_t[0], ACT.Exp, scale=-1.0).then_inc(act_step, 1)
            for c in range(RING):
                split_high(c)
            norm(0)

            def rgate(i):
                fn(gelu_gate[:, i, :], tile("rgate", i), ACT.Gelu_apprx_tanh).then_inc(tile_free["act"], 1)

            stage("rgate", rgate)

            def kvc(i):
                b = tile("kvc", i)
                if i == 0:
                    act.wait_ge(kv2_ready, 1)
                g = 4 * (i // 2) + 2 * (i % 2)
                for j in range(2):
                    rows = slice(HD * j, HD * (j + 1))
                    fn(kv2[0:HD, g + j, :], b[rows, :], ACT.Copy)
                    ins = fn(kv2[HD:P, g + j, 0:S - 1], b[rows, 1:S], ACT.Copy)
                freed(ins)
                if i == 3:
                    tile_read(act, "kvc", 3)
                    fn(r_high[:, 0:8, :], kv2[:, :, :], ACT.Copy).then_inc(r_high_ready, 1)

            stage("kvc", kvc)

            def hidden_cmp(i):
                if i < 3:
                    return
                for which in range(2):
                    ins = fn(cmp_bias[:, which:which + 1], acc[2 * which + 1][:, 0:1], ACT.Copy)
                ins.then_inc(act_step, 1)
                act.wait_ge(act_step, 3)
                for which in range(2):
                    ins = fn(cmp_hid[:, 60 * which:60 * which + 60], acc[2 * which][:, 0:60],
                             ACT.Gelu_apprx_tanh, bias=cmp_bias[:, which:which + 1])
                ins.then_inc(cmp_hid_ready, 1)

            stage("w1", hidden_cmp)

            def conv_high(i):
                tile_read(act, "rx", i)
                fn(r_high[:, i, :], conv[:, i, :], ACT.Copy).then_inc(r_high_ready, 1)

            def rx(i):
                fn(conv[:, i, :], tile("rx", i), ACT.Identity, scale=par("rcw", 3 * RT + i, 1),
                   bias=par("rcb", i, 1)).then_inc(tap_ready, 1)
                if i:
                    conv_high(i - 1)
                if i == 2:
                    act.wait_ge(cmp_kv_ready, 1)
                    fn(cmp_kraw, acc[0][:, 0:60], ACT.Identity, scale=par("hg", 1, 1))
                    fn(cmp_ksq, acc[0][:, 0:60], ACT.Square).then_inc(cmp_sq_ready, 1)
                if i == 4:
                    act.wait_ge(cmp_sumsq_ready, 1)
                    fn(cmp_std[0:60, :], acc[2][0:60, 0:1], ACT.Sqrt, bias=eps_col[0:60, :],
                       scale=1.0 / HD).then_inc(cmp_std_ready, 1)

            stage("rx", rx)
            conv_high(RT - 1)

            def lru_gate(t, gate, m):
                dst, bias = ((r_gate, "rba"), (i_gate, "rbx"))[gate]
                freed(fn(dst[:, m, :], tile("lru", t), ACT.Sigmoid, bias=par(bias, m, 1)))

            lru_posts(act, split_high, lru_gate)
            stage("v", lambda i: None)

            def v_and_gates(i):
                for t in range(TT):
                    read_acc(t, v0[:, :, t, :])
                for t in range(TT):
                    fn(stats[:, 200 + 48 * t:248 + 48 * t], acc[2 + t][:, 0:3 * NH],
                       ACT.Sigmoid).then_inc(acc_read, 1)

            stage("g", v_and_gates)

            def heads(e):
                b = tile("k", e)
                if e >= 2:
                    act.wait_ge(head_sumsq_done, e - 1)
                fn(head_sq[:, e % 2, :], b, ACT.Square).then_inc(head_sq_ready, 1)
                if e < 4:
                    if e == 0:
                        act.wait_ge(zeros_ready, 1)
                    branch, g = e // 2, 2 * (e % 2)
                    for j in range(2):
                        rows = slice(HD * j, HD * (j + 1))
                        ins = fn(k0[rows, branch, j, g + j, :], b[rows, :], ACT.Identity,
                                 scale=par("hg", 2 + branch, 1)[rows, :])
                else:
                    ins = fn(q0[:, e - 4, :], b, ACT.Identity, scale=par("hg", 0, 1))
                freed(ins)
                if e < RT:
                    fn(decay[:, e, :], r_gate[:, e, :], ACT.Exp, scale=lru_k[:, e:e + 1])
                    fn(r_gate[:, e, :], r_gate[:, e, :], ACT.Tanh, scale=lru_kn[:, e:e + 1]).then_inc(decay_ready, 1)

            tile_read(act, "lru", 2 * RT - 1)
            stage("k", heads)
            stage("q", lambda i: heads(4 + i))
            act.wait_ge(head_sumsq_done, 12)
            head_sumsq = acc[0][:, 0:48].rearrange("p (t e j) -> p t e j", t=TT, j=2)
            fn(head_std[:, :, 0:4, :], head_sumsq[:, :, 0:4, :], ACT.Sqrt, bias=eps_col,
               scale=1.0 / HD).then_inc(head_std_ready, 1)
            fn(head_std[:, :, 4:12, :], head_sumsq[:, :, 4:12, :], ACT.Sqrt, bias=eps64_col).then_inc(head_std_ready, 1)
            act.wait_ge(var_ready, RT)
            fn(conv[:, :, :], conv[:, :, :], ACT.Sqrt).then_inc(scale_ready, 1)
            for m in range(RT):
                act.wait_ge(gated_ready, m + 1)
                fn(r_high[:, m, :], i_gate[:, m, :], ACT.Copy).then_inc(r_high_ready, 1)
            stage("yr", lambda i: None)
            for p in range(4):
                read_acc(p, pieces(y_rnn, p).rearrange("p k t -> p (k t)"))
            act.wait_ge(cmp_shifted, 1)
            fn(cmp_p[:, :, :, 0:NC], cmp_s, ACT.Exp).then_inc(cmp_probs, 1)
            act.wait_ge(cmp_turned, 1)
            fn(cmp_pt[:, 0:4, :], bank[1][:, :], ACT.Copy).then_inc(cmp_copied, 1)
            attention(0, probs0)
            attention(1, probs0)
            output_high(0)
            stage("mg", lambda i: freed(fn(merge[:, i, :], tile("mg", i), ACT.Sigmoid)))

            def merged(i):
                act.wait_ge(z_ready, i + 1)
                fn(h_high[:, i, :], y_rnn[:, i, :], ACT.Copy).then_inc(h_high_ready, 1)

            stage("ao", merged)
            stage("wo", lambda i: None)
            norm(1, BASE["wo"] + 8)
            feed_forward(0)

            norm(2, BASE["q1"])

            def rope_operand(e):
                if e >= 2:
                    act.wait_ge(rope_done, e - 1)
                freed(fn(rope_in[:, e % 2, :], tile("q1", e), ACT.Copy, scale=HD ** -0.5 if e < 8 else 1.0))

            stage("q1", rope_operand)
            stage("k1", lambda i: rope_operand(8 + i))
            stage("v1", lambda i: None)
            for p in range(4):
                read_acc(p, v1[:, p // 2, (p % 2) * 512:(p % 2 + 1) * 512])
            attention(2, probs1)
            output_high(1)
            stage("wo1", lambda i: None)
            norm(3, BASE["wo1"] + 8)
            feed_forward(1)

            norm(4, BASE["c2"])

            def latents(e):
                b = tile("c2", e)
                if e < 5:
                    ins = fn(c_sq[:, e, :], b, ACT.Square)
                    if e == 4:
                        ins.then_inc(c_sq_ready, 1)
                    freed(fn(c_raw[:, e, :], b, ACT.Identity, scale=par("ln2", e, 1)))
                else:
                    freed(fn(c_raw[:, e, :], b, ACT.Copy))

            stage("c2", latents)
            act.wait_ge(c_sumsq, 1)
            for which, n in enumerate((QL, KVL)):
                ins = fn(c_std[:, 2 * which:2 * which + 2], acc[0][:, 2 * which:2 * which + 2], ACT.Sqrt,
                         bias=eps_col, scale=1.0 / n)
            ins.then_inc(c_std_ready, 1)
            for e in range(5):
                act.wait_ge(c_normed, e + 1)
                fn(h_high[:, e, :], c_norm[:, e, :], ACT.Copy).then_inc(h_high_ready, 1)
            at = 0
            for q in range(SIZE["uq"]):
                act.wait_ge(chunk_used, BASE["uq"] + q + 1)
                while at < NH and (3 * at + 2) // 8 <= q:
                    freed(fn(q2[:, at, :], tile("uq", at), ACT.Copy, scale=(HD + ROPE) ** -0.5))
                    at += 1
                split_high(BASE["uq"] + q + RING)
            for q in range(SIZE["uk"]):
                act.wait_ge(chunk_used, BASE["uk"] + q + 1)
                for m in range(4 * q, 4 * q + 4):
                    for j in range(2):
                        ins = fn(k2[0:HD, 2 * m + j, :], tile("uk", m)[HD * j:HD * (j + 1), :], ACT.Copy)
                    freed(ins)
                split_high(BASE["uk"] + q + RING)
            act.wait_ge(rope_done, 17)
            fn(k2[HD:HD + ROPE, :, :], c_raw[HD:HD + ROPE, 5:6, :].to_broadcast([ROPE, NH, S]),
               ACT.Copy).then_inc(k2_ready, 1)
            stage("uv", lambda i: None)
            for p in range(4):
                read_acc(p, v2[:, p // 2, (p % 2) * 512:(p % 2 + 1) * 512])
            attention(3, probs2)
            output_high(2)
            stage("wo2", lambda i: None)
            norm(5, BASE["wo2"] + 8)
            feed_forward(2)
            norm(6, N_CHUNKS)

        @block.vector
        def _(dve):
            v = nc.vector
            steps = [0]

            def mark(ins):
                ins.then_inc(dve_step, 1)
                steps[0] += 1
                return steps[0]

            def link(ins):
                dve.wait_ge(dve_step, mark(ins))

            def split_low(c, i=None):
                if c >= N_CHUNKS:
                    return
                dve.wait_ge(high_ready, (0 if i is None else BODY * i) + c + 1)
                v.tensor_tensor(w_low[:, c % RING, :], w_raw[:, c % RAW, :], f(w_high[:, c % RING, :]),
                                ALU.subtract).then_inc(low_ready, 1)

            def stage(name, post, wait=True):
                for i in range(SIZE[name]):
                    c = BASE[name] + i
                    if wait:
                        dve.wait_ge(chunk_used, c + 1)
                    post(i)
                    split_low(c + RING)

            def tile(name, i):
                return bank[(TILE0[name] + i) % TILE_BANKS][:, 0:S]

            def low(dst, src, high, ready, n, done):
                dve.wait_ge(ready, n)
                v.tensor_tensor(dst, src, f(high), ALU.subtract).then_inc(done, 1)

            def norm(n, acc_use=None):
                for p in range(4):
                    if acc_use is not None:
                        dve.wait_ge(acc_read, 4 * acc_use + p + 1)
                    v.tensor_tensor(pieces(squares, p), pieces(x, p), pieces(x, p), ALU.mult).then_inc(squares_ready, 1)
                for k in range(DT):
                    ins = v.tensor_scalar(x_gain[:, k, :], x[:, k, :], par("norm", n * DT + k, 1), None, ALU.mult)
                gained = mark(ins)
                dve.wait_ge(std_ready, n + 1)
                v.reciprocal(st_rstd, st_std).then_inc(rstd_ready, 1)
                dve.wait_ge(rstd_spread, n + 1)
                dve.wait_ge(dve_step, gained)
                for p in range(5):
                    if p < 4:
                        v.tensor_tensor(pieces(x_norm, p), pieces(x_gain, p),
                                        bank[2][:, 0:S].unsqueeze(1).to_broadcast([P, 2, S]),
                                        ALU.mult).then_inc(norm_ready, 1)
                    if p and n < 6:
                        low(pieces(h_low, p - 1), pieces(x_norm, p - 1), pieces(h_high, p - 1), h_high_ready,
                            H_N[n] + p, h_low_ready)

            def attention(n, o, probs_t, branch=None):
                def row_max(h):
                    dve.wait_ge(scores_ready, NH * n + h + 1)
                    b = bank[h % 3]
                    v.tensor_reduce(neg_max[:, h, 0:1], b[:, 0:P], AX.X, ALU.max, negate=True)
                    v.tensor_reduce(neg_max[:, h, 1:2], b[:, P:3 * P], AX.X, ALU.max, negate=True).then_inc(max_ready, 1)

                def copy_turned(h):
                    dve.wait_ge(probs_turned, NH * n + h + 1)
                    if h >= 2:
                        dve.wait_ge(pv_done, NH * n + h - 1)
                    v.tensor_copy(probs_t[:, h % 2, :], bank[3 + h % 2][:, 0:3 * P]).then_inc(probs_copied, 1)

                def output(g):
                    dve.wait_ge(pv_done, NH * n + 4 * g + 4)
                    w = weights_o[:, :, 4 * g:4 * g + 4]
                    link(v.reciprocal(w, sums[:, :, 4 * g:4 * g + 4]))
                    if branch is not None:
                        link(v.tensor_tensor(w, w, nsa_gate[:, :, 4 * g:4 * g + 4, branch], ALU.mult))
                    dst = o[:, :, 4 * g:4 * g + 4, :]
                    src = bank[5 + g % 2][:, :].rearrange("p (t h d) -> p t h d", t=TT, h=4)
                    wide = w.unsqueeze(3).to_broadcast([P, TT, 4, HD])
                    if branch is None:
                        v.tensor_tensor(dst, src, wide, ALU.mult).then_inc(o_read, 1)
                    else:
                        link(v.tensor_tensor(o_part, src, wide, ALU.mult))
                        v.tensor_tensor(dst, dst, o_part, ALU.add).then_inc(o_read, 1)

                for h in range(NH + 3):
                    if h < NH:
                        row_max(h)
                    if 1 <= h <= NH:
                        copy_turned(h - 1)
                    if h >= 3 and h % 4 == 2:
                        output((h - 3) // 4)

            def output_low(n):
                for m in range(DT):
                    low(r_low[:, m, :], bank[m][:, 0:S], r_high[:, m, :], r_high_ready, R_O[n] + m + 1, r_low_ready)

            def feed_forward(n):
                base, s0, blocks, both = BASE[f"ffn{n}"], FFN_STEP0[n], FFN_BLOCKS[n], n == 0

                def tap(row, j):
                    at = AT[f"fcw{n}"][0] + row * blocks
                    return small[:, at + j:at + j + 1] if isinstance(j, int) else small[:, bass.ds(j + at, 1)]

                def taps(dst, b, row, j, first, second, done, count):
                    dve.wait_ge(first, count)
                    v.scalar_tensor_tensor(dst[:, 1:S], b[:, 0:S - 1], tap(row + 1, j), dst[:, 1:S],
                                           ALU.mult, ALU.add).then_inc(second, 1)
                    dve.wait_ge(second, count)
                    v.scalar_tensor_tensor(dst[:, 2:S], b[:, 0:S - 2], tap(row, j), dst[:, 2:S],
                                           ALU.mult, ALU.add).then_inc(done, 1)

                def step(j, c, i=None):
                    k = 0 if i is None else 2 * i
                    taps(taps_g[:, j % 2, :], bank[j % 2], 0, k + j, tap_g, tap_g2, conv_g, k + (s0 + j + 1))
                    split_low(c + RING, i)
                    if both:
                        taps(taps_v[:, j % 2, :], bank[2 + j % 2], 3, k + j, tap_v, tap_v2, conv_v, k + (j + 1))
                    split_low(c + 1 + RING, i)
                    dve.wait_ge(gelu_ready, k + (s0 + j + 1))
                    if both:
                        dve.wait_ge(conv_v, k + (j + 1))
                    else:
                        dve.wait_ge(chunk_used, (0 if i is None else BODY * i) + c + 2)
                    value = taps_v[:, j % 2, :] if both else bank[2 + j % 2][:, 0:S]
                    v.tensor_tensor(hidden[:, j % 2, :], gelu_g[:, j % 2, :], value, ALU.mult).then_inc(hidden_ready, 1)
                    if j:
                        split_low(c + 2 + RING, i)
                    low(r_low[:, j % 2, :], hidden[:, j % 2, :], r_high[:, j % 2, :], hid_high,
                        k + (s0 + j + 1), hid_low)

                step(0, base)
                turns = (blocks - 2) // 2 - (n == 2)
                with dve.Fori(0, turns) as i:
                    for q in range(2):
                        step(1 + q, base + 2 + 3 * q, i)
                for j in range(1 + 2 * turns, blocks):
                    step(j, base + 3 * j - 1)
                split_low(base + 3 * blocks - 1 + RING)

            dve.wait_ge(small_loaded, 16)
            dve.wait_ge(x_loaded, 16)
            for c in range(RING // 2):
                split_low(c)
            norm(0)
            for c in range(RING // 2, RING):
                split_low(c)
            z, s, s2, t = lru_t[1], lru_t[0], lru_t[2], lru_t[3]
            dve.wait_ge(act_step, 2)
            link(v.tensor_scalar(s2, z, 2.0, None, ALU.add))
            link(v.reciprocal(s, s2))
            link(v.tensor_tensor(s, s, z, ALU.mult))
            link(v.tensor_tensor(s2, s, s, ALU.mult))
            link(v.tensor_scalar(t, s2, 1.0 / 17, None, ALU.mult))
            for n in range(7, 0, -1):
                link(v.scalar_tensor_tensor(t, t, 1.0 / (2 * n + 1), s2, ALU.add, ALU.mult))
            link(v.scalar_tensor_tensor(t, t, 1.0, s, ALU.add, ALU.mult))
            link(v.tensor_scalar(s, par("lam"), -1.0, 0.0, ALU.mult, ALU.max))
            link(v.scalar_tensor_tensor(t, t, 2.0, s, ALU.mult, ALU.add))
            v.tensor_scalar(lru_kn, t, LRU_C, None, ALU.mult)
            v.tensor_scalar(lru_k, t, -LRU_C, None, ALU.mult)
            dve.wait_ge(pe_high_ready, 1)
            v.tensor_tensor(pe_low[:, :], par2("pek", 64), f(pe_high[:, :]), ALU.subtract)
            v.memset(kv2[:, :, S - 1:S], 0.0).then_inc(kv2_ready, 1)
            stage("rgate", lambda i: None, wait=False)
            stage("kvc", lambda i: low(r_low[:, 0:8, :], kv2[:, :, :], r_high[:, 0:8, :], r_high_ready, 1, r_low_ready)
                  if i == 3 else None)

            def spread_hidden(i):
                if i < 3:
                    return
                dve.wait_ge(cmp_hid_ready, 1)
                dve.wait_ge(zeros_ready, 1)
                for r in range(4):
                    ins = v.tensor_copy(cmp_hv[:, :, r, 0:NC],
                                        cmp_hid[:, 60:120].rearrange("p (c g) -> p g c", g=NKV))
                ins.then_inc(cmp_hv_ready, 1)

            stage("w1", spread_hidden)

            def conv_low(i):
                low(r_low[:, i, :], conv[:, i, :], r_high[:, i, :], r_high_ready, R_CONV + i + 1, r_low_ready)

            def rx(i):
                dve.wait_ge(tap_ready, i + 1)
                b = tile("rx", i)
                for back in (1, 2, 3):
                    ins = v.scalar_tensor_tensor(conv[:, i, back:S], b[:, 0:S - back], par("rcw", (3 - back) * RT + i, 1),
                                                 conv[:, i, back:S], ALU.mult, ALU.add)
                    if back < 3:
                        link(ins)
                ins.then_inc(tile_free["dve"], 1)
                if i:
                    conv_low(i - 1)
                if i == 2:
                    dve.wait_ge(cmp_kv_ready, 1)
                    for r in range(4):
                        v.tensor_copy(cmp_v[32 * r:32 * r + 32, :, r * HD:(r + 1) * HD],
                                      acc[1][32 * r:32 * r + 32, 0:4 * HD].rearrange("p (g d) -> p g d", g=NKV))
                if i == 5:
                    dve.wait_ge(cmp_std_ready, 1)
                    v.reciprocal(cmp_rstd[0:60, :], cmp_std[0:60, :]).then_inc(cmp_rstd_ready, 1)
                if i == 8:
                    dve.wait_ge(cmp_spread, 1)
                    for j in range(2):
                        rows = slice(HD * j, HD * (j + 1))
                        ins = v.tensor_tensor(cmp_k[rows, j, :], cmp_kraw[rows, :], acc[3][rows, 0:60], ALU.mult)
                    ins.then_inc(head_normed, 1)

            stage("rx", rx)
            conv_low(RT - 1)
            inputs_marked = [0]

            def lru_input(t, gate, m):
                if gate == 1:
                    tile_read(dve, "lru", t)
                    inputs_marked[0] = mark(v.tensor_tensor(i_gate[:, m, :], i_gate[:, m, :], conv[:, m, :], ALU.mult))

            lru_posts(dve, split_low, lru_input)
            stage("v", lambda i: None)
            stage("g", lambda i: None)
            squared = []

            def variance(m):
                dve.wait_ge(dve_step, squared[m])
                v.scalar_tensor_tensor(conv[:, m, :], conv[:, m, :], 1.0, r_gate[:, m, :], ALU.add,
                                       ALU.mult).then_inc(var_ready, 1)

            def lru_step(e):
                if e < RT:
                    dve.wait_ge(decay_ready, e + 1)
                    squared.append(mark(v.tensor_tensor(conv[:, e, :], decay[:, e, :], decay[:, e, :], ALU.mult)))
                if e >= 1:
                    variance(e - 1)

            stage("k", lru_step)
            stage("q", lambda i: lru_step(4 + i))
            dve.wait_ge(head_std_ready, 2)
            v.reciprocal(stats[:, 148:196], stats[:, 100:148]).then_inc(head_rstd_ready, 1)
            dve.wait_ge(scale_ready, 1)
            dve.wait_ge(dve_step, inputs_marked[0])
            driven, scanned = [], []
            for m in range(RT + 3):
                if m < RT:
                    driven.append(mark(v.tensor_tensor(conv[:, m, :], conv[:, m, :], i_gate[:, m, :], ALU.mult)))
                if 1 <= m <= RT:
                    dve.wait_ge(dve_step, driven[m - 1])
                    v.tensor_tensor_scan(r_gate[:, m - 1, :], decay[:, m - 1, :], conv[:, m - 1, :], 0.0, ALU.mult,
                                         ALU.add).then_inc(scan_ready, 1)
                if 2 <= m <= RT + 1:
                    dve.wait_ge(scan_ready, m - 1)
                    v.tensor_tensor(i_gate[:, m - 2, :], r_gate[:, m - 2, :], gelu_gate[:, m - 2, :],
                                    ALU.mult).then_inc(gated_ready, 1)
                if m >= 3:
                    low(r_low[:, m - 3, :], i_gate[:, m - 3, :], r_high[:, m - 3, :], r_high_ready,
                        R_SCAN + m - 2, r_low_ready)
            v.memset(cmp_p[:, :, :, :], 0.0)

            def normed_heads(e):
                dve.wait_ge(head_spread, e + 1)
                b = bank[e % TILE_BANKS][:, 0:S]
                if e >= 4:
                    ins = v.tensor_tensor(q0[:, e - 4, :], q0[:, e - 4, :], b, ALU.mult)
                else:
                    branch, g = e // 2, 2 * (e % 2)
                    for j in range(2):
                        own, other = slice(HD * j, HD * (j + 1)), slice(HD * (1 - j), HD * (2 - j))
                        v.tensor_tensor(k0[other, branch, 1 - j, g + j, :], k0[own, branch, j, g + j, :], b[own, :],
                                        ALU.mult)
                        ins = v.tensor_tensor(k0[own, branch, j, g + j, :], k0[own, branch, j, g + j, :], b[own, :],
                                              ALU.mult)
                ins.then_inc(head_normed, 1)

            stage("yr", normed_heads, wait=False)
            normed_heads(RT)
            dve.wait_ge(cmp_scores, 1)
            src = bank[0][:, :].rearrange("p (t h c) -> p t h c", t=TT, h=NH)
            masks = par("cmpmask").rearrange("p (t c) -> p t c", t=TT)
            for t in range(TT):
                ins = v.tensor_tensor(cmp_s[:, t, :, :], src[:, t, :, 0:NC],
                                      masks[:, t, :].unsqueeze(1).to_broadcast([P, NH, NC]), ALU.add)
            link(ins)
            link(v.tensor_reduce(cmp_max, cmp_s, AX.X, ALU.max))
            for t in range(TT):
                ins = v.tensor_tensor(cmp_s[:, t, :, :], cmp_s[:, t, :, :],
                                      cmp_max[:, t, :].unsqueeze(2).to_broadcast([P, NH, NC]), ALU.subtract)
            ins.then_inc(cmp_shifted, 1)
            dve.wait_ge(cmp_probs, 1)
            link(v.tensor_reduce(cmp_sum, cmp_p[:, :, :, 0:NC], AX.X, ALU.add))
            dve.wait_ge(cmp_turned, 1)
            v.tensor_copy(cmp_pt[:, 4:8, :], bank[2][:, :].rearrange("p (a b) -> p a b", a=4)).then_inc(cmp_copied, 1)
            link(v.reciprocal(cmp_max, cmp_sum))
            for t in range(TT):
                ins = v.scalar_tensor_tensor(weights_o[:, t, :], cmp_max[:, t, :], par("rowok", t, 1),
                                             nsa_gate[:, t, :, 0], ALU.mult, ALU.mult)
            link(ins)
            for t in range(TT):
                dve.wait_ge(cmp_pv, t + 1)
                for half in range(2):
                    v.tensor_tensor(o0[:, t, 8 * half:8 * half + 8, :],
                                    bank[3 + 2 * t + half][:, :].rearrange("p (h d) -> p h d", h=8),
                                    weights_o[:, t, 8 * half:8 * half + 8].unsqueeze(2).to_broadcast([P, 8, HD]),
                                    ALU.mult).then_inc(cmp_done, 1)
            dve.wait_ge(cmp_done, 4)
            attention(0, o0, probs_t0, branch=1)
            dve.wait_ge(o_read, 4)
            attention(1, o0, probs_t0, branch=2)
            output_low(0)
            stage("mg", lambda i: None)

            def merge_low(i):
                low(h_low[:, i, :], y_rnn[:, i, :], h_high[:, i, :], h_high_ready, H_Z + i + 1, h_low_ready)

            def merged(i):
                tile_read(dve, "mg", 8 + i)
                v.tensor_tensor(merge[:, 8 + i, :], merge[:, 8 + i, :], tile("ao", i), ALU.mult).then_inc(tile_free["dve"], 1)
                link(v.tensor_tensor(merge[:, i, :], merge[:, i, :], y_rnn[:, i, :], ALU.mult))
                v.tensor_tensor(y_rnn[:, i, :], merge[:, i, :], merge[:, 8 + i, :], ALU.add).then_inc(z_ready, 1)
                if i:
                    merge_low(i - 1)

            stage("ao", merged)
            merge_low(DT - 1)
            stage("wo", lambda i: None)
            norm(1, ACC_WO)
            feed_forward(0)

            norm(2, ACC_FFN0)

            def rope(e):
                name, i = ("q1", e) if e < 8 else ("k1", e - 8)
                tile_read(dve, name, i)
                a, b = rope_a[:, e % 2, :], rope_b[:, e % 2, :]
                v.tensor_tensor(a, rope_in[:, e % 2, :], par("c64"), ALU.mult)
                dve.wait_ge(rope_turned, e + 1)
                link(v.tensor_tensor(b, acc[e % 2][:, 0:S], par("s64"), ALU.mult))
                if e < 8:
                    ins = v.tensor_tensor(q1[:, i, :], a, b, ALU.add)
                else:
                    for j in range(2):
                        rows = slice(HD * j, HD * (j + 1))
                        ins = v.tensor_tensor(k1[rows, j, i, :], a[rows, :], b[rows, :], ALU.add)
                ins.then_inc(rope_done, 1)

            stage("q1", lambda i: rope(i - 1) if i else None)
            stage("k1", lambda i: rope(i + 7))
            rope(15)
            stage("v1", lambda i: None)
            attention(2, o1, probs_t1)
            output_low(1)
            stage("wo1", lambda i: None)
            norm(3, ACC_WO1)
            feed_forward(1)

            norm(4, ACC_FFN1)
            stage("c2", lambda i: None)
            dve.wait_ge(c_std_ready, 1)
            v.reciprocal(c_rstd, c_std).then_inc(c_rstd_ready, 1)
            dve.wait_ge(c_spread, 1)
            for e in range(6):
                if e < 5:
                    v.tensor_tensor(c_norm[:, e, :], c_raw[:, e, :], acc[1 if e < 3 else 2][:, 0:S],
                                    ALU.mult).then_inc(c_normed, 1)
                if e:
                    low(h_low[:, e - 1, :], c_norm[:, e - 1, :], h_high[:, e - 1, :], h_high_ready, H_C + e, h_low_ready)
            rows = slice(HD, HD + ROPE)
            dve.wait_ge(rope_turned, 17)
            v.tensor_tensor(rope_a2[rows, 0, 0:S], c_raw[rows, 5, :], par("c32")[rows, :], ALU.mult)
            link(v.tensor_tensor(rope_b2[rows, 0, 0:S], acc[3][rows, 0:S], par("s32")[rows, :], ALU.mult))
            v.tensor_tensor(c_raw[rows, 5, :], rope_a2[rows, 0, 0:S], rope_b2[rows, 0, 0:S], ALU.add).then_inc(rope_done, 1)
            stage("uq", lambda i: None)
            stage("uk", lambda i: None)
            for e in range(8):
                a = rope_a2[rows, e % 2, :].rearrange("p (h t) -> p h t", h=2)
                b = rope_b2[rows, e % 2, :].rearrange("p (h t) -> p h t", h=2)
                q = q2[rows, 2 * e:2 * e + 2, :]
                tile_read(dve, "uq", 2 * e + 1)
                v.tensor_tensor(a, q, par("c32")[rows, :].unsqueeze(1).to_broadcast([ROPE, 2, S]), ALU.mult)
                dve.wait_ge(rope_turned, 17 + e + 1)
                link(v.tensor_tensor(b, acc[e % 2][rows, :].rearrange("p (h t) -> p h t", h=2),
                                     par("s32")[rows, :].unsqueeze(1).to_broadcast([ROPE, 2, S]), ALU.mult))
                v.tensor_tensor(q, a, b, ALU.add).then_inc(rope_done, 1)
            stage("uv", lambda i: None)
            attention(3, o2, probs_t2)
            output_low(2)
            stage("wo2", lambda i: None)
            norm(5, ACC_WO2)
            feed_forward(2)
            norm(6, ACC_FFN2)


def column_chunks(w, width=P):
    k, n = w.shape
    padded = np.zeros((k, -(-n // width) * width), w.dtype)
    padded[:, :n] = w
    return padded.reshape(k // P, P, -1, width).transpose(2, 1, 0, 3).reshape(-1, P, k // P * width)


def row_chunks(w):
    n, m = w.shape
    padded = np.zeros((-(-n // P) * P, m), w.dtype)
    padded[:n] = w
    return padded.reshape(-1, P, m)


def block_chunks(blocks):
    out = np.zeros((-(-len(blocks) // 8), P, 8, P), blocks[0].dtype)
    for n, b in enumerate(blocks):
        out[n // 8, :b.shape[0], n % 8, :b.shape[1]] = b
    return out.reshape(-1, P, D)


def ffn_chunks(gate, up, down):
    g, u, d = column_chunks(gate), column_chunks(up), row_chunks(down)
    order = [g[0], u[0]]
    for j in range(1, len(g)):
        order += [g[j], u[j], d[j - 1]]
    return np.stack(order + [d[-1]])


def lay_out_weights(a):
    w_in = a["w_in"]
    sizes = [D_RNN, D_RNN, NH * HD] + [KVW] * 6 + [3 * NH, D, D]
    cut = np.concatenate([[0], np.cumsum(sizes)])
    rx, rg, q, kc, vc, ks, vs, kw, vw, g, mr, ma = (w_in[:, cut[i]:cut[i + 1]] for i in range(12))
    full = []
    for w in (a["rg_w_a"], a["rg_w_x"]):
        band = np.zeros((RT * P, RT * P), w.dtype)
        for n in range(RNN_BLOCKS):
            band[n * BW:(n + 1) * BW, n * BW:(n + 1) * BW] = w[n]
        full.append(band)
    gates = [full[gate][k * P:(k + 1) * P, m * P:(m + 1) * P] for gate, m, k in GATES]
    qkv = a["a_w_qkv_2"][0]
    c2 = a["b_w_in_2"][0]
    uq = a["b_w_uq_2"][0].reshape(QL, NH, HD + ROPE)
    ukv = a["b_w_ukv_2"][0].reshape(KVL, NH, 2, HD)
    uk = ukv[:, :, 0, :].reshape(KVL, D)
    uv = ukv[:, :, 1, :].reshape(KVL, D)
    d0 = FF0
    parts = {
        "rgate": column_chunks(rg), "kvc": column_chunks(np.concatenate([kc, vc], 1)),
        "w1": np.concatenate([a[n].reshape(2, 8, P, P).transpose(0, 2, 1, 3).reshape(2, P, D)
                              for n in ("cmp_w1_k", "cmp_w1_v")]),
        "rx": column_chunks(rx), "lru": block_chunks(gates),
        "v": np.concatenate([vs, vw], 1).reshape(4, 2, P, 512).transpose(0, 2, 1, 3).reshape(4, P, D),
        "g": column_chunks(g), "k": column_chunks(np.concatenate([ks, kw], 1)), "q": column_chunks(q),
        "yr": row_chunks(a["w_rnn_out"]), "mg": column_chunks(np.concatenate([mr, ma], 1)),
        "ao": column_chunks(a["w_attn_out"]), "wo": row_chunks(a["w_out"]),
        "ffn0": ffn_chunks(a["w_up"][:, :d0], a["w_up"][:, d0:], a["w_down"]),
        "q1": column_chunks(qkv[:, :D]), "k1": column_chunks(qkv[:, D:2 * D]), "v1": row_chunks(qkv[:, 2 * D:]),
        "wo1": row_chunks(a["a_w_o_2"][0]),
        "ffn1": ffn_chunks(a["ffn_w_gate_2"][0], a["ffn_w_up_2"][0], a["ffn_w_down_2"][0]),
        "c2": np.concatenate([column_chunks(c2[:, :QL + KVL]),
                              column_chunks(c2[:, QL + KVL - HD:QL + KVL + ROPE])]),
        "uq": block_chunks([uq[k * P:(k + 1) * P, h] for h in range(NH) for k in range(3)]),
        "uk": block_chunks([uk[k * P:(k + 1) * P, m * P:(m + 1) * P] for m in range(8) for k in range(2)]),
        "uv": row_chunks(uv), "wo2": row_chunks(a["b_w_o_2"][0]),
        "ffn2": ffn_chunks(a["ffn_w_gate_2"][1], a["ffn_w_up_2"][1], a["ffn_w_down_2"][1]),
    }
    for name, n in STAGES:
        assert parts[name].shape == (n, P, D), (name, parts[name].shape)
    return np.concatenate([parts[name] for name, _ in STAGES])


def feature_tiles(v):
    padded = np.zeros(-(-v.shape[0] // P) * P, v.dtype)
    padded[:v.shape[0]] = v
    return padded.reshape(-1, P).T


def lay_out_small(a):
    out = np.zeros((P, N_SMALL), np.float32)

    def put(name, value):
        at, n = AT[name]
        out[:, at:at + n] = np.asarray(value).reshape(P, n)

    token, row = np.arange(S), np.arange(P)
    put("ident", np.eye(P))
    put("mask", np.where(row[None, :] <= row[:, None], 0.0, NEG))
    end = np.arange(NC) * CS + CL - 1
    t = np.arange(TT)[None, :] * P + row[:, None]
    put("cmpmask", np.where(end <= t[:, :, None], 0.0, NEG))
    put("rowok", t >= CL - 1)
    put("blk2", row[:, None] // HD == np.arange(2))
    put("ones", np.ones((P, 2)))
    put("eps", np.tile([EPS, HD * EPS], (P, 1)))
    for name, dim, first in (("64", HD, 0), ("32", ROPE, HD)):
        inv = (np.float32(10000.0) ** (-np.arange(0, dim, 2, dtype=np.float32) / np.float32(dim))).astype(np.float32)
        angle = (token.astype(np.float32)[None, :] * inv[:, None]).astype(np.float32)
        table = np.tile(angle, (P // (dim // 2), 1))
        put("c" + name, np.cos(table))
        put("s" + name, np.sin(table))
        rot = np.zeros((P, P))
        for at in range(first, P if first == 0 else first + dim, dim):
            for j in range(dim // 2):
                rot[at + dim // 2 + j, at + j] = -1.0
                rot[at + j, at + dim // 2 + j] = 1.0
        put("rot" + name, rot)
    norms = [a["norm1_g"], a["norm2_g"], a["norm_mix_2"][0], a["norm_ffn_2"][0], a["norm_mix_2"][1],
             a["norm_ffn_2"][1], a["norm_final_2"]]
    put("norm", np.concatenate([feature_tiles(g) for g in norms], 1))
    put("rcw", np.concatenate([feature_tiles(w) for w in a["rnn_conv_w"]], 1))
    for name, key in (("rcb", "rnn_conv_b"), ("rba", "rg_b_a"), ("rbx", "rg_b_x"), ("lam", "lru_lambda")):
        put(name, feature_tiles(a[key]))
    put("hg", np.stack([np.tile(a[n], 2) for n in ("q_norm_g", "k_cmp_norm_g", "k_slc_norm_g", "k_win_norm_g")], 1))
    for name, key in (("pek", "cmp_pe_k"), ("pev", "cmp_pe_v")):
        put(name, np.repeat(a[key].reshape(CL // 2, P).T, 2, axis=1))
    put("w2k", np.tile(a["cmp_w2_k"], (1, 2)))
    put("w2v", a["cmp_w2_v"])
    put("fcw0", np.concatenate([feature_tiles(w) for half in (slice(0, FF0), slice(FF0, None))
                                for w in a["ffn_conv_w"][:, half]], 1))
    put("fcb0", np.concatenate([feature_tiles(a["ffn_conv_b"][half]) for half in (slice(0, FF0), slice(FF0, None))], 1))
    for n in (1, 2):
        put(f"fcw{n}", np.concatenate([feature_tiles(w) for w in a["ffn_conv_w_2"][n - 1]], 1))
        put(f"fcb{n}", feature_tiles(a["ffn_conv_b_2"][n - 1]))
    put("ln2", np.concatenate([feature_tiles(a["b_q_norm_2"][0]), feature_tiles(a["b_kv_norm_2"][0])], 1))
    return out


def kernel(**inputs):
    import concourse.bacc as bacc
    from concourse.bass_utils import run_bass_kernel_spmd

    a = {name: np.asarray(value) for name, value in inputs.items()}
    arrays = {
        "weight_stream": lay_out_weights(a),
        "small_in": lay_out_small(a),
        "x_in": np.ascontiguousarray(a["x"][0].T.reshape(DT, P, S).transpose(1, 0, 2)),
    }
    nc = bacc.Bacc("TRN2", target_bir_lowering=False, num_devices=1)
    args = [nc.dram_tensor(n, v.shape, mybir.dt.from_np(v.dtype), kind="ExternalInput").ap() for n, v in arrays.items()]
    out = nc.dram_tensor("out", (P, DT, S), F32, kind="ExternalOutput").ap()
    build(nc, *args, out)
    r = run_bass_kernel_spmd(nc, [arrays], core_ids=[0])
    y = r.results[0]["out"]
    return np.ascontiguousarray(y.transpose(2, 1, 0).reshape(1, S, D))
```

```python
from contextlib import ExitStack

import numpy as np

import concourse.bass as bass
from concourse import mybir

F32 = mybir.dt.float32
F32R = mybir.dt.float32r
BF16 = mybir.dt.bfloat16
ALU = mybir.AluOpType
ACT = mybir.ActivationFunctionType
AX = mybir.AxisListType

P = 128
S = 256
TT = S // P
D = 1024
DT = D // P
D_RNN, RNN_BLOCKS = 1344, 16
BW = D_RNN // RNN_BLOCKS
RT = -(-D_RNN // P)
LRU_C = 8.0
NH, NKV, HD = 16, 4, 64
KVW = NKV * HD
CL, CS = 32, 16
NC = (S - CL) // CS + 1
FF0, FF2 = 3072, 2816
QL, KVL, ROPE = 384, 256, 32
EPS = 1e-6
NEG = -1e30

RAW = 3
LATE = 3
RING = 6
WIN = 124
BODY = 6


def gate_blocks():
    out = []
    for m in range(RT):
        lo = BW * (P * m // BW)
        hi = BW * (min(P * m + P - 1, D_RNN - 1) // BW + 1) - 1
        for gate in range(2):
            out += [(gate, m, k) for k in range(lo // P, hi // P + 1)]
    return out


GATES = gate_blocks()
FFN_BLOCKS = {0: FF0 // P, 1: FF2 // P, 2: FF2 // P}

STAGES = [("kvc", 4), ("rgate", RT), ("w1", 4), ("rx", RT), ("lru", -(-len(GATES) // 8)), ("v", 4),
          ("g", 1), ("k", 4), ("q", 8), ("yr", RT), ("mg", 16), ("ao", 8), ("wo", 8),
          ("ffn0", 3 * FFN_BLOCKS[0]),
          ("q1", 8), ("k1", 8), ("v1", 8), ("wo1", 8), ("ffn1", 3 * FFN_BLOCKS[1]),
          ("c2", 6), ("uq", 6), ("uk", 2), ("uv", 2), ("wo2", 8), ("ffn2", 3 * FFN_BLOCKS[2])]
BASE, N_CHUNKS = {}, 0
for _name, _n in STAGES:
    BASE[_name] = N_CHUNKS
    N_CHUNKS += _n
SIZE = dict(STAGES)



SMALL = [("norm", 7 * DT), ("ones", 2), ("eps", 2), ("ident", 128), ("mask", 128), ("cmpmask", TT * NC), ("rowok", TT), ("blk2", 2),
         ("c64", S), ("s64", S), ("rot64", P), ("c32", S), ("s32", S),
         ("rcw", 4 * RT), ("rcb", RT), ("rba", RT), ("rbx", RT), ("lam", RT),
         ("hg", 4), ("pek", CL // 2), ("pev", CL // 2), ("w2k", P), ("w2v", HD),
         ("fcw0", 6 * FFN_BLOCKS[0]), ("fcb0", 2 * FFN_BLOCKS[0]), ("fcw1", 3 * FFN_BLOCKS[1]),
         ("fcb1", FFN_BLOCKS[1]), ("fcw2", 3 * FFN_BLOCKS[2]), ("fcb2", FFN_BLOCKS[2]),
         ("ln2", 5)]
AT, N_SMALL = {}, 0
for _name, _n in SMALL:
    AT[_name] = (N_SMALL, _n)
    N_SMALL += _n

N_FIRST = AT["ident"][0]

TILE_STAGES = [("kvc", 4, "dve"), ("rgate", RT, "dve"), ("rx", RT, "dve"), ("lru", 2 * RT, "act"),
               ("k", 4, "dve"), ("q", 8, "dve"), ("ao", 8, "dve"),
               ("q1", 8, "act"), ("k1", 8, "act"), ("c2", 6, "dve"), ("uq", NH, "act"), ("uk", 8, "act")]
TILE0, TILE_OWNER = {}, []
for _name, _n, _who in TILE_STAGES:
    TILE0[_name] = len(TILE_OWNER)
    for _ in range(_n):
        TILE_OWNER.append((_who, sum(w == _who for w, _ in TILE_OWNER) + 1))
TILE_BANKS = 4


def lru_groups():
    out = []
    for n, (gate, m, k) in enumerate(GATES):
        if not out or out[-1][:2] != (gate, m):
            out.append((gate, m, []))
        out[-1][2].append((n, k))
    return out


LRU_GROUPS = lru_groups()


def build(nc, weight_stream, small_in, x_in, out):
    with ExitStack() as ctx:
        def sb(name, shape, dt=F32):
            return ctx.enter_context(nc.sbuf_tensor(name, shape, dt))

        def sem(name):
            return ctx.enter_context(nc.semaphore(name))

        w_raw = sb("w_raw", [P, RAW, D])
        w_high = sb("w_high", [P, RING, D], F32R)
        w_low = sb("w_low", [P, RING, D], F32R)
        small = sb("small", [P, N_SMALL])
        x = sb("x", [P, DT, S])
        h_high = sb("h_high", [P, DT, S], F32R)
        h_low = sb("h_low", [P, DT, S], F32R)
        r_high = sb("r_high", [P, RT, S], F32R)
        r_low = sb("r_low", [P, RT, S], F32R)
        ident_b = sb("ident_b", [P, P], BF16)
        mask_b = sb("mask_b", [P, P], BF16)
        rstd = sb("rstd", [P, S])
        stats = sb("stats", [P, 464])
        arena = sb("arena", [P, 22904])
        bank = [ctx.enter_context(nc.psum_tensor(f"bank{i}", [P, 512], F32)) for i in range(8)]
        acc = bank[4:8]

        def par(name, a=0, n=None):
            at, size = AT[name]
            return small[:, at + a:at + (size if n is None else a + n)]

        def tiles(at, n, w=S):
            return arena[:, at:at + n * w].rearrange("p (k t) -> p k t", t=w)

        ident = par("ident")
        blk2 = par("blk2")
        ones = par("ones", 0, 1)
        eps_col = par("eps", 0, 1)
        eps64_col = par("eps", 1, 1)

        squares = tiles(0, DT)
        x_norm = tiles(4096, DT)
        gelu_gate = tiles(0, RT)
        conv = tiles(2816, RT)
        r_gate = tiles(5632, RT)
        i_gate = tiles(8448, RT)
        decay = tiles(11264, RT)
        kv2 = tiles(2816, 8)
        windows = arena[:, 5632:5632 + CL // 2 * WIN]
        kv_scaled = tiles(8448, 4)
        rx_scaled = tiles(8448, 3)
        cmp_ht = arena[:, 12032:12160]
        cmp_hid = arena[:, 11264:11384]
        cmp_kraw = arena[:, 11384:11444]
        cmp_ksq = arena[:, 11444:11504]
        cmp_hv = arena[:, 11520:12032].rearrange("p (g r c) -> p g r c", g=NKV, r=4)
        q0 = tiles(14080, DT)
        k0 = arena[:, 16128:20224].rearrange("p (b v g t) -> p b v g t", b=2, v=2, g=NKV)
        v0 = arena[:, 20224:21248].rearrange("p (b t c) -> p b t c", b=2, t=TT)
        cmp_v = arena[:, 21248:22272].rearrange("p (g c) -> p g c", g=NKV)
        cmp_k = arena[:, 22272:22392].rearrange("p (v n) -> p v n", v=2)
        head_sq = tiles(22392, 2)
        y_rnn = tiles(0, DT)
        o0 = arena[:, 2048:4096].rearrange("p (t h d) -> p t h d", t=TT, h=NH)
        merge = tiles(4096, 16)
        cmp_p = arena[:, 8192:9216].rearrange("p (t h c) -> p t h c", t=TT, h=NH)
        probs0 = tiles(9216, 3, 384)
        probs_t0 = tiles(10368, 2, 384)
        o_part = arena[:, 11136:11648].rearrange("p (t h d) -> p t h d", t=TT, h=4)
        cmp_s = arena[:, 11648:12128].rearrange("p (t h c) -> p t h c", t=TT, h=NH)
        cmp_pt = tiles(12288, 8, P)
        q1 = tiles(0, 8)
        k1 = arena[:, 2048:6144].rearrange("p (v k t) -> p v k t", v=2, k=8)
        v1 = arena[:, 6144:8192].rearrange("p (t c) -> p t c", t=TT)
        o1 = arena[:, 8192:10240].rearrange("p (t h d) -> p t h d", t=TT, h=NH)
        probs1 = tiles(10240, 3, 384)
        probs_t1 = tiles(11392, 2, 384)
        rope_in = tiles(12288, 2)
        rope_a = tiles(12800, 2)
        rope_b = tiles(13312, 2)
        q2 = tiles(0, NH)
        k2 = tiles(4096, NH)
        v2 = arena[:, 8192:10240].rearrange("p (t c) -> p t c", t=TT)
        o2 = arena[:, 10240:12288].rearrange("p (t h d) -> p t h d", t=TT, h=NH)
        probs2 = tiles(12288, 3, 384)
        probs_t2 = tiles(13440, 2, 384)
        c_raw = tiles(14336, 6)
        c_sq = tiles(15872, 5)
        c_norm = tiles(17152, 5)
        rope_a2 = tiles(18432, 2, 512)
        rope_b2 = tiles(19456, 2, 512)
        c64r = arena[:, 13824:14080]
        s64r = arena[:, 14080:14336]
        scaled_g = tiles(19456, 2)
        scaled_v = tiles(19968, 2)
        taps_g = tiles(20480, 2)
        taps_v = tiles(20992, 2)
        gelu_g = tiles(21504, 2)
        hidden = tiles(22016, 2)

        std_col = stats[:, 0:2]
        rstd_col = stats[:, 2:4]
        lru_k = stats[:, 16:16 + RT]
        lru_kn = stats[:, 32:32 + RT]
        lru_t = [stats[:, 48 + 12 * i:48 + 12 * i + RT] for i in range(4)]
        cmp_std = stats[:, 98:99]
        cmp_rstd = stats[:, 99:100]
        head_std = stats[:, 100:148].rearrange("p (t e j) -> p t e j", t=TT, j=2)
        head_rstd = stats[:, 148:196].rearrange("p (t e j) -> p t e j", t=TT, j=2)
        nsa_gate = stats[:, 200:296].rearrange("p (t h b) -> p t h b", t=TT, b=3)
        neg_max = stats[:, 296:328].rearrange("p (h t) -> p h t", t=TT)
        sums = stats[:, 328:360].rearrange("p (t h) -> p t h", t=TT)
        weights_o = stats[:, 360:392].rearrange("p (t h) -> p t h", t=TT)
        cmp_max = stats[:, 392:424].rearrange("p (t h) -> p t h", t=TT)
        cmp_sum = stats[:, 424:456].rearrange("p (t h) -> p t h", t=TT)
        c_std = stats[:, 456:460]
        c_rstd = stats[:, 460:464]

        chunk_loaded = [sem(f"chunk_loaded{i}") for i in range(RAW)]
        high_ready = sem("high_ready")
        low_ready = sem("low_ready")
        chunk_used = sem("chunk_used")
        norm_loaded = sem("norm_operands_loaded")
        small_loaded = sem("small_loaded")
        x_loaded = sem("x_loaded")
        out_stored = sem("out_stored")
        consts_ready = sem("consts_ready")
        zeros_ready = sem("zeros_ready")
        fill_done = sem("fill_done")
        dve_step = sem("dve_step")
        act_step = sem("act_step")
        tile_free = {"act": sem("tile_read_act"), "dve": sem("tile_read_dve")}
        acc_read = sem("accumulator_banks_read")
        acc_done = sem("accumulator_banks_done")
        x_squared = sem("x_squared")
        squares_ready = sem("squares_added")
        sumsq_ready = sem("sumsq_ready")
        std_ready = sem("std_ready")
        rstd_ready = sem("rstd_ready")
        norm_ready = sem("norm_ready")
        h_high_ready = sem("h_high_ready")
        h_low_ready = sem("h_low_ready")
        kv2_ready = sem("kv2_ready")
        r_high_ready = sem("r_high_ready")
        r_low_ready = sem("r_low_ready")
        windows_ready = sem("windows_ready")
        cmp_ht_ready = sem("cmp_hidden_ready")
        cmp_ht_turned = sem("cmp_hidden_turned")
        cmp_hid_ready = sem("cmp_hid_ready")
        cmp_hv_ready = sem("cmp_hv_ready")
        cmp_kv_ready = sem("cmp_kv_ready")
        cmp_sq_ready = sem("cmp_sq_ready")
        cmp_sumsq_ready = sem("cmp_sumsq_ready")
        cmp_std_ready = sem("cmp_std_ready")
        cmp_rstd_ready = sem("cmp_rstd_ready")
        cmp_spread = sem("cmp_spread")
        tap_ready = sem("first_tap_ready")
        conv_ready = sem("conv_ready")
        decay_ready = sem("decay_ready")
        var_ready = sem("input_scale_squared_ready")
        scale_ready = sem("input_scale_ready")
        scan_ready = sem("scan_ready")
        gated_ready = sem("gated_scan_ready")
        heads_scaled = sem("heads_scaled")
        head_sq_ready = sem("head_squares_ready")
        head_sumsq_done = sem("head_sumsq_done")
        head_std_ready = sem("head_std_ready")
        head_rstd_ready = sem("head_rstd_ready")
        head_spread = sem("head_spread")
        head_normed = sem("head_normed")
        scores_ready = sem("scores_ready")
        max_ready = sem("max_ready")
        probs_ready = sem("probs_ready")
        probs_turned = sem("probs_turned")
        probs_copied = sem("probs_copied")
        pv_done = sem("pv_done")
        o_read = sem("o_read")
        cmp_scores = sem("cmp_scores")
        cmp_shifted = sem("cmp_shifted")
        cmp_probs = sem("cmp_probs")
        cmp_turned = sem("cmp_turned")
        cmp_copied = sem("cmp_copied")
        cmp_pv = sem("cmp_pv")
        cmp_done = sem("cmp_done")
        o_turned = sem("o_turned")
        mg_scaled = sem("merge_gates_scaled")
        merge_gated = sem("merge_gates_ready")
        z_ready = sem("merged_ready")
        rope_turned = sem("rope_turned")
        rope_done = sem("rope_done")
        c_sq_ready = sem("latent_squares_ready")
        c_sumsq = sem("latent_sumsq_ready")
        c_std_ready = sem("latent_std_ready")
        c_rstd_ready = sem("latent_rstd_ready")
        c_spread = sem("latent_rstd_spread")
        c_normed = sem("latent_normed")
        k2_ready = sem("mla_keys_ready")
        g_scaled = sem("ffn_gate_scaled")
        v_scaled = sem("ffn_value_scaled")
        tap_g = sem("ffn_first_tap_gate")
        tap_g2 = sem("ffn_second_tap_gate")
        conv_g = sem("ffn_conv_gate")
        tap_v = sem("ffn_first_tap_value")
        tap_v2 = sem("ffn_second_tap_value")
        conv_v = sem("ffn_conv_value")
        gelu_ready = sem("ffn_gelu")
        hidden_ready = sem("ffn_hidden")
        hid_high = sem("ffn_hidden_high")
        hid_low = sem("ffn_hidden_low")

        FFN_STEP0 = {0: 0, 1: FFN_BLOCKS[0], 2: FFN_BLOCKS[0] + FFN_BLOCKS[1]}
        CONV_V0 = FFN_BLOCKS[0]
        ACC_V, ACC_YR, ACC_WO, ACC_FFN0, ACC_V1, ACC_WO1, ACC_FFN1, ACC_V2, ACC_WO2, ACC_FFN2 = range(10)
        R_CMP, R_CONV, R_SCAN = 0, 1, 1 + RT
        R_O = [1 + 2 * RT + DT * n for n in range(3)]
        H_N = {0: 0, 1: 4 + 8, 2: 16, 3: 20, 4: 24, 5: 28 + 5}
        H_Z, H_C = 4, 28

        def f(ap):
            return ap.bitcast(F32)

        block = ctx.enter_context(nc.Block())

        def tile_read(eng, stage, i):
            who, n = TILE_OWNER[TILE0[stage] + i]
            eng.wait_ge(tile_free[who], n)

        MG_EARLY = 4
        MG_PER_BRANCH = (SIZE["mg"] - MG_EARLY) // 2

        def mg_bank(i):
            return bank[{1: 6, 2: 5}.get(i, 7)][:, 0:S]

        NORM_CHUNKS = [None, BASE["ffn0"], BASE["q1"], BASE["ffn1"], BASE["c2"], BASE["ffn2"], N_CHUNKS]
        ACC_OF_NORM = [None, ACC_WO, ACC_FFN0, ACC_WO1, ACC_FFN1, ACC_WO2, ACC_FFN2]

        def acc_bank_done(eng, n, p):
            if p < 3:
                eng.wait_ge(acc_done, 3 * (n - 1) + p + 1)
            else:
                eng.wait_ge(chunk_used, NORM_CHUNKS[n])

        def pieces(ap, p):
            return ap[:, 2 * p:2 * p + 2, :]

        def lru_posts(eng, split, post):
            at = 0
            for q in range(SIZE["lru"]):
                c = BASE["lru"] + q
                eng.wait_ge(chunk_used, c + 1)
                while at < len(LRU_GROUPS) and LRU_GROUPS[at][2][-1][0] // 8 <= q:
                    post(at, *LRU_GROUPS[at][:2])
                    at += 1
                split(c + RING)

        @block.sync
        def _(sp):
            def load(c, turn=0, wait=True):
                if wait:
                    sp.wait_ge(low_ready, turn + c - RAW + 1)
                sp.dma_start(w_raw[:, c % RAW, :], weight_stream[turn + c]).then_inc(chunk_loaded[c % RAW], 16)

            for c in range(BODY):
                load(c, wait=c >= RAW)
            turns = N_CHUNKS // BODY
            with sp.Fori(1, turns) as i:
                for c in range(BODY):
                    load(c, BODY * i)
            for c in range(turns * BODY, N_CHUNKS):
                load(c)
            for p in range(4):
                sp.wait_ge(norm_ready, p + 1)
                sp.dma_start(out[:, 2 * p:2 * p + 2, :], pieces(x_norm, p)).then_inc(out_stored, 16)
            sp.wait_ge(out_stored, 64)

        @block.gpsimd
        def _(pool):
            nc.gpsimd.memset(k0[HD:P, :, 0, :, :], 0.0).then_inc(fill_done, 1)
            pool.wait_ge(fill_done, 1)
            nc.gpsimd.memset(k0[0:HD, :, 1, :, :], 0.0).then_inc(fill_done, 1)
            pool.wait_ge(fill_done, 2)
            nc.gpsimd.memset(cmp_k[HD:P, 0, :], 0.0).then_inc(fill_done, 1)
            pool.wait_ge(fill_done, 3)
            nc.gpsimd.memset(cmp_k[0:HD, 1, :], 0.0).then_inc(fill_done, 1)
            pool.wait_ge(fill_done, 4)
            nc.gpsimd.memset(cmp_hv[:, :, :, :], 0.0).then_inc(fill_done, 1)
            pool.wait_ge(fill_done, 5)
            nc.gpsimd.memset(cmp_v[:, :, :], 0.0).then_inc(zeros_ready, 1)
            pool.wait_ge(zeros_ready, 1)
            pool.wait_ge(acc_read, 4 * ACC_WO + 4)
            nc.gpsimd.memset(k1[HD:P, 0, :, :], 0.0).then_inc(fill_done, 1)
            pool.wait_ge(fill_done, 6)
            nc.gpsimd.memset(k1[0:HD, 1, :, :], 0.0).then_inc(zeros_ready, 1)
            pool.wait_ge(zeros_ready, 2)
            pool.wait_ge(acc_read, 4 * ACC_WO1 + 4)
            nc.gpsimd.memset(k2[96:P, :, :], 0.0).then_inc(zeros_ready, 1)

        @block.tensor
        def _(pe):
            mm = nc.tensor.matmul

            def split_product(out_ap, c, col, high, low, start, stop):
                wh = w_high[:, c % RING, col:col + P]
                wl = w_low[:, c % RING, col:col + P]
                mm(out_ap, wh, high, start=start, stop=False, skip_group_check=True)
                mm(out_ap, wh, low, start=False, stop=False, skip_group_check=True)
                return mm(out_ap, wl, high, start=False, stop=stop, skip_group_check=True)

            def moving_product(out_ap, c, col, n, high, low, start, stop):
                wh = w_high[:, c % RING, col:col + n]
                wl = w_low[:, c % RING, col:col + n]
                mm(out_ap, high, wh, start=start, stop=False, skip_group_check=True)
                mm(out_ap, high, wl, start=False, stop=False, skip_group_check=True)
                return mm(out_ap, low, wh, start=False, stop=stop, skip_group_check=True)

            def chunk_here(c, turn=0):
                pe.wait_ge(low_ready, turn + c + 1)

            def tile_bank(t):
                if t >= TILE_BANKS:
                    who, n = TILE_OWNER[t - TILE_BANKS]
                    pe.wait_ge(tile_free[who], n)
                return bank[t % TILE_BANKS]

            def column_tiles(stage, high, low, h_wait=None, after=None):
                for i in range(SIZE[stage]):
                    c = BASE[stage] + i
                    chunk_here(c)
                    b = tile_bank(TILE0[stage] + i)
                    for k in range(DT):
                        if i == 0 and h_wait:
                            h_wait(k)
                        last = split_product(b[:, 0:S], c, k * P, high[:, k, :], low[:, k, :],
                                             k == 0, k == DT - 1)
                    last.then_inc(chunk_used, 1)
                    if after:
                        after(i)

            def rows_of_bank(c, p, high, low, first, last):
                for m in (2 * p, 2 * p + 1):
                    ins = split_product(acc[p][:, (m % 2) * S:(m % 2 + 1) * S], c, m * P, high, low,
                                        first and m % 2 == 0, last)
                return ins

            def row_chunk(c, high, low, first=False, last=False, sum_next=False):
                for p in range(4):
                    ins = rows_of_bank(c, p, high, low, first, last)
                    if sum_next and p < 3:
                        ins.then_inc(acc_done, 1)
                ins.then_inc(chunk_used, 1)

            def output_projection(stage, high, low, h_wait=None):
                for k in range(DT - LATE):
                    chunk_here(BASE[stage] + k)
                    if h_wait:
                        h_wait(k)
                    row_chunk(BASE[stage] + k, high[:, k, :], low[:, k, :], first=k == 0)
                chunk_here(BASE[stage] + DT - 1)
                if h_wait:
                    h_wait(DT - 1)
                for p in range(4):
                    for k in range(DT - LATE, DT):
                        ins = rows_of_bank(BASE[stage] + k, p, high[:, k, :], low[:, k, :], False, k == DT - 1)
                        if p == 3:
                            ins.then_inc(chunk_used, 1)
                    if p < 3:
                        ins.then_inc(acc_done, 1)

            def norm_sums(n):
                if n:
                    pe.wait_ge(acc_read, 4 * ACC_OF_NORM[n] + 4)
                pe.wait_ge(squares_ready, n + 1)
                for k in range(2):
                    ins = mm(acc[0][:, 0:S], ones.to_broadcast([P, P]), squares[:, k, :], start=k == 0, stop=k == 1)
                if n in (0, 2):
                    for t in range(TT):
                        for k in range(2):
                            ins = mm(acc[1][:, t:t + 1], squares[:, k, t * P:(t + 1) * P], ones,
                                     start=k == 0, stop=k == 1)
                ins.then_inc(sumsq_ready, 1)

            def attention(n, q, kpad, v, probs, probs_t, between=None):
                def scores(h):
                    if h >= 3:
                        pe.wait_ge(probs_ready, NH * n + h - 2)
                    b = bank[h % 3]
                    mm(b[:, 0:P], q(h, 0), kpad(h)[:, 0:P], start=True, stop=False, skip_group_check=True)
                    mm(b[:, 0:P], ident_b[:, :], mask_b[:, :], start=False, stop=True, skip_group_check=True)
                    mm(b[:, P:3 * P], q(h, 1), kpad(h), start=True, stop=False, skip_group_check=True)
                    mm(b[:, 2 * P:3 * P], ident_b[:, :], mask_b[:, :], start=False, stop=True,
                       skip_group_check=True).then_inc(scores_ready, 1)

                def turn(h):
                    pe.wait_ge(probs_ready, NH * n + h + 1)
                    if h >= 2:
                        pe.wait_ge(probs_copied, NH * n + h - 1)
                    for j in range(3):
                        ins = nc.tensor.transpose(bank[3 + h % 2][:, j * P:(j + 1) * P],
                                                  probs[:, h % 3, j * P:(j + 1) * P], ident)
                    ins.then_inc(probs_turned, 1)

                def values(h):
                    pe.wait_ge(probs_copied, NH * n + h + 1)
                    g = h // 4
                    if h % 4 == 0 and g >= 2:
                        pe.wait_ge(o_read, 4 * n + g - 1)
                    b = bank[5 + g % 2]
                    pt = probs_t[:, h % 2, :]
                    at = (h % 4) * HD
                    mm(b[:, at:at + HD], pt[:, 0:P], v(h, 0), start=True, stop=True)
                    mm(b[:, S + at:S + at + HD], pt[:, P:2 * P], v(h, 0), start=True, stop=False)
                    mm(b[:, S + at:S + at + HD], pt[:, 2 * P:3 * P], v(h, 1), start=False,
                       stop=True).then_inc(pv_done, 1)

                for h in range(NH + 3):
                    if h < NH:
                        scores(h)
                    if n == 0 and h == 2:
                        pe.wait_ge(cmp_done, 4)
                    if 2 <= h < NH + 2:
                        turn(h - 2)
                    if h >= 3:
                        values(h - 3)
                    if between and h < NH:
                        between(h)
                pe.wait_ge(o_read, 4 * n + 4)

            def turn_output(n, o):
                flat = o.rearrange("p t h d -> p t (h d)")
                for m in range(DT):
                    for t in range(TT):
                        ins = nc.tensor.transpose(bank[m][:, t * P:(t + 1) * P],
                                                  flat[:, t, m * P:(m + 1) * P], ident)
                    ins.then_inc(o_turned, 1)
                pe.wait_ge(r_low_ready, R_O[n] + DT)

            def feed_forward(n, acc_use):
                base, s0, blocks = BASE[f"ffn{n}"], FFN_STEP0[n], FFN_BLOCKS[n]

                def gate_and_up(j, c, turn=0, first=False):
                    for which in range(2):
                        chunk_here(c + which, turn)
                        for k in range(DT):
                            if first and which == 0 and k % 2 == 0:
                                pe.wait_ge(h_low_ready, H_N[2 * n + 1] + k // 2 + 1)
                            last = split_product(bank[2 * which + j % 2][:, 0:S], c + which, k * P,
                                                 h_high[:, k, :], h_low[:, k, :], k == 0, k == DT - 1)
                        last.then_inc(chunk_used, 1)
                        if first and which == 0:
                            norm_sums(2 * n + 1)

                def down(j, c, turn=0, more=0, first=False, last=False, sum_next=False):
                    pe.wait_ge(hid_low, s0 + j + more + 1)
                    chunk_here(c, turn)
                    row_chunk(c, r_high[:, j % 2, :], r_low[:, j % 2, :], first=first, last=last,
                              sum_next=sum_next)

                gate_and_up(0, base, first=True)
                gate_and_up(1, base + 2)
                pe.wait_ge(std_ready, 2 * n + 2)
                down(0, base + 4, first=True)
                turns = (blocks - 3) // 2
                with pe.Fori(0, turns) as i:
                    for q in range(2):
                        c = base + 5 + 3 * q
                        gate_and_up(2 + q, c, BODY * i)
                        down(1 + q, c + 2, BODY * i, more=2 * i)
                for j in range(2 + 2 * turns, blocks):
                    c = base + 3 * j - 1
                    gate_and_up(j, c)
                    down(j - 1, c + 2)
                down(blocks - 1, base + 3 * blocks - 1, last=True, sum_next=True)

            pe.wait_ge(norm_loaded, 16)
            column_tiles("kvc", h_high, h_low,
                         lambda k: pe.wait_ge(h_low_ready, H_N[0] + k // 2 + 1) if k % 2 == 0 else None,
                         after=lambda i: norm_sums(0) if i == 0 else None)
            column_tiles("rgate", h_high, h_low)
            pe.wait_ge(small_loaded, 16)
            pe.wait_ge(r_low_ready, R_CMP + 1)
            flat_high, flat_low = (r[:, :, :].rearrange("p k t -> p (k t)") for r in (r_high, r_low))
            for j in range(CL // 2):
                c = BASE["w1"] + j // 4
                if j % 4 == 0:
                    chunk_here(c)
                ins = moving_product(acc[2][0:WIN, 0:2 * P], c, (j % 4) * 2 * P, 2 * P,
                                     flat_high[:, j * WIN:(j + 1) * WIN], flat_low[:, j * WIN:(j + 1) * WIN],
                                     j == 0, j == CL // 2 - 1)
                if j % 4 == 3:
                    ins.then_inc(chunk_used, 1)

            def compression(i):
                if i == 0:
                    pe.wait_ge(cmp_ht_ready, 1)
                    nc.tensor.transpose(acc[3][:, 0:WIN], cmp_ht[0:WIN, :], ident[0:WIN, 0:WIN]).then_inc(cmp_ht_turned, 1)
                if i == 3:
                    pe.wait_ge(std_ready, 1)
                    pe.wait_ge(cmp_hv_ready, 1)
                    mm(acc[0][:, 0:60], par("w2k"), cmp_hid[:, 0:60], start=True, stop=True)
                    for g in range(NKV):
                        ins = mm(acc[1][:, g * HD:(g + 1) * HD], cmp_hv[:, g, :, :].rearrange("p r c -> p (r c)"),
                                 par("w2v"), start=True, stop=True)
                    ins.then_inc(cmp_kv_ready, 1)
                if i == 5:
                    pe.wait_ge(cmp_sq_ready, 1)
                    mm(acc[2][0:60, 0:1], cmp_ksq, blk2[:, 0:1], start=True, stop=True).then_inc(cmp_sumsq_ready, 1)
                if i == 8:
                    pe.wait_ge(cmp_rstd_ready, 1)
                    mm(acc[3][:, 0:60], cmp_rstd[0:60, :].to_broadcast([60, P]), ident[0:60, 0:60],
                       start=True, stop=True).then_inc(cmp_spread, 1)

            column_tiles("rx", h_high, h_low, after=compression)
            for t, (gate, m, blocks) in enumerate(LRU_GROUPS):
                b = tile_bank(TILE0["lru"] + t)
                pe.wait_ge(r_low_ready, R_CONV + blocks[-1][1] + 1)
                for n, (at, k) in enumerate(blocks):
                    c = BASE["lru"] + at // 8
                    if at % 8 == 0:
                        chunk_here(c)
                    ins = split_product(b[:, 0:S], c, at % 8 * P, r_high[:, k, :], r_low[:, k, :],
                                        n == 0, n == len(blocks) - 1)
                    if at % 8 == 7 or at == len(GATES) - 1:
                        ins.then_inc(chunk_used, 1)
            pe.wait_ge(cmp_spread, 1)
            pe.wait_ge(head_normed, 1)
            for i in range(4):
                c = BASE["v"] + i
                chunk_here(c)
                for k in (2 * i, 2 * i + 1):
                    for t in range(TT):
                        ins = moving_product(acc[t][:, :], c, (k % 2) * 512, 512, h_high[:, k, t * P:(t + 1) * P],
                                             h_low[:, k, t * P:(t + 1) * P], k == 0, k == DT - 1)
                ins.then_inc(chunk_used, 1)
            c = BASE["g"]
            chunk_here(c)
            for k in range(DT):
                for t in range(TT):
                    ins = moving_product(acc[2 + t][:, 0:3 * NH], c, k * P, 3 * NH, h_high[:, k, t * P:(t + 1) * P],
                                         h_low[:, k, t * P:(t + 1) * P], k == 0, k == DT - 1)
            ins.then_inc(chunk_used, 1)

            def head_sums(e):
                pe.wait_ge(head_sq_ready, e + 1)
                if e == 0:
                    pe.wait_ge(acc_read, 4 * ACC_V + 4)
                for t in range(TT):
                    at = (t * 12 + e) * 2
                    ins = mm(acc[0][:, at:at + 2], head_sq[:, e % 2, t * P:(t + 1) * P], blk2,
                             start=True, stop=True)
                ins.then_inc(head_sumsq_done, 1)

            column_tiles("k", h_high, h_low, after=lambda i: head_sums(i - 1) if i else None)
            column_tiles("q", h_high, h_low, after=lambda i: head_sums(i + 3))
            head_sums(11)

            def spread_heads(e):
                if e == 0:
                    pe.wait_ge(head_rstd_ready, 1)
                if e >= TILE_BANKS:
                    pe.wait_ge(head_normed, 1 + e - TILE_BANKS + 1)
                for t in range(TT):
                    for j in range(2):
                        ins = mm(bank[e % TILE_BANKS][HD * j:HD * (j + 1), t * P:(t + 1) * P],
                                 head_rstd[:, t, e, j:j + 1].to_broadcast([P, HD]), ident, start=True, stop=True)
                ins.then_inc(head_spread, 1)

            tile_read(pe, "q", 7)
            pe.wait_ge(head_std_ready, 2)
            for k in range(RT):
                chunk_here(BASE["yr"] + k)
                pe.wait_ge(r_low_ready, R_SCAN + k + 1)
                row_chunk(BASE["yr"] + k, r_high[:, k, :], r_low[:, k, :], first=k == 0, last=k == RT - 1)
                spread_heads(k)
            spread_heads(RT)
            pe.wait_ge(head_normed, 1 + 12)

            def merge_gates(i, halves=(0, 1)):
                c = BASE["mg"] + i
                if 0 in halves:
                    chunk_here(c)
                    if i >= 3:
                        pe.wait_ge(mg_scaled, 1 if i == 3 else i)
                b = mg_bank(i)
                for half in halves:
                    for k in range(4 * half, 4 * half + 4):
                        ins = split_product(b, c, k * P, h_high[:, k, :], h_low[:, k, :], k == 0, k == DT - 1)
                if 1 in halves:
                    ins.then_inc(chunk_used, 1)

            pe.wait_ge(consts_ready, 1)
            for t in range(TT):
                for h in range(NH):
                    at = (t * NH + h) * 16
                    ins = mm(bank[0][:, at:at + NC], q0[:, h // 2, t * P:(t + 1) * P],
                             cmp_k[:, h % 2, h // 4:h // 4 + NKV * (NC - 1) + 1:NKV], start=True, stop=True)
            ins.then_inc(cmp_scores, 1)
            pe.wait_ge(acc_read, 4 * ACC_YR + 4)
            for i in range(3):
                merge_gates(i)
            pe.wait_ge(cmp_probs, 1)
            for i in range(8):
                ins = nc.tensor.transpose(bank[1 + i // 4][:, (i % 4) * P:(i % 4 + 1) * P],
                                          cmp_p[:, i // 4, 4 * (i % 4):4 * (i % 4) + 4, :]
                                          .rearrange("p h c -> p (h c)"), ident)
            ins.then_inc(cmp_turned, 1)
            merge_gates(3)
            pe.wait_ge(cmp_copied, 2)
            pe.wait_ge(mg_scaled, 3)
            for t in range(TT):
                for g in range(NKV):
                    ins = mm(bank[3 + 2 * t + g // 2][:, (g % 2) * 256:(g % 2 + 1) * 256],
                             cmp_pt[:, 4 * t + g, :], cmp_v[:, g, :], start=True, stop=True)
                ins.then_inc(cmp_pv, 1)

            def merge_between(h, n):
                if h < 2 * MG_PER_BRANCH:
                    merge_gates(MG_EARLY + MG_PER_BRANCH * n + h // 2, (h % 2,))

            for n in range(2):
                attention(n, lambda h, t: q0[:, h // 2, t * P:(t + 1) * P],
                          lambda h: k0[:, n, h % 2, h // 4, :],
                          lambda h, t: v0[:, n, t, (h // 4) * HD:(h // 4 + 1) * HD], probs0, probs_t0,
                          lambda h: merge_between(h, n))
            pe.wait_ge(mg_scaled, 16)
            turn_output(0, o0)
            column_tiles("ao", r_high, r_low)
            pe.wait_ge(acc_read, 4 * ACC_YR + 4)
            output_projection("wo", h_high, h_low, lambda k: pe.wait_ge(h_low_ready, H_Z + k + 1))
            feed_forward(0, ACC_FFN0)


            def turn_rope(e):
                if e == 0:
                    pe.wait_ge(std_ready, 3)
                tile_read(pe, "q1" if e < 8 else "k1", e % 8)
                if e >= 2:
                    pe.wait_ge(rope_done, e - 1)
                mm(acc[e % 2][:, 0:S], par("rot64"), rope_in[:, e % 2, :], start=True,
                   stop=True).then_inc(rope_turned, 1)

            column_tiles("q1", h_high, h_low,
                         lambda k: pe.wait_ge(h_low_ready, H_N[2] + k // 2 + 1) if k % 2 == 0 else None,
                         after=lambda i: turn_rope(i - 1) if i else norm_sums(2))
            column_tiles("k1", h_high, h_low, after=lambda i: turn_rope(i + 7))
            turn_rope(15)
            pe.wait_ge(rope_done, 16)

            def values_all(stage, n_k):
                for k in range(n_k):
                    c = BASE[stage] + k
                    chunk_here(c)
                    for t in range(TT):
                        for half in range(2):
                            ins = moving_product(acc[2 * t + half][:, :], c, half * 512, 512,
                                                 h_high[:, k, t * P:(t + 1) * P], h_low[:, k, t * P:(t + 1) * P],
                                                 k == 0, k == n_k - 1)
                    ins.then_inc(chunk_used, 1)

            values_all("v1", DT)
            pe.wait_ge(zeros_ready, 2)
            tile_read(pe, "k1", 7)
            pe.wait_ge(acc_read, 4 * ACC_V1 + 4)
            attention(2, lambda h, t: q1[:, h // 2, t * P:(t + 1) * P], lambda h: k1[:, h % 2, h // 2, :],
                      lambda h, t: v1[:, t, h * HD:(h + 1) * HD], probs1, probs_t1)
            turn_output(1, o1)
            output_projection("wo1", r_high, r_low)
            feed_forward(1, ACC_FFN1)

            column_tiles("c2", h_high, h_low,
                         lambda k: pe.wait_ge(h_low_ready, H_N[4] + k // 2 + 1) if k % 2 == 0 else None,
                         after=lambda i: norm_sums(4) if i == 0 else None)
            pe.wait_ge(std_ready, 5)
            pe.wait_ge(c_sq_ready, 1)
            for which, (a, b) in enumerate(((0, 3), (3, 5))):
                for t in range(TT):
                    for e in range(a, b):
                        ins = mm(acc[0][:, 2 * which + t:2 * which + t + 1], c_sq[:, e, t * P:(t + 1) * P], ones,
                                 start=e == a, stop=e == b - 1)
            ins.then_inc(c_sumsq, 1)
            pe.wait_ge(c_rstd_ready, 1)
            for which in range(2):
                for t in range(TT):
                    ins = mm(acc[1 + which][:, t * P:(t + 1) * P],
                             c_rstd[:, 2 * which + t:2 * which + t + 1].to_broadcast([P, P]), ident,
                             start=True, stop=True)
            ins.then_inc(c_spread, 1)
            for h in range(NH):
                b = tile_bank(TILE0["uq"] + h)
                for k in range(3):
                    n = 3 * h + k
                    c = BASE["uq"] + n // 8
                    if n % 8 == 0:
                        chunk_here(c)
                    if h == 0:
                        pe.wait_ge(h_low_ready, H_C + k + 1)
                    ins = split_product(b[:, 0:S], c, n % 8 * P, h_high[:, k, :], h_low[:, k, :], k == 0, k == 2)
                    if n % 8 == 7:
                        ins.then_inc(chunk_used, 1)
            pe.wait_ge(h_low_ready, H_C + 5)
            for m in range(8):
                b = tile_bank(TILE0["uk"] + m)
                for k in range(2):
                    n = 2 * m + k
                    c = BASE["uk"] + n // 8
                    if n % 8 == 0:
                        chunk_here(c)
                    ins = split_product(b[:, 0:S], c, n % 8 * P, h_high[:, 3 + k, :], h_low[:, 3 + k, :],
                                        k == 0, k == 1)
                    if n % 8 == 7:
                        ins.then_inc(chunk_used, 1)
            for k in range(2):
                c = BASE["uv"] + k
                chunk_here(c)
                for t in range(TT):
                    for half in range(2):
                        ins = moving_product(acc[2 * t + half][:, :], c, half * 512, 512,
                                             h_high[:, 3 + k, t * P:(t + 1) * P],
                                             h_low[:, 3 + k, t * P:(t + 1) * P], k == 0, k == 1)
                ins.then_inc(chunk_used, 1)
            tile_read(pe, "uk", 7)
            pe.wait_ge(k2_ready, 1)
            pe.wait_ge(rope_done, 16 + 1 + 8)
            pe.wait_ge(zeros_ready, 3)
            pe.wait_ge(acc_read, 4 * ACC_V2 + 4)
            attention(3, lambda h, t: q2[:, h, t * P:(t + 1) * P], lambda h: k2[:, h, :],
                      lambda h, t: v2[:, t, h * HD:(h + 1) * HD], probs2, probs_t2)
            turn_output(2, o2)
            output_projection("wo2", r_high, r_low)
            feed_forward(2, ACC_FFN2)
            norm_sums(6)

        @block.scalar
        def _(act):
            fn = nc.scalar.activation

            def split_high(c, i=None):
                if c >= N_CHUNKS:
                    return
                turn, turn_dma = (0, 0) if i is None else (BODY * i, 16 * (BODY // RAW) * i)
                act.wait_ge(chunk_loaded[c % RAW], turn_dma + 16 * (c // RAW + 1))
                if c >= RING:
                    act.wait_ge(chunk_used, turn + c - RING + 1)
                fn(w_high[:, c % RING, :], w_raw[:, c % RAW, :], ACT.Copy).then_inc(high_ready, 1)

            def stage(name, post, count=None):
                for i in range(count or SIZE[name]):
                    c = BASE[name] + i
                    act.wait_ge(chunk_used, c + 1)
                    post(i)
                    split_high(c + RING)

            def stage_behind(name, post):
                for i in range(SIZE[name]):
                    c = BASE[name] + i
                    split_high(c + RING)
                    post(i)

            def late_splits(end, count):
                for c in range(end - count, end):
                    split_high(c + RING)

            def tile(name, i):
                return bank[(TILE0[name] + i) % TILE_BANKS][:, 0:S]

            def freed(ins):
                ins.then_inc(tile_free["act"], 1)

            def read_acc(p, ap, scale=1.0):
                fn(ap, acc[p][:, :], ACT.Identity, scale=scale).then_inc(acc_read, 1)

            def norm(n):
                if n == 0:
                    act.wait_ge(x_loaded, 16)
                for p in range(4):
                    if n:
                        act.wait_ge(acc_read, 4 * ACC_OF_NORM[n] + p + 1)
                    if n == 1 and p >= 2:
                        acc_bank_done(act, n, 3)
                    if n < 6:
                        for k in (2 * p, 2 * p + 1):
                            ins = fn(h_high[:, k, :], x[:, k, :], ACT.Identity, scale=par("norm", n * DT + k, 1))
                        ins.then_inc(h_high_ready, 1)
                    fn(pieces(squares, p), pieces(x, p), ACT.Square).then_inc(x_squared, 1)

            def roots(n):
                act.wait_ge(sumsq_ready, n + 1)
                ins = fn(rstd[:, :], acc[0][:, 0:S], ACT.Sqrt, bias=eps_col, scale=1.0 / D)
                if n in (0, 2):
                    ins = fn(std_col, acc[1][:, 0:TT], ACT.Sqrt, bias=eps_col, scale=1.0 / D)
                ins.then_inc(std_ready, 1)

            def attention(n, probs, between=None):
                for h in range(NH + 1):
                    if h == NH:
                        if between:
                            between(h)
                        break
                    act.wait_ge(max_ready, NH * n + h + 1)
                    if h >= 3:
                        act.wait_ge(probs_turned, NH * n + h - 2)
                    b = bank[h % 3]
                    fn(probs[:, h % 3, 0:P], b[:, 0:P], ACT.Exp, bias=neg_max[:, h, 0:1],
                       accum_out=sums[:, 0, h:h + 1])
                    fn(probs[:, h % 3, P:3 * P], b[:, P:3 * P], ACT.Exp, bias=neg_max[:, h, 1:2],
                       accum_out=sums[:, 1, h:h + 1]).then_inc(probs_ready, 1)
                    if between:
                        between(h)

            def output_high(n):
                for m in range(DT):
                    act.wait_ge(o_turned, DT * n + m + 1)
                    fn(r_high[:, m, :], bank[m][:, 0:S], ACT.Copy).then_inc(r_high_ready, 1)

            def feed_forward(n):
                base, s0, blocks, both = BASE[f"ffn{n}"], FFN_STEP0[n], FFN_BLOCKS[n], n == 0
                func = ACT.Gelu_apprx_tanh if both else ACT.Gelu

                def tap(name, row, j):
                    at = AT[name][0] + row * blocks
                    return small[:, at + j:at + j + 1] if isinstance(j, int) else small[:, bass.ds(j + at, 1)]

                def step(j, c, i=None):
                    turn, k = (0, 0) if i is None else (BODY * i, 2 * i)
                    act.wait_ge(chunk_used, turn + c + 1)
                    if i is None and j == 0:
                        roots(2 * n + 1)
                    split_high(c + RING, i)
                    act.wait_ge(g_scaled, k + (s0 + j + 1))
                    fn(taps_g[:, j % 2, :], scaled_g[:, j % 2, :], ACT.Identity, scale=tap(f"fcw{n}", 2, k + j),
                       bias=tap(f"fcb{n}", 0, k + j)).then_inc(tap_g, 1)
                    act.wait_ge(chunk_used, turn + c + 2)
                    split_high(c + 1 + RING, i)
                    if both:
                        act.wait_ge(v_scaled, k + (s0 + j + 1))
                        fn(taps_v[:, j % 2, :], scaled_v[:, j % 2, :], ACT.Identity,
                           scale=tap("fcw0", 5, k + j), bias=tap("fcb0", 1, k + j)).then_inc(tap_v, 1)
                    act.wait_ge(conv_g, k + (s0 + j + 1))
                    fn(gelu_g[:, j % 2, :], taps_g[:, j % 2, :], func).then_inc(gelu_ready, 1)
                    if 0 < j < blocks - 1:
                        split_high(c + 2 + RING, i)
                    act.wait_ge(hidden_ready, k + (s0 + j + 1))
                    fn(r_high[:, j % 2, :], hidden[:, j % 2, :], ACT.Copy).then_inc(hid_high, 1)
                    if j == blocks - 1:
                        split_high(c + 2 + RING, i)

                step(0, base)
                turns = (blocks - 2) // 2 - (n == 2)
                with act.Fori(0, turns) as i:
                    for q in range(2):
                        step(1 + q, base + 2 + 3 * q, i)
                for j in range(1 + 2 * turns, blocks):
                    step(j, base + 3 * j - 1)

            act.dma_start(small[:, 0:N_FIRST], small_in[:, 0:N_FIRST]).then_inc(norm_loaded, 16)
            act.dma_start(x[:, :, :], x_in).then_inc(x_loaded, 16)
            act.dma_start(small[:, N_FIRST:], small_in[:, N_FIRST:]).then_inc(small_loaded, 16)
            act.wait_ge(norm_loaded, 16)
            split_high(0)
            norm(0)
            for c in range(1, RING // 2):
                split_high(c)
            act.wait_ge(small_loaded, 16)
            fn(ident_b[:, :], ident, ACT.Copy)
            fn(mask_b[:, :], par("mask"), ACT.Copy).then_inc(consts_ready, 1)
            fn(lru_t[0], par("lam"), ACT.Abs).then_inc(act_step, 1)
            act.wait_ge(act_step, 1)
            fn(lru_t[1], lru_t[0], ACT.Exp, scale=-1.0).then_inc(act_step, 1)
            roots(0)
            for c in range(RING // 2, RING):
                split_high(c)

            def kvc(i):
                tile_read(act, "kvc", i)
                g = 4 * (i // 2) + 2 * (i % 2)
                for j in range(2):
                    rows = slice(HD * j, HD * (j + 1))
                    fn(kv2[0:HD, g + j, :], kv_scaled[rows, i, :], ACT.Copy)
                    ins = fn(kv2[HD:P, g + j, 0:S - 1], kv_scaled[rows, i, 1:S], ACT.Copy)
                ins.then_inc(kv2_ready, 1)

            stage_behind("kvc", kvc)

            def rgate(i):
                tile_read(act, "rgate", i)
                fn(gelu_gate[:, i, :], gelu_gate[:, i, :], ACT.Gelu_apprx_tanh)
                if i == 4:
                    act.wait_ge(windows_ready, 2)
                    fn(r_high[:, :, :].rearrange("p k t -> p (k t)")[:, 0:CL // 2 * WIN], windows,
                       ACT.Copy).then_inc(r_high_ready, 1)

            stage_behind("rgate", rgate)

            def hidden_cmp(i):
                if i < 3:
                    return
                fn(cmp_ht[0:HD, :], acc[2][0:HD, 0:P], ACT.Gelu_apprx_tanh)
                fn(cmp_ht[HD:WIN, :], acc[2][HD:WIN, P:2 * P], ACT.Gelu_apprx_tanh).then_inc(cmp_ht_ready, 1)

            stage("w1", hidden_cmp)

            def conv_high(i):
                act.wait_ge(conv_ready, i + 1)
                fn(r_high[:, i, :], conv[:, i, :], ACT.Copy).then_inc(r_high_ready, 1)

            def rx(i):
                tile_read(act, "rx", i)
                fn(conv[:, i, :], rx_scaled[:, i % 3, :], ACT.Identity, scale=par("rcw", 3 * RT + i, 1),
                   bias=par("rcb", i, 1)).then_inc(tap_ready, 1)
                if i >= 2:
                    conv_high(i - 2)
                if i == 1:
                    act.wait_ge(cmp_ht_turned, 1)
                    fn(cmp_hid[:, 0:60], acc[3][:, 0:60], ACT.Copy)
                    fn(cmp_hid[:, 60:120], acc[3][:, HD:HD + 60], ACT.Copy).then_inc(cmp_hid_ready, 1)
                if i == 4:
                    act.wait_ge(cmp_kv_ready, 1)
                    fn(cmp_kraw, acc[0][:, 0:60], ACT.Identity, scale=par("hg", 1, 1))
                    fn(cmp_ksq, acc[0][:, 0:60], ACT.Square).then_inc(cmp_sq_ready, 1)
                if i == 6:
                    act.wait_ge(cmp_sumsq_ready, 1)
                    fn(cmp_std[0:60, :], acc[2][0:60, 0:1], ACT.Sqrt, bias=eps_col[0:60, :],
                       scale=1.0 / HD).then_inc(cmp_std_ready, 1)

            stage_behind("rx", rx)
            conv_high(RT - 2)
            conv_high(RT - 1)

            def lru_gate(t, gate, m):
                dst, bias = ((r_gate, "rba"), (i_gate, "rbx"))[gate]
                freed(fn(dst[:, m, :], tile("lru", t), ACT.Sigmoid, bias=par(bias, m, 1)))

            lru_posts(act, split_high, lru_gate)
            stage("v", lambda i: None)

            def v_and_gates(i):
                act.wait_ge(rstd_ready, 1)
                for t in range(TT):
                    read_acc(t, v0[:, :, t, :], scale=rstd_col[:, t:t + 1])
                for t in range(TT):
                    fn(stats[:, 200 + 48 * t:248 + 48 * t], acc[2 + t][:, 0:3 * NH],
                       ACT.Sigmoid, scale=rstd_col[:, t:t + 1]).then_inc(acc_read, 1)

            stage("g", v_and_gates)

            def heads(e):
                act.wait_ge(heads_scaled, e + 1)
                fn(head_sq[:, e % 2, :], head_sq[:, e % 2, :], ACT.Square).then_inc(head_sq_ready, 1)
                if e < RT:
                    fn(decay[:, e, :], r_gate[:, e, :], ACT.Exp, scale=lru_k[:, e:e + 1])
                    fn(r_gate[:, e, :], r_gate[:, e, :], ACT.Tanh, scale=lru_kn[:, e:e + 1]).then_inc(decay_ready, 1)

            tile_read(act, "lru", 2 * RT - 1)
            stage_behind("k", heads)
            stage_behind("q", lambda i: heads(4 + i))
            act.wait_ge(head_sumsq_done, 12)
            head_sumsq = acc[0][:, 0:48].rearrange("p (t e j) -> p t e j", t=TT, j=2)
            fn(head_std[:, :, 0:4, :], head_sumsq[:, :, 0:4, :], ACT.Sqrt, bias=eps_col,
               scale=1.0 / HD).then_inc(head_std_ready, 1)
            fn(head_std[:, :, 4:12, :], head_sumsq[:, :, 4:12, :], ACT.Sqrt, bias=eps64_col).then_inc(head_std_ready, 1)
            act.wait_ge(var_ready, RT)
            fn(conv[:, :, :], conv[:, :, :], ACT.Sqrt).then_inc(scale_ready, 1)
            for m in range(RT):
                act.wait_ge(gated_ready, m + 1)
                fn(r_high[:, m, :], i_gate[:, m, :], ACT.Copy).then_inc(r_high_ready, 1)
            stage("yr", lambda i: None)
            for p in range(4):
                read_acc(p, pieces(y_rnn, p).rearrange("p k t -> p (k t)"))
            act.wait_ge(cmp_shifted, 1)
            fn(cmp_p[:, :, :, 0:NC], cmp_s, ACT.Exp).then_inc(cmp_probs, 1)
            for i in range(3):
                split_high(BASE["mg"] + i + RING)
            act.wait_ge(cmp_turned, 1)
            fn(cmp_pt[:, 0:4, :], bank[1][:, :], ACT.Copy).then_inc(cmp_copied, 1)
            split_high(BASE["mg"] + 3 + RING)

            def merge_gate(h, n):
                if h % 2 == 0 and 0 < h <= 2 * MG_PER_BRANCH:
                    split_high(BASE["mg"] + MG_EARLY + MG_PER_BRANCH * n + h // 2 - 1 + RING)

            for n in range(2):
                attention(n, probs0, lambda h: merge_gate(h, n))
            output_high(0)
            act.wait_ge(mg_scaled, 16)
            for i in range(4):
                fn(merge[:, 4 * i:4 * i + 4, :], merge[:, 4 * i:4 * i + 4, :], ACT.Sigmoid).then_inc(merge_gated, 1)

            def merged(i):
                act.wait_ge(z_ready, i + 1)
                fn(h_high[:, i, :], y_rnn[:, i, :], ACT.Copy).then_inc(h_high_ready, 1)

            stage("ao", merged)
            stage("wo", lambda i: None, DT - LATE)
            norm(1)
            late_splits(BASE["ffn0"], LATE)
            feed_forward(0)

            norm(2)
            late_splits(BASE["q1"], 1)
            roots(2)

            def rope_operand(e):
                if e >= 2:
                    act.wait_ge(rope_done, e - 1)
                freed(fn(rope_in[:, e % 2, :], tile("q1", e), ACT.Copy, scale=HD ** -0.5 if e < 8 else 1.0))

            stage("q1", rope_operand)
            stage("k1", lambda i: rope_operand(8 + i))
            stage("v1", lambda i: None)
            for p in range(4):
                read_acc(p, v1[:, p // 2, (p % 2) * 512:(p % 2 + 1) * 512], scale=rstd_col[:, p // 2:p // 2 + 1])
            attention(2, probs1)
            output_high(1)
            stage("wo1", lambda i: None, DT - LATE)
            norm(3)
            late_splits(BASE["ffn1"], LATE)
            feed_forward(1)

            norm(4)
            late_splits(BASE["c2"], 1)
            roots(4)

            def latents(e):
                tile_read(act, "c2", e)
                if e < 5:
                    ins = fn(c_sq[:, e, :], c_raw[:, e, :], ACT.Square)
                    if e == 4:
                        ins.then_inc(c_sq_ready, 1)

            stage_behind("c2", latents)
            act.wait_ge(c_sumsq, 1)
            for which, n in enumerate((QL, KVL)):
                ins = fn(c_std[:, 2 * which:2 * which + 2], acc[0][:, 2 * which:2 * which + 2], ACT.Sqrt,
                         bias=eps_col, scale=1.0 / n)
            ins.then_inc(c_std_ready, 1)
            for e in range(5):
                act.wait_ge(c_normed, e + 1)
                fn(h_high[:, e, :], c_norm[:, e, :], ACT.Copy).then_inc(h_high_ready, 1)
            at = 0
            for q in range(SIZE["uq"]):
                act.wait_ge(chunk_used, BASE["uq"] + q + 1)
                while at < NH and (3 * at + 2) // 8 <= q:
                    freed(fn(q2[:, at, :], tile("uq", at), ACT.Copy, scale=(HD + ROPE) ** -0.5))
                    at += 1
                split_high(BASE["uq"] + q + RING)
            for q in range(SIZE["uk"]):
                act.wait_ge(chunk_used, BASE["uk"] + q + 1)
                for m in range(4 * q, 4 * q + 4):
                    for j in range(2):
                        ins = fn(k2[0:HD, 2 * m + j, :], tile("uk", m)[HD * j:HD * (j + 1), :], ACT.Copy)
                    freed(ins)
                split_high(BASE["uk"] + q + RING)
            act.wait_ge(rope_done, 17)
            fn(k2[HD:HD + ROPE, :, :], c_raw[HD:HD + ROPE, 5:6, :].to_broadcast([ROPE, NH, S]),
               ACT.Copy).then_inc(k2_ready, 1)
            stage("uv", lambda i: None)
            for p in range(4):
                read_acc(p, v2[:, p // 2, (p % 2) * 512:(p % 2 + 1) * 512])
            attention(3, probs2)
            output_high(2)
            stage("wo2", lambda i: None, DT - LATE)
            norm(5)
            late_splits(BASE["ffn2"], LATE)
            feed_forward(2)
            norm(6)
            roots(6)

        @block.vector
        def _(dve):
            v = nc.vector
            steps = [0]

            def mark(ins):
                ins.then_inc(dve_step, 1)
                steps[0] += 1
                return steps[0]

            def link(ins):
                dve.wait_ge(dve_step, mark(ins))

            def split_low(c, i=None):
                if c >= N_CHUNKS:
                    return
                dve.wait_ge(high_ready, (0 if i is None else BODY * i) + c + 1)
                v.tensor_tensor(w_low[:, c % RING, :], w_raw[:, c % RAW, :], f(w_high[:, c % RING, :]),
                                ALU.subtract).then_inc(low_ready, 1)

            def stage(name, post, wait=True, count=None, then=None):
                for i in range(count or SIZE[name]):
                    c = BASE[name] + i
                    if wait:
                        dve.wait_ge(chunk_used, c + 1)
                    post(i)
                    split_low(c + RING)
                    if then:
                        then(i)

            def late_splits(end, count):
                for c in range(end - count, end):
                    split_low(c + RING)

            def tile(name, i):
                return bank[(TILE0[name] + i) % TILE_BANKS][:, 0:S]

            def low(dst, src, high, ready, n, done):
                dve.wait_ge(ready, n)
                v.tensor_tensor(dst, src, f(high), ALU.subtract).then_inc(done, 1)

            def norm(n):
                for p in range(5):
                    if p < 4 and n:
                        acc_bank_done(dve, n, p)
                        v.tensor_tensor(pieces(x, p), acc[p][:, :].rearrange("p (k t) -> p k t", k=2), pieces(x, p),
                                        ALU.add).then_inc(acc_read, 1)
                    if p and n < 6:
                        dve.wait_ge(h_high_ready, H_N[n] + p)
                        for k in (2 * p - 2, 2 * p - 1):
                            ins = v.scalar_tensor_tensor(h_low[:, k, :], x[:, k, :], par("norm", n * DT + k, 1),
                                                         f(h_high[:, k, :]), ALU.mult, ALU.subtract)
                        ins.then_inc(h_low_ready, 1)
                for p, count in ((0, 2), (2, 4)):
                    dve.wait_ge(x_squared, 4 * n + count)
                    ins = v.tensor_tensor(pieces(squares, p), pieces(squares, p), pieces(squares, p + 1), ALU.add)
                    link(ins)
                v.tensor_tensor(pieces(squares, 0), pieces(squares, 0), pieces(squares, 2),
                                ALU.add).then_inc(squares_ready, 1)

            def inverse_roots(n):
                dve.wait_ge(std_ready, n + 1)
                if n in (0, 2):
                    v.reciprocal(rstd_col, std_col)
                v.reciprocal(rstd[:, :], rstd[:, :]).then_inc(rstd_ready, 1)
                dve.wait_ge(rstd_ready, n + 1)

            def scaled(dst, name, i):
                dve.wait_ge(chunk_used, BASE[name] + i + 1)
                v.tensor_tensor(dst, tile(name, i), rstd[:, :], ALU.mult).then_inc(tile_free["dve"], 1)

            def attention(n, o, probs_t, branch=None, before=None, after=None):
                def row_max(h):
                    dve.wait_ge(scores_ready, NH * n + h + 1)
                    b = bank[h % 3]
                    v.tensor_reduce(neg_max[:, h, 0:1], b[:, 0:P], AX.X, ALU.max, negate=True)
                    v.tensor_reduce(neg_max[:, h, 1:2], b[:, P:3 * P], AX.X, ALU.max, negate=True).then_inc(max_ready, 1)

                def copy_turned(h):
                    dve.wait_ge(probs_turned, NH * n + h + 1)
                    if h >= 2:
                        dve.wait_ge(pv_done, NH * n + h - 1)
                    v.tensor_copy(probs_t[:, h % 2, :], bank[3 + h % 2][:, 0:3 * P]).then_inc(probs_copied, 1)

                def output(g):
                    dve.wait_ge(pv_done, NH * n + 4 * g + 4)
                    w = weights_o[:, :, 4 * g:4 * g + 4]
                    link(v.reciprocal(w, sums[:, :, 4 * g:4 * g + 4]))
                    if branch is not None:
                        link(v.tensor_tensor(w, w, nsa_gate[:, :, 4 * g:4 * g + 4, branch], ALU.mult))
                    dst = o[:, :, 4 * g:4 * g + 4, :]
                    src = bank[5 + g % 2][:, :].rearrange("p (t h d) -> p t h d", t=TT, h=4)
                    wide = w.unsqueeze(3).to_broadcast([P, TT, 4, HD])
                    if branch is None:
                        v.tensor_tensor(dst, src, wide, ALU.mult).then_inc(o_read, 1)
                    else:
                        link(v.tensor_tensor(o_part, src, wide, ALU.mult))
                        v.tensor_tensor(dst, dst, o_part, ALU.add).then_inc(o_read, 1)

                for h in range(NH + 3):
                    if before and h <= NH:
                        before(h)
                    if h < NH:
                        row_max(h)
                    if 2 <= h < NH + 2:
                        copy_turned(h - 2)
                    if after and h <= NH:
                        after(h)
                    if h >= 3 and h % 4 == 2:
                        output((h - 3) // 4)

            def output_low(n):
                for m in range(DT):
                    low(r_low[:, m, :], bank[m][:, 0:S], r_high[:, m, :], r_high_ready, R_O[n] + m + 1, r_low_ready)

            def feed_forward(n):
                base, s0, blocks, both = BASE[f"ffn{n}"], FFN_STEP0[n], FFN_BLOCKS[n], n == 0

                def tap(row, j):
                    at = AT[f"fcw{n}"][0] + row * blocks
                    return small[:, at + j:at + j + 1] if isinstance(j, int) else small[:, bass.ds(j + at, 1)]

                def back(dst, src, tokens, row, j):
                    return v.scalar_tensor_tensor(dst[:, tokens:S], src[:, 0:S - tokens], tap(row, j), dst[:, tokens:S],
                                                  ALU.mult, ALU.add)

                def hidden_low(j, k):
                    low(r_low[:, j % 2, :], hidden[:, j % 2, :], r_high[:, j % 2, :], hid_high,
                        k + (s0 + j + 1), hid_low)

                def step(j, c, i=None):
                    turn, k = (0, 0) if i is None else (BODY * i, 2 * i)
                    count, slot, end = k + (s0 + j + 1), j % 2, j == blocks - 1
                    dve.wait_ge(chunk_used, turn + c + 1)
                    if i is None and j == 0:
                        inverse_roots(2 * n + 1)
                    v.tensor_tensor(scaled_g[:, slot, :], bank[slot][:, 0:S], rstd[:, :], ALU.mult).then_inc(g_scaled, 1)
                    if j:
                        hidden_low(j - 1, k)
                    split_low(c + RING, i)
                    dve.wait_ge(tap_g, count)
                    back(taps_g[:, slot, :], scaled_g[:, slot, :], 1, 1, k + j).then_inc(tap_g2, 1)
                    dve.wait_ge(chunk_used, turn + c + 2)
                    v.tensor_tensor(scaled_v[:, slot, :], bank[2 + slot][:, 0:S], rstd[:, :],
                                    ALU.mult).then_inc(v_scaled, 1)
                    dve.wait_ge(tap_g2, count)
                    back(taps_g[:, slot, :], scaled_g[:, slot, :], 2, 0, k + j).then_inc(conv_g, 1)
                    if not end:
                        split_low(c + 1 + RING, i)
                    if both:
                        dve.wait_ge(tap_v, count)
                        back(taps_v[:, slot, :], scaled_v[:, slot, :], 1, 4, k + j).then_inc(tap_v2, 1)
                        dve.wait_ge(tap_v2, count)
                        back(taps_v[:, slot, :], scaled_v[:, slot, :], 2, 3, k + j).then_inc(conv_v, 1)
                        dve.wait_ge(conv_v, count)
                    else:
                        dve.wait_ge(v_scaled, count)
                    value = (taps_v if both else scaled_v)[:, slot, :]
                    dve.wait_ge(gelu_ready, count)
                    v.tensor_tensor(hidden[:, slot, :], gelu_g[:, slot, :], value, ALU.mult).then_inc(hidden_ready, 1)
                    if end:
                        hidden_low(j, k)
                        split_low(c + 1 + RING, i)
                    if j:
                        split_low(c + 2 + RING, i)

                step(0, base)
                turns = (blocks - 2) // 2 - (n == 2)
                with dve.Fori(0, turns) as i:
                    for q in range(2):
                        step(1 + q, base + 2 + 3 * q, i)
                for j in range(1 + 2 * turns, blocks):
                    step(j, base + 3 * j - 1)

            dve.wait_ge(norm_loaded, 16)
            dve.wait_ge(x_loaded, 16)
            split_low(0)
            norm(0)
            for c in range(1, RING // 2):
                split_low(c)
            inverse_roots(0)
            for c in range(RING // 2, RING):
                split_low(c)
            dve.wait_ge(small_loaded, 16)
            z, s, s2, t = lru_t[1], lru_t[0], lru_t[2], lru_t[3]
            dve.wait_ge(act_step, 2)
            link(v.tensor_scalar(s2, z, 2.0, None, ALU.add))
            link(v.reciprocal(s, s2))
            link(v.tensor_tensor(s, s, z, ALU.mult))
            link(v.tensor_tensor(s2, s, s, ALU.mult))
            link(v.tensor_scalar(t, s2, 1.0 / 17, None, ALU.mult))
            for n in range(7, 0, -1):
                link(v.scalar_tensor_tensor(t, t, 1.0 / (2 * n + 1), s2, ALU.add, ALU.mult))
            link(v.scalar_tensor_tensor(t, t, 1.0, s, ALU.add, ALU.mult))
            link(v.tensor_scalar(s, par("lam"), -1.0, 0.0, ALU.mult, ALU.max))
            link(v.scalar_tensor_tensor(t, t, 2.0, s, ALU.mult, ALU.add))
            v.tensor_scalar(lru_kn, t, LRU_C, None, ALU.mult)
            v.tensor_scalar(lru_k, t, -LRU_C, None, ALU.mult)
            v.memset(windows.rearrange("p (j n) -> p j n", n=WIN)[:, :, 60:HD], 0.0)
            stage("kvc", lambda i: scaled(kv_scaled[:, i, :], "kvc", i))

            def window(which):
                dve.wait_ge(kv2_ready, 2 * which + 2)
                dst = windows.rearrange("p (j n) -> p j n", n=WIN)[:, :, HD * which:HD * which + 60]
                dst = dst.rearrange("p j (c g) -> p g j c", g=NKV)
                pos = par(("pek", "pev")[which]).unsqueeze(2).to_broadcast([P, CL // 2, NC])
                for g in range(NKV):
                    pairs = kv2[:, 4 * which + g, :].rearrange("p (n j) -> p j n", j=2)[:, 0, :]
                    for half in range(2):
                        src = pairs[:, 8 * half:8 * half + 8 * NC].rearrange("p (c j) -> p j c", j=8)
                        at = slice(8 * half, 8 * half + 8)
                        ins = v.tensor_tensor(dst[:, g, at, :], src, pos[:, at, :], ALU.add)
                ins.then_inc(windows_ready, 1)

            def rgate(i):
                if i in (1, 2):
                    window(i - 1)
                if i == 6:
                    flat = [r[:, :, :].rearrange("p k t -> p (k t)")[:, 0:CL // 2 * WIN] for r in (r_low, r_high)]
                    low(flat[0], windows, flat[1], r_high_ready, 1, r_low_ready)

            stage("rgate", lambda i: scaled(gelu_gate[:, i, :], "rgate", i), then=rgate)

            stage("w1", lambda i: None)

            def conv_low(i):
                low(r_low[:, i, :], conv[:, i, :], r_high[:, i, :], r_high_ready, R_CONV + i + 1, r_low_ready)

            def conv_tap(i, back):
                if back > 1:
                    dve.wait_ge(dve_step, conv_taps[i, back - 1])
                ins = v.scalar_tensor_tensor(conv[:, i, back:S], rx_scaled[:, i % 3, 0:S - back],
                                             par("rcw", (3 - back) * RT + i, 1), conv[:, i, back:S], ALU.mult, ALU.add)
                if back < 3:
                    conv_taps[i, back] = mark(ins)
                else:
                    ins.then_inc(conv_ready, 1)

            conv_taps = {}

            def rx_scale(i):
                scaled(rx_scaled[:, i % 3, :], "rx", i)
                if i:
                    conv_tap(i - 1, 2)

            def rx(i):
                if i:
                    conv_tap(i - 1, 3)
                dve.wait_ge(tap_ready, i + 1)
                conv_tap(i, 1)
                if i >= 2:
                    conv_low(i - 2)
                if i == 2:
                    dve.wait_ge(cmp_hid_ready, 1)
                    dve.wait_ge(zeros_ready, 1)
                    for r in range(4):
                        ins = v.tensor_copy(cmp_hv[:, :, r, 0:NC],
                                            cmp_hid[:, 60:120].rearrange("p (c g) -> p g c", g=NKV))
                    ins.then_inc(cmp_hv_ready, 1)
                if i == 4:
                    dve.wait_ge(cmp_kv_ready, 1)
                    for r in range(4):
                        v.tensor_copy(cmp_v[32 * r:32 * r + 32, :, r * HD:(r + 1) * HD],
                                      acc[1][32 * r:32 * r + 32, 0:4 * HD].rearrange("p (g d) -> p g d", g=NKV))
                if i == 7:
                    dve.wait_ge(cmp_std_ready, 1)
                    v.reciprocal(cmp_rstd[0:60, :], cmp_std[0:60, :]).then_inc(cmp_rstd_ready, 1)
                if i == 10:
                    dve.wait_ge(cmp_spread, 1)
                    for j in range(2):
                        rows = slice(HD * j, HD * (j + 1))
                        ins = v.tensor_tensor(cmp_k[rows, j, :], cmp_kraw[rows, :], acc[3][rows, 0:60], ALU.mult)
                    ins.then_inc(head_normed, 1)

            stage("rx", rx_scale, then=rx)
            conv_tap(RT - 1, 2)
            conv_low(RT - 2)
            conv_tap(RT - 1, 3)
            conv_low(RT - 1)
            inputs_marked = [0]

            def lru_input(t, gate, m):
                if gate == 1:
                    tile_read(dve, "lru", t)
                    inputs_marked[0] = mark(v.tensor_tensor(i_gate[:, m, :], i_gate[:, m, :], conv[:, m, :], ALU.mult))

            lru_posts(dve, split_low, lru_input)
            stage("v", lambda i: None)
            stage("g", lambda i: None)
            squared = []

            def variance(m):
                dve.wait_ge(dve_step, squared[m])
                v.scalar_tensor_tensor(conv[:, m, :], conv[:, m, :], 1.0, r_gate[:, m, :], ALU.add,
                                       ALU.mult).then_inc(var_ready, 1)

            def lru_step(e):
                if e < RT:
                    dve.wait_ge(decay_ready, e + 1)
                    squared.append(mark(v.tensor_tensor(conv[:, e, :], decay[:, e, :], decay[:, e, :], ALU.mult)))
                if e >= 1:
                    variance(e - 1)

            def heads(e):
                if e >= 2:
                    dve.wait_ge(head_sumsq_done, e - 1)
                name, i = ("k", e) if e < 4 else ("q", e - 4)
                scaled(head_sq[:, e % 2, :], name, i)
                tile_read(dve, name, i)
                if e < 4:
                    if e == 0:
                        dve.wait_ge(zeros_ready, 1)
                    branch, g = e // 2, 2 * (e % 2)
                    for j in range(2):
                        rows = slice(HD * j, HD * (j + 1))
                        ins = v.tensor_scalar(k0[rows, branch, j, g + j, :], head_sq[rows, e % 2, :],
                                              par("hg", 2 + branch, 1)[rows, :], None, ALU.mult)
                else:
                    ins = v.tensor_scalar(q0[:, e - 4, :], head_sq[:, e % 2, :], par("hg", 0, 1), None, ALU.mult)
                ins.then_inc(heads_scaled, 1)

            stage("k", heads, then=lru_step)
            stage("q", lambda i: heads(4 + i), then=lambda i: lru_step(4 + i))
            dve.wait_ge(head_std_ready, 2)
            v.reciprocal(stats[:, 148:196], stats[:, 100:148]).then_inc(head_rstd_ready, 1)
            dve.wait_ge(scale_ready, 1)
            dve.wait_ge(dve_step, inputs_marked[0])
            driven, scanned = [], []
            for m in range(RT + 3):
                if m < RT:
                    driven.append(mark(v.tensor_tensor(conv[:, m, :], conv[:, m, :], i_gate[:, m, :], ALU.mult)))
                if 1 <= m <= RT:
                    dve.wait_ge(dve_step, driven[m - 1])
                    v.tensor_tensor_scan(r_gate[:, m - 1, :], decay[:, m - 1, :], conv[:, m - 1, :], 0.0, ALU.mult,
                                         ALU.add).then_inc(scan_ready, 1)
                if 2 <= m <= RT + 1:
                    dve.wait_ge(scan_ready, m - 1)
                    v.tensor_tensor(i_gate[:, m - 2, :], r_gate[:, m - 2, :], gelu_gate[:, m - 2, :],
                                    ALU.mult).then_inc(gated_ready, 1)
                if m >= 3:
                    low(r_low[:, m - 3, :], i_gate[:, m - 3, :], r_high[:, m - 3, :], r_high_ready,
                        R_SCAN + m - 2, r_low_ready)
            v.memset(cmp_p[:, :, :, :], 0.0)

            def normed_heads(e):
                dve.wait_ge(head_spread, e + 1)
                b = bank[e % TILE_BANKS][:, 0:S]
                if e >= 4:
                    ins = v.tensor_tensor(q0[:, e - 4, :], q0[:, e - 4, :], b, ALU.mult)
                else:
                    branch, g = e // 2, 2 * (e % 2)
                    for j in range(2):
                        own, other = slice(HD * j, HD * (j + 1)), slice(HD * (1 - j), HD * (2 - j))
                        v.tensor_tensor(k0[other, branch, 1 - j, g + j, :], k0[own, branch, j, g + j, :], b[own, :],
                                        ALU.mult)
                        ins = v.tensor_tensor(k0[own, branch, j, g + j, :], k0[own, branch, j, g + j, :], b[own, :],
                                              ALU.mult)
                ins.then_inc(head_normed, 1)

            stage("yr", normed_heads, wait=False)
            normed_heads(RT)
            dve.wait_ge(cmp_scores, 1)
            src = bank[0][:, :].rearrange("p (t h c) -> p t h c", t=TT, h=NH)
            masks = par("cmpmask").rearrange("p (t c) -> p t c", t=TT)
            for t in range(TT):
                ins = v.tensor_tensor(cmp_s[:, t, :, :], src[:, t, :, 0:NC],
                                      masks[:, t, :].unsqueeze(1).to_broadcast([P, NH, NC]), ALU.add)
            link(ins)
            link(v.tensor_reduce(cmp_max, cmp_s, AX.X, ALU.max))
            for t in range(TT):
                ins = v.tensor_tensor(cmp_s[:, t, :, :], cmp_s[:, t, :, :],
                                      cmp_max[:, t, :].unsqueeze(2).to_broadcast([P, NH, NC]), ALU.subtract)
            ins.then_inc(cmp_shifted, 1)

            def merge_scaled(i):
                dve.wait_ge(chunk_used, BASE["mg"] + i + 1)
                v.tensor_tensor(merge[:, i, :], mg_bank(i), rstd[:, :], ALU.mult).then_inc(mg_scaled, 1)

            for i in range(3):
                merge_scaled(i)
                split_low(BASE["mg"] + i + RING)
            dve.wait_ge(cmp_probs, 1)
            link(v.tensor_reduce(cmp_sum, cmp_p[:, :, :, 0:NC], AX.X, ALU.add))
            dve.wait_ge(cmp_turned, 1)
            v.tensor_copy(cmp_pt[:, 4:8, :], bank[2][:, :].rearrange("p (a b) -> p a b", a=4)).then_inc(cmp_copied, 1)
            link(v.reciprocal(cmp_max, cmp_sum))
            for t in range(TT):
                ins = v.scalar_tensor_tensor(weights_o[:, t, :], cmp_max[:, t, :], par("rowok", t, 1),
                                             nsa_gate[:, t, :, 0], ALU.mult, ALU.mult)
            link(ins)
            merge_scaled(3)
            split_low(BASE["mg"] + 3 + RING)
            for t in range(TT):
                dve.wait_ge(cmp_pv, t + 1)
                for half in range(2):
                    v.tensor_tensor(o0[:, t, 8 * half:8 * half + 8, :],
                                    bank[3 + 2 * t + half][:, :].rearrange("p (h d) -> p h d", h=8),
                                    weights_o[:, t, 8 * half:8 * half + 8].unsqueeze(2).to_broadcast([P, 8, HD]),
                                    ALU.mult).then_inc(cmp_done, 1)
            dve.wait_ge(cmp_done, 4)

            def merge_gate(h, n):
                if h % 2 == 0 and 0 < h <= 2 * MG_PER_BRANCH:
                    merge_scaled(MG_EARLY + MG_PER_BRANCH * n + h // 2 - 1)

            def merge_split(h, n):
                if h % 2 == 0 and 0 < h <= 2 * MG_PER_BRANCH:
                    split_low(BASE["mg"] + MG_EARLY + MG_PER_BRANCH * n + h // 2 - 1 + RING)

            for n in range(2):
                if n:
                    dve.wait_ge(o_read, 4)
                attention(n, o0, probs_t0, branch=1 + n, before=lambda h: merge_gate(h, n),
                          after=lambda h: merge_split(h, n))
            output_low(0)

            def merge_low(i):
                low(h_low[:, i, :], y_rnn[:, i, :], h_high[:, i, :], h_high_ready, H_Z + i + 1, h_low_ready)

            def merged(i):
                dve.wait_ge(merge_gated, 3 + i // 4)
                v.tensor_tensor(merge[:, 8 + i, :], merge[:, 8 + i, :], tile("ao", i), ALU.mult).then_inc(tile_free["dve"], 1)
                link(v.tensor_tensor(merge[:, i, :], merge[:, i, :], y_rnn[:, i, :], ALU.mult))
                v.tensor_tensor(y_rnn[:, i, :], merge[:, i, :], merge[:, 8 + i, :], ALU.add).then_inc(z_ready, 1)
                if i:
                    merge_low(i - 1)

            stage("ao", merged)
            merge_low(DT - 1)
            stage("wo", lambda i: None, count=DT - LATE)
            norm(1)
            late_splits(BASE["ffn0"], LATE)
            feed_forward(0)

            norm(2)
            late_splits(BASE["q1"], 1)
            inverse_roots(2)
            v.tensor_tensor(c64r, par("c64"), rstd[:, :], ALU.mult)
            link(v.tensor_tensor(s64r, par("s64"), rstd[:, :], ALU.mult))

            def rope(e):
                name, i = ("q1", e) if e < 8 else ("k1", e - 8)
                tile_read(dve, name, i)
                a, b = rope_a[:, e % 2, :], rope_b[:, e % 2, :]
                v.tensor_tensor(a, rope_in[:, e % 2, :], c64r, ALU.mult)
                dve.wait_ge(rope_turned, e + 1)
                link(v.tensor_tensor(b, acc[e % 2][:, 0:S], s64r, ALU.mult))
                if e < 8:
                    ins = v.tensor_tensor(q1[:, i, :], a, b, ALU.add)
                else:
                    for j in range(2):
                        rows = slice(HD * j, HD * (j + 1))
                        ins = v.tensor_tensor(k1[rows, j, i, :], a[rows, :], b[rows, :], ALU.add)
                ins.then_inc(rope_done, 1)

            stage("q1", lambda i: rope(i - 1) if i else None)
            stage("k1", lambda i: rope(i + 7))
            rope(15)
            stage("v1", lambda i: None)
            attention(2, o1, probs_t1)
            output_low(1)
            stage("wo1", lambda i: None, count=DT - LATE)
            norm(3)
            late_splits(BASE["ffn1"], LATE)
            feed_forward(1)

            norm(4)
            late_splits(BASE["c2"], 1)
            inverse_roots(4)
            stage("c2", lambda i: scaled(c_raw[:, i, :], "c2", i))
            dve.wait_ge(c_std_ready, 1)
            v.reciprocal(c_rstd, c_std).then_inc(c_rstd_ready, 1)
            dve.wait_ge(c_spread, 1)
            for e in range(6):
                if e < 5:
                    v.scalar_tensor_tensor(c_norm[:, e, :], c_raw[:, e, :], par("ln2", e, 1),
                                           acc[1 if e < 3 else 2][:, 0:S], ALU.mult, ALU.mult).then_inc(c_normed, 1)
                if e:
                    low(h_low[:, e - 1, :], c_norm[:, e - 1, :], h_high[:, e - 1, :], h_high_ready, H_C + e, h_low_ready)
            rows, other = slice(HD, HD + ROPE), slice(HD + ROPE, P)
            tile_read(dve, "c2", 5)
            v.tensor_tensor(rope_a2[rows, 0, 0:S], c_raw[rows, 5, :], par("c32")[rows, :], ALU.mult)
            link(v.tensor_tensor(rope_b2[rows, 0, 0:S], c_raw[other, 5, :], par("s32")[other, :], ALU.mult))
            v.tensor_tensor(c_raw[rows, 5, :], rope_a2[rows, 0, 0:S], rope_b2[rows, 0, 0:S], ALU.add).then_inc(rope_done, 1)

            def query_rope(e):
                a = rope_a2[rows, e % 2, :].rearrange("p (h t) -> p h t", h=2)
                b = rope_b2[rows, e % 2, :].rearrange("p (h t) -> p h t", h=2)
                tile_read(dve, "uq", 2 * e + 1)
                if e != 1:
                    dve.wait_ge(rope_done, 17 if e == 0 else 16 + e)
                v.tensor_tensor(a, q2[rows, 2 * e:2 * e + 2, :],
                                par("c32")[rows, :].unsqueeze(1).to_broadcast([ROPE, 2, S]), ALU.mult)
                link(v.tensor_tensor(b, q2[other, 2 * e:2 * e + 2, :],
                                     par("s32")[other, :].unsqueeze(1).to_broadcast([ROPE, 2, S]), ALU.mult))
                v.tensor_tensor(q2[rows, 2 * e:2 * e + 2, :], a, b, ALU.add).then_inc(rope_done, 1)

            roped = 0
            for i in range(SIZE["uq"]):
                dve.wait_ge(chunk_used, BASE["uq"] + i + 1)
                split_low(BASE["uq"] + i + RING)
                while (3 * (2 * roped + 1) + 2) // 8 <= i and roped < 8:
                    query_rope(roped)
                    roped += 1
            stage("uk", lambda i: None)
            stage("uv", lambda i: None)
            attention(3, o2, probs_t2)
            output_low(2)
            stage("wo2", lambda i: None, count=DT - LATE)
            norm(5)
            late_splits(BASE["ffn2"], LATE)
            feed_forward(2)
            norm(6)
            inverse_roots(6)
            for k in range(DT):
                ins = v.scalar_tensor_tensor(x_norm[:, k, :], x[:, k, :], par("norm", 6 * DT + k, 1), rstd[:, :],
                                             ALU.mult, ALU.mult)
                if k % 2:
                    ins.then_inc(norm_ready, 1)


def column_chunks(w, width=P):
    k, n = w.shape
    padded = np.zeros((k, -(-n // width) * width), w.dtype)
    padded[:, :n] = w
    return padded.reshape(k // P, P, -1, width).transpose(2, 1, 0, 3).reshape(-1, P, k // P * width)


def row_chunks(w):
    n, m = w.shape
    padded = np.zeros((-(-n // P) * P, m), w.dtype)
    padded[:n] = w
    return padded.reshape(-1, P, m)


def block_chunks(blocks):
    out = np.zeros((-(-len(blocks) // 8), P, 8, P), blocks[0].dtype)
    for n, b in enumerate(blocks):
        out[n // 8, :b.shape[0], n % 8, :b.shape[1]] = b
    return out.reshape(-1, P, D)


def ffn_chunks(gate, up, down):
    g, u, d = column_chunks(gate), column_chunks(up), row_chunks(down)
    order = [g[0], u[0]]
    for j in range(1, len(g)):
        order += [g[j], u[j], d[j - 1]]
    return np.stack(order + [d[-1]])


def lay_out_weights(a):
    w_in = a["w_in"]
    sizes = [D_RNN, D_RNN, NH * HD] + [KVW] * 6 + [3 * NH, D, D]
    cut = np.concatenate([[0], np.cumsum(sizes)])
    rx, rg, q, kc, vc, ks, vs, kw, vw, g, mr, ma = (w_in[:, cut[i]:cut[i + 1]] for i in range(12))
    full = []
    for w in (a["rg_w_a"], a["rg_w_x"]):
        band = np.zeros((RT * P, RT * P), w.dtype)
        for n in range(RNN_BLOCKS):
            band[n * BW:(n + 1) * BW, n * BW:(n + 1) * BW] = w[n]
        full.append(band)
    gates = [full[gate][k * P:(k + 1) * P, m * P:(m + 1) * P] for gate, m, k in GATES]
    qkv = a["a_w_qkv_2"][0]
    c2 = a["b_w_in_2"][0]
    uq = a["b_w_uq_2"][0].reshape(QL, NH, HD + ROPE)
    ukv = a["b_w_ukv_2"][0].reshape(KVL, NH, 2, HD)
    uk = ukv[:, :, 0, :].reshape(KVL, D)
    uv = ukv[:, :, 1, :].reshape(KVL, D)
    d0 = FF0
    swap = np.roll(np.arange(ROPE), ROPE // 2)
    parts = {
        "kvc": column_chunks(np.concatenate([kc, vc], 1)), "rgate": column_chunks(rg),
        "w1": np.stack([a[n].reshape(4, 4, P, P).transpose(0, 2, 1, 3) for n in ("cmp_w1_k", "cmp_w1_v")],
                       3).reshape(4, P, D),
        "rx": column_chunks(rx), "lru": block_chunks(gates),
        "v": np.concatenate([vs, vw], 1).reshape(4, 2, P, 512).transpose(0, 2, 1, 3).reshape(4, P, D),
        "g": column_chunks(g), "k": column_chunks(np.concatenate([ks, kw], 1)), "q": column_chunks(q),
        "yr": row_chunks(a["w_rnn_out"]), "mg": column_chunks(np.concatenate([mr, ma], 1)),
        "ao": column_chunks(a["w_attn_out"]), "wo": row_chunks(a["w_out"]),
        "ffn0": ffn_chunks(a["w_up"][:, :d0], a["w_up"][:, d0:], a["w_down"]),
        "q1": column_chunks(qkv[:, :D]), "k1": column_chunks(qkv[:, D:2 * D]), "v1": row_chunks(qkv[:, 2 * D:]),
        "wo1": row_chunks(a["a_w_o_2"][0]),
        "ffn1": ffn_chunks(a["ffn_w_gate_2"][0], a["ffn_w_up_2"][0], a["ffn_w_down_2"][0]),
        "c2": np.concatenate([column_chunks(c2[:, :QL + KVL]),
                              column_chunks(np.concatenate([c2[:, QL + KVL - HD:], c2[:, QL + KVL:][:, swap]], 1))]),
        "uq": block_chunks([np.concatenate([uq[k * P:(k + 1) * P, h], uq[k * P:(k + 1) * P, h, HD:][:, swap]], 1)
                            for h in range(NH) for k in range(3)]),
        "uk": block_chunks([uk[k * P:(k + 1) * P, m * P:(m + 1) * P] for m in range(8) for k in range(2)]),
        "uv": row_chunks(uv), "wo2": row_chunks(a["b_w_o_2"][0]),
        "ffn2": ffn_chunks(a["ffn_w_gate_2"][1], a["ffn_w_up_2"][1], a["ffn_w_down_2"][1]),
    }
    for name, n in STAGES:
        assert parts[name].shape == (n, P, D), (name, parts[name].shape)
    return np.concatenate([parts[name] for name, _ in STAGES])


def feature_tiles(v):
    padded = np.zeros(-(-v.shape[0] // P) * P, v.dtype)
    padded[:v.shape[0]] = v
    return padded.reshape(-1, P).T


def lay_out_small(a):
    out = np.zeros((P, N_SMALL), np.float32)

    def put(name, value):
        at, n = AT[name]
        out[:, at:at + n] = np.asarray(value).reshape(P, n)

    token, row = np.arange(S), np.arange(P)
    put("ident", np.eye(P))
    put("mask", np.where(row[None, :] <= row[:, None], 0.0, NEG))
    end = np.arange(NC) * CS + CL - 1
    t = np.arange(TT)[None, :] * P + row[:, None]
    put("cmpmask", np.where(end <= t[:, :, None], 0.0, NEG))
    put("rowok", t >= CL - 1)
    put("blk2", row[:, None] // HD == np.arange(2))
    put("ones", np.ones((P, 2)))
    put("eps", np.tile([EPS, HD * EPS], (P, 1)))
    for name, dim in (("64", HD), ("32", ROPE)):
        inv = (np.float32(10000.0) ** (-np.arange(0, dim, 2, dtype=np.float32) / np.float32(dim))).astype(np.float32)
        angle = (token.astype(np.float32)[None, :] * inv[:, None]).astype(np.float32)
        table = np.tile(angle, (P // (dim // 2), 1))
        put("c" + name, np.cos(table))
        put("s" + name, np.sin(table))
    half = ROPE // 2
    sines = out[:, AT["s32"][0]:AT["s32"][0] + S]
    sines[HD + ROPE:HD + ROPE + half] *= -1.0
    rot = np.zeros((P, P))
    for at in range(0, P, HD):
        for j in range(HD // 2):
            rot[at + HD // 2 + j, at + j] = -1.0
            rot[at + j, at + HD // 2 + j] = 1.0
    put("rot64", rot)
    norms = [a["norm1_g"], a["norm2_g"], a["norm_mix_2"][0], a["norm_ffn_2"][0], a["norm_mix_2"][1],
             a["norm_ffn_2"][1], a["norm_final_2"]]
    put("norm", np.concatenate([feature_tiles(g) for g in norms], 1))
    put("rcw", np.concatenate([feature_tiles(w) for w in a["rnn_conv_w"]], 1))
    for name, key in (("rcb", "rnn_conv_b"), ("rba", "rg_b_a"), ("rbx", "rg_b_x"), ("lam", "lru_lambda")):
        put(name, feature_tiles(a[key]))
    put("hg", np.stack([np.tile(a[n], 2) for n in ("q_norm_g", "k_cmp_norm_g", "k_slc_norm_g", "k_win_norm_g")], 1))
    for name, key in (("pek", "cmp_pe_k"), ("pev", "cmp_pe_v")):
        put(name, a[key].reshape(CL // 2, P).T)
    put("w2k", np.tile(a["cmp_w2_k"], (1, 2)))
    put("w2v", a["cmp_w2_v"])
    put("fcw0", np.concatenate([feature_tiles(w) for half in (slice(0, FF0), slice(FF0, None))
                                for w in a["ffn_conv_w"][:, half]], 1))
    put("fcb0", np.concatenate([feature_tiles(a["ffn_conv_b"][half]) for half in (slice(0, FF0), slice(FF0, None))], 1))
    for n in (1, 2):
        put(f"fcw{n}", np.concatenate([feature_tiles(w) for w in a["ffn_conv_w_2"][n - 1]], 1))
        put(f"fcb{n}", feature_tiles(a["ffn_conv_b_2"][n - 1]))
    put("ln2", np.concatenate([feature_tiles(a["b_q_norm_2"][0]), feature_tiles(a["b_kv_norm_2"][0])], 1))
    return out


def kernel(**inputs):
    import concourse.bacc as bacc
    from concourse.bass_utils import run_bass_kernel_spmd

    a = {name: np.asarray(value) for name, value in inputs.items()}
    arrays = {
        "weight_stream": lay_out_weights(a),
        "small_in": lay_out_small(a),
        "x_in": np.ascontiguousarray(a["x"][0].T.reshape(DT, P, S).transpose(1, 0, 2)),
    }
    nc = bacc.Bacc("TRN2", target_bir_lowering=False, num_devices=1)
    args = [nc.dram_tensor(n, v.shape, mybir.dt.from_np(v.dtype), kind="ExternalInput").ap() for n, v in arrays.items()]
    out = nc.dram_tensor("out", (P, DT, S), F32, kind="ExternalOutput").ap()
    build(nc, *args, out)
    r = run_bass_kernel_spmd(nc, [arrays], core_ids=[0])
    y = r.results[0]["out"]
    return np.ascontiguousarray(y.transpose(2, 1, 0).reshape(1, S, D))
```

```python
from contextlib import ExitStack

import numpy as np

import concourse.bass as bass
from concourse import mybir

F32 = mybir.dt.float32
F32R = mybir.dt.float32r
BF16 = mybir.dt.bfloat16
ALU = mybir.AluOpType
ACT = mybir.ActivationFunctionType
AX = mybir.AxisListType

P = 128
S = 256
TT = S // P
D = 1024
DT = D // P
D_RNN, RNN_BLOCKS = 1344, 16
BW = D_RNN // RNN_BLOCKS
RT = -(-D_RNN // P)
LRU_C = 8.0
NH, NKV, HD = 16, 4, 64
KVW = NKV * HD
CL, CS = 32, 16
NC = (S - CL) // CS + 1
FF0, FF2 = 3072, 2816
QL, KVL, ROPE = 384, 256, 32
EPS = 1e-6
NEG = -1e30

RAW = 3
LATE = 3
RING = 6
WIN = 124
BODY = 6


def gate_blocks():
    out = []
    for m in range(RT):
        lo = BW * (P * m // BW)
        hi = BW * (min(P * m + P - 1, D_RNN - 1) // BW + 1) - 1
        for gate in range(2):
            out += [(gate, m, k) for k in range(lo // P, hi // P + 1)]
    return out


GATES = gate_blocks()
FFN_BLOCKS = {0: FF0 // P, 1: FF2 // P, 2: FF2 // P}

STAGES = [("kvc", 4), ("rgate", RT), ("w1", 4), ("rx", RT), ("lru", -(-len(GATES) // 8)), ("k", 4), ("q", 8),
          ("v", 4), ("g", 1), ("yr", RT), ("mg", 16), ("ao", 8), ("wo", 8),
          ("ffn0", 3 * FFN_BLOCKS[0]),
          ("v1", 8), ("q1", 8), ("k1", 8), ("wo1", 8), ("ffn1", 3 * FFN_BLOCKS[1]),
          ("c2", 6), ("uv", 2), ("uq", 6), ("uk", 2), ("wo2", 8), ("ffn2", 3 * FFN_BLOCKS[2])]
BASE, N_CHUNKS = {}, 0
for _name, _n in STAGES:
    BASE[_name] = N_CHUNKS
    N_CHUNKS += _n
SIZE = dict(STAGES)



SMALL = [("norm", 7 * DT), ("ones", 2), ("eps", 2), ("ident", 128), ("mask", 128), ("cmpmask", TT * NC), ("rowok", TT), ("blk2", 2),
         ("c64", S), ("s64", S), ("rot64", P), ("c32", S), ("s32", S),
         ("rcw", 4 * RT), ("rcb", RT), ("rba", RT), ("rbx", RT), ("lam", RT),
         ("hg", 4), ("pek", CL // 2), ("pev", CL // 2), ("w2k", P), ("w2v", HD),
         ("fcw0", 6 * FFN_BLOCKS[0]), ("fcb0", 2 * FFN_BLOCKS[0]), ("fcw1", 3 * FFN_BLOCKS[1]),
         ("fcb1", FFN_BLOCKS[1]), ("fcw2", 3 * FFN_BLOCKS[2]), ("fcb2", FFN_BLOCKS[2]),
         ("ln2", 5)]
AT, N_SMALL = {}, 0
for _name, _n in SMALL:
    AT[_name] = (N_SMALL, _n)
    N_SMALL += _n

N_FIRST = AT["ident"][0]

TILE_STAGES = [("kvc", 4, "dve"), ("rgate", RT, "dve"), ("rx", RT, "dve"), ("lru", 2 * RT, "act"),
               ("k", 4, "dve"), ("q", 8, "dve"), ("ao", 8, "dve"),
               ("q1", 8, "act"), ("k1", 8, "act"), ("c2", 6, "dve"), ("uq", NH, "act"), ("uk", 8, "act")]
TILE0, TILE_OWNER = {}, []
for _name, _n, _who in TILE_STAGES:
    TILE0[_name] = len(TILE_OWNER)
    for _ in range(_n):
        TILE_OWNER.append((_who, sum(w == _who for w, _ in TILE_OWNER) + 1))
TILE_BANKS = 4


def lru_groups():
    out = []
    for n, (gate, m, k) in enumerate(GATES):
        if not out or out[-1][:2] != (gate, m):
            out.append((gate, m, []))
        out[-1][2].append((n, k))
    return out


LRU_GROUPS = lru_groups()


def build(nc, weight_stream, small_in, x_in, out):
    with ExitStack() as ctx:
        def sb(name, shape, dt=F32):
            return ctx.enter_context(nc.sbuf_tensor(name, shape, dt))

        def sem(name):
            return ctx.enter_context(nc.semaphore(name))

        w_raw = sb("w_raw", [P, RAW, D])
        w_high = sb("w_high", [P, RING, D], F32R)
        w_low = sb("w_low", [P, RING, D], F32R)
        small = sb("small", [P, N_SMALL])
        x = sb("x", [P, DT, S])
        h_high = sb("h_high", [P, DT, S], F32R)
        h_low = sb("h_low", [P, DT, S], F32R)
        r_high = sb("r_high", [P, RT, S], F32R)
        r_low = sb("r_low", [P, RT, S], F32R)
        ident_b = sb("ident_b", [P, P], BF16)
        mask_b = sb("mask_b", [P, P], BF16)
        rstd = sb("rstd", [P, S])
        stats = sb("stats", [P, 464])
        arena = sb("arena", [P, 22904])
        bank = [ctx.enter_context(nc.psum_tensor(f"bank{i}", [P, 512], F32)) for i in range(8)]
        acc = bank[4:8]

        def par(name, a=0, n=None):
            at, size = AT[name]
            return small[:, at + a:at + (size if n is None else a + n)]

        def tiles(at, n, w=S):
            return arena[:, at:at + n * w].rearrange("p (k t) -> p k t", t=w)

        ident = par("ident")
        blk2 = par("blk2")
        ones = par("ones", 0, 1)
        eps_col = par("eps", 0, 1)
        eps64_col = par("eps", 1, 1)

        squares = tiles(0, DT)
        x_norm = tiles(4096, DT)
        gelu_gate = tiles(0, RT)
        conv = tiles(2816, RT)
        r_gate = tiles(5632, RT)
        i_gate = tiles(8448, RT)
        decay = tiles(11264, RT)
        kv2 = tiles(2816, 8)
        windows = arena[:, 5632:5632 + CL // 2 * WIN]
        kv_scaled = tiles(8448, 4)
        rx_scaled = tiles(8448, 3)
        cmp_ht = arena[:, 12032:12160]
        cmp_hid = arena[:, 11264:11324]
        cmp_kraw = arena[:, 11384:11444]
        cmp_ksq = arena[:, 11444:11504]
        cmp_hv = arena[:, 11520:12032].rearrange("p (g r c) -> p g r c", g=NKV, r=4)
        q0 = tiles(14080, DT)
        k0 = arena[:, 16128:20224].rearrange("p (b v g t) -> p b v g t", b=2, v=2, g=NKV)
        v0 = arena[:, 20224:21248].rearrange("p (b t c) -> p b t c", b=2, t=TT)
        cmp_v = arena[:, 21248:22272].rearrange("p (g c) -> p g c", g=NKV)
        cmp_k = arena[:, 22272:22392].rearrange("p (v n) -> p v n", v=2)
        head_sq = tiles(22392, 2)
        y_rnn = tiles(0, DT)
        o0 = arena[:, 2048:4096].rearrange("p (t h d) -> p t h d", t=TT, h=NH)
        merge = tiles(4096, 16)
        cmp_p = arena[:, 8192:9216].rearrange("p (t h c) -> p t h c", t=TT, h=NH)
        probs0 = tiles(9216, 3, 384)
        probs_t0 = tiles(10368, 2, 384)
        o_part = arena[:, 11136:11648].rearrange("p (t h d) -> p t h d", t=TT, h=4)
        cmp_s = arena[:, 11648:12128].rearrange("p (t h c) -> p t h c", t=TT, h=NH)
        cmp_pt = tiles(12288, 8, P)
        q1 = tiles(0, 8)
        k1 = arena[:, 2048:6144].rearrange("p (v k t) -> p v k t", v=2, k=8)
        v1 = arena[:, 6144:8192].rearrange("p (t c) -> p t c", t=TT)
        o1 = arena[:, 8192:10240].rearrange("p (t h d) -> p t h d", t=TT, h=NH)
        probs1 = tiles(10240, 3, 384)
        probs_t1 = tiles(11392, 2, 384)
        rope_in = tiles(12288, 2)
        rope_a = tiles(12800, 2)
        rope_b = tiles(13312, 2)
        q2 = tiles(0, NH)
        k2 = tiles(4096, NH)
        v2 = arena[:, 8192:10240].rearrange("p (t c) -> p t c", t=TT)
        o2 = arena[:, 10240:12288].rearrange("p (t h d) -> p t h d", t=TT, h=NH)
        probs2 = tiles(12288, 3, 384)
        probs_t2 = tiles(13440, 2, 384)
        c_raw = tiles(14336, 6)
        c_sq = tiles(15872, 5)
        c_norm = tiles(17152, 5)
        rope_a2 = tiles(18432, 2, 512)
        rope_b2 = tiles(19456, 2, 512)
        c64r = arena[:, 13824:14080]
        s64r = arena[:, 14080:14336]
        scaled_g = tiles(19456, 2)
        scaled_v = tiles(19968, 2)
        taps_g = tiles(20480, 2)
        taps_v = tiles(20992, 2)
        gelu_g = tiles(21504, 2)
        hidden = tiles(22016, 2)

        std_col = stats[:, 0:2]
        rstd_col = stats[:, 2:4]
        lru_k = stats[:, 16:16 + RT]
        lru_kn = stats[:, 32:32 + RT]
        lru_t = [stats[:, 48 + 12 * i:48 + 12 * i + RT] for i in range(4)]
        cmp_std = stats[:, 98:99]
        cmp_rstd = stats[:, 99:100]
        head_std = stats[:, 100:148].rearrange("p (t e j) -> p t e j", t=TT, j=2)
        head_rstd = stats[:, 148:196].rearrange("p (t e j) -> p t e j", t=TT, j=2)
        nsa_gate = stats[:, 200:296].rearrange("p (t h b) -> p t h b", t=TT, b=3)
        neg_max = stats[:, 296:328].rearrange("p (h t) -> p h t", t=TT)
        sums = stats[:, 328:360].rearrange("p (t h) -> p t h", t=TT)
        weights_o = stats[:, 360:392].rearrange("p (t h) -> p t h", t=TT)
        cmp_max = stats[:, 392:424].rearrange("p (t h) -> p t h", t=TT)
        cmp_sum = stats[:, 424:456].rearrange("p (t h) -> p t h", t=TT)
        c_std = stats[:, 456:460]
        c_rstd = stats[:, 460:464]

        chunk_loaded = [sem(f"chunk_loaded{i}") for i in range(RAW)]
        high_ready = sem("high_ready")
        low_ready = sem("low_ready")
        chunk_used = sem("chunk_used")
        norm_loaded = sem("norm_operands_loaded")
        small_loaded = sem("small_loaded")
        x_loaded = [sem(f"x_loaded{p}") for p in range(4)]
        out_stored = sem("out_stored")
        consts_ready = sem("consts_ready")
        zeros_ready = sem("zeros_ready")
        fill_done = sem("fill_done")
        dve_step = sem("dve_step")
        act_step = sem("act_step")
        tile_free = {"act": sem("tile_read_act"), "dve": sem("tile_read_dve")}
        acc_read = sem("accumulator_banks_read")
        acc_done = sem("accumulator_banks_done")
        x_squared = sem("x_squared")
        squares_ready = sem("squares_added")
        sumsq_ready = sem("sumsq_ready")
        std_ready = sem("std_ready")
        rstd_ready = sem("rstd_ready")
        norm_ready = sem("norm_ready")
        h_high_ready = sem("h_high_ready")
        h_low_ready = sem("h_low_ready")
        kv2_ready = sem("kv2_ready")
        r_high_ready = sem("r_high_ready")
        r_low_ready = sem("r_low_ready")
        windows_ready = sem("windows_ready")
        cmp_ht_ready = sem("cmp_hidden_ready")
        cmp_ht_turned = sem("cmp_hidden_turned")
        cmp_hv_ready = sem("cmp_hv_ready")
        cmp_kv_ready = sem("cmp_kv_ready")
        cmp_sq_ready = sem("cmp_sq_ready")
        cmp_sumsq_ready = sem("cmp_sumsq_ready")
        cmp_std_ready = sem("cmp_std_ready")
        cmp_rstd_ready = sem("cmp_rstd_ready")
        cmp_spread = sem("cmp_spread")
        tap_ready = sem("first_tap_ready")
        conv_ready = sem("conv_ready")
        decay_ready = sem("decay_ready")
        var_ready = sem("input_scale_squared_ready")
        scale_ready = sem("input_scale_ready")
        scan_ready = sem("scan_ready")
        gated_ready = sem("gated_scan_ready")
        heads_scaled = sem("heads_scaled")
        head_sq_ready = sem("head_squares_ready")
        head_sumsq_done = sem("head_sumsq_done")
        head_std_ready = sem("head_std_ready")
        head_rstd_ready = sem("head_rstd_ready")
        head_spread = sem("head_spread")
        head_normed = sem("head_normed")
        scores_ready = sem("scores_ready")
        max_ready = sem("max_ready")
        probs_ready = sem("probs_ready")
        probs_turned = sem("probs_turned")
        probs_copied = sem("probs_copied")
        pv_done = sem("pv_done")
        o_read = sem("o_read")
        cmp_scores = sem("cmp_scores")
        cmp_shifted = sem("cmp_shifted")
        cmp_probs = sem("cmp_probs")
        cmp_turned = sem("cmp_turned")
        cmp_copied = sem("cmp_copied")
        cmp_pv = sem("cmp_pv")
        cmp_done = sem("cmp_done")
        o_turned = sem("o_turned")
        mg_scaled = sem("merge_gates_scaled")
        merge_gated = sem("merge_gates_ready")
        z_ready = sem("merged_ready")
        rope_turned = sem("rope_turned")
        rope_done = sem("rope_done")
        c_sq_ready = sem("latent_squares_ready")
        c_sumsq = sem("latent_sumsq_ready")
        c_std_ready = sem("latent_std_ready")
        c_rstd_ready = sem("latent_rstd_ready")
        c_spread = sem("latent_rstd_spread")
        c_normed = sem("latent_normed")
        k2_ready = sem("mla_keys_ready")
        g_scaled = sem("ffn_gate_scaled")
        v_scaled = sem("ffn_value_scaled")
        tap_g = sem("ffn_first_tap_gate")
        tap_g2 = sem("ffn_second_tap_gate")
        conv_g = sem("ffn_conv_gate")
        tap_v = sem("ffn_first_tap_value")
        tap_v2 = sem("ffn_second_tap_value")
        conv_v = sem("ffn_conv_value")
        gelu_ready = sem("ffn_gelu")
        hidden_ready = sem("ffn_hidden")
        hid_high = sem("ffn_hidden_high")
        hid_low = sem("ffn_hidden_low")

        FFN_STEP0 = {0: 0, 1: FFN_BLOCKS[0], 2: FFN_BLOCKS[0] + FFN_BLOCKS[1]}
        CONV_V0 = FFN_BLOCKS[0]
        ACC_V, ACC_YR, ACC_WO, ACC_FFN0, ACC_V1, ACC_WO1, ACC_FFN1, ACC_V2, ACC_WO2, ACC_FFN2 = range(10)
        R_CMP, R_CONV, R_SCAN = 0, 1, 1 + RT
        R_O = [1 + 2 * RT + DT // 2 * n for n in range(3)]
        H_N = {0: 0, 1: 4 + 8, 2: 16, 3: 20, 4: 24, 5: 28 + 5}
        H_Z, H_C = 4, 28

        def f(ap):
            return ap.bitcast(F32)

        block = ctx.enter_context(nc.Block())

        def tile_read(eng, stage, i):
            who, n = TILE_OWNER[TILE0[stage] + i]
            eng.wait_ge(tile_free[who], n)

        LATENTS = (3, 4, 0, 1, 2)
        MG_EARLY = 6
        MG_PER_BRANCH = (SIZE["mg"] - MG_EARLY) // 2

        MG_START = (8, 2)

        def mg_late(h, n):
            h -= MG_START[n]
            return MG_EARLY + MG_PER_BRANCH * n + h // 2 - 1 if h % 2 == 0 and 0 < h <= 2 * MG_PER_BRANCH else None

        def spread_bank(which):
            return bank[(TILE0["uq"] + 2 + which) % TILE_BANKS]

        def mg_bank(i):
            return bank[{0: 1, 2: 6, 3: 5}.get(i, 7)][:, 0:S]

        NORM_CHUNKS = [None, BASE["ffn0"], BASE["v1"], BASE["ffn1"], BASE["c2"], BASE["ffn2"], N_CHUNKS]
        ACC_OF_NORM = [None, ACC_WO, ACC_FFN0, ACC_WO1, ACC_FFN1, ACC_WO2, ACC_FFN2]

        def acc_bank_done(eng, n, p):
            if p < 3:
                eng.wait_ge(acc_done, 3 * (n - 1) + p + 1)
            else:
                eng.wait_ge(chunk_used, NORM_CHUNKS[n])

        def sum_banks(n):
            a, b = (bank[2], bank[3]) if n == 2 else (acc[0], acc[1])
            return a[:, 0:S], b[:, 0:TT]

        def pieces(ap, p):
            return ap[:, 2 * p:2 * p + 2, :]

        def lru_posts(eng, split, post):
            at = 0
            for q in range(SIZE["lru"]):
                c = BASE["lru"] + q
                eng.wait_ge(chunk_used, c + 1)
                while at < len(LRU_GROUPS) and LRU_GROUPS[at][2][-1][0] // 8 <= q:
                    post(at, *LRU_GROUPS[at][:2])
                    at += 1
                split(c + RING)

        @block.sync
        def _(sp):
            def load(c, turn=0, wait=True):
                if wait:
                    sp.wait_ge(low_ready, turn + c - RAW + 1)
                sp.dma_start(w_raw[:, c % RAW, :], weight_stream[turn + c]).then_inc(chunk_loaded[c % RAW], 16)

            for c in range(BODY):
                load(c, wait=c >= RAW)
                if c == 0:
                    for p in range(4):
                        sp.dma_start(pieces(x, p), x_in[:, 2 * p:2 * p + 2, :]).then_inc(x_loaded[p], 16)
            turns = N_CHUNKS // BODY
            with sp.Fori(1, turns) as i:
                for c in range(BODY):
                    load(c, BODY * i)
            for c in range(turns * BODY, N_CHUNKS):
                load(c)
            for p in range(4):
                sp.wait_ge(norm_ready, p + 1)
                sp.dma_start(out[:, 2 * p:2 * p + 2, :], pieces(x_norm, p)).then_inc(out_stored, 16)
            sp.wait_ge(out_stored, 64)

        @block.gpsimd
        def _(pool):
            nc.gpsimd.memset(k0[HD:P, :, 0, :, :], 0.0).then_inc(fill_done, 1)
            pool.wait_ge(fill_done, 1)
            nc.gpsimd.memset(k0[0:HD, :, 1, :, :], 0.0).then_inc(fill_done, 1)
            pool.wait_ge(fill_done, 2)
            nc.gpsimd.memset(cmp_k[HD:P, 0, :], 0.0).then_inc(fill_done, 1)
            pool.wait_ge(fill_done, 3)
            nc.gpsimd.memset(cmp_k[0:HD, 1, :], 0.0).then_inc(fill_done, 1)
            pool.wait_ge(fill_done, 4)
            nc.gpsimd.memset(cmp_hv[:, :, :, :], 0.0).then_inc(fill_done, 1)
            pool.wait_ge(fill_done, 5)
            nc.gpsimd.memset(cmp_v[:, :, :], 0.0).then_inc(zeros_ready, 1)
            pool.wait_ge(zeros_ready, 1)
            pool.wait_ge(acc_read, 4 * ACC_WO + 4)
            nc.gpsimd.memset(k1[HD:P, 0, :, :], 0.0).then_inc(fill_done, 1)
            pool.wait_ge(fill_done, 6)
            nc.gpsimd.memset(k1[0:HD, 1, :, :], 0.0).then_inc(zeros_ready, 1)
            pool.wait_ge(zeros_ready, 2)
            pool.wait_ge(acc_read, 4 * ACC_WO1 + 4)
            nc.gpsimd.memset(k2[96:P, :, :], 0.0).then_inc(zeros_ready, 1)
            pool.wait_ge(rope_done, 17)
            nc.gpsimd.tensor_copy(k2[HD:HD + ROPE, :, :],
                                  c_raw[HD:HD + ROPE, 5:6, :].to_broadcast([ROPE, NH, S])).then_inc(k2_ready, 1)

        @block.tensor
        def _(pe):
            mm = nc.tensor.matmul

            def split_product(out_ap, c, col, high, low, start, stop):
                wh = w_high[:, c % RING, col:col + P]
                wl = w_low[:, c % RING, col:col + P]
                mm(out_ap, wh, high, start=start, stop=False, skip_group_check=True)
                mm(out_ap, wh, low, start=False, stop=False, skip_group_check=True)
                return mm(out_ap, wl, high, start=False, stop=stop, skip_group_check=True)

            def moving_product(out_ap, c, col, n, high, low, start, stop):
                wh = w_high[:, c % RING, col:col + n]
                wl = w_low[:, c % RING, col:col + n]
                mm(out_ap, high, wh, start=start, stop=False, skip_group_check=True)
                mm(out_ap, high, wl, start=False, stop=False, skip_group_check=True)
                return mm(out_ap, low, wh, start=False, stop=stop, skip_group_check=True)

            def chunk_here(c, turn=0):
                pe.wait_ge(low_ready, turn + c + 1)

            def tile_bank(t):
                if t >= TILE_BANKS:
                    who, n = TILE_OWNER[t - TILE_BANKS]
                    pe.wait_ge(tile_free[who], n)
                return bank[t % TILE_BANKS]

            def column_tiles(stage, high, low, h_wait=None, after=None):
                for i in range(SIZE[stage]):
                    c = BASE[stage] + i
                    chunk_here(c)
                    b = tile_bank(TILE0[stage] + i)
                    for k in range(DT):
                        if i == 0 and h_wait:
                            h_wait(k)
                        last = split_product(b[:, 0:S], c, k * P, high[:, k, :], low[:, k, :],
                                             k == 0, k == DT - 1)
                    last.then_inc(chunk_used, 1)
                    if after:
                        after(i)

            def rows_of_bank(c, p, high, low, first, last):
                for m in (2 * p, 2 * p + 1):
                    ins = split_product(acc[p][:, (m % 2) * S:(m % 2 + 1) * S], c, m * P, high, low,
                                        first and m % 2 == 0, last)
                return ins

            def row_chunk(c, high, low, first=False, last=False, sum_next=False):
                for p in range(4):
                    ins = rows_of_bank(c, p, high, low, first, last)
                    if sum_next and p < 3:
                        ins.then_inc(acc_done, 1)
                ins.then_inc(chunk_used, 1)

            def output_projection(stage, high, low, h_wait=None):
                for k in range(DT - LATE):
                    chunk_here(BASE[stage] + k)
                    if h_wait:
                        h_wait(k)
                    row_chunk(BASE[stage] + k, high[:, k, :], low[:, k, :], first=k == 0)
                chunk_here(BASE[stage] + DT - 1)
                for k in range(DT - LATE, DT):
                    if h_wait:
                        h_wait(k)
                for p in range(4):
                    for k in range(DT - LATE, DT):
                        ins = rows_of_bank(BASE[stage] + k, p, high[:, k, :], low[:, k, :], False, k == DT - 1)
                        if p == 3:
                            ins.then_inc(chunk_used, 1)
                    if p < 3:
                        ins.then_inc(acc_done, 1)

            def norm_sums(n):
                if n:
                    pe.wait_ge(acc_read, 4 * ACC_OF_NORM[n] + 4)
                pe.wait_ge(squares_ready, n + 1)
                every, column = sum_banks(n)
                for k in range(2):
                    ins = mm(every, ones.to_broadcast([P, P]), squares[:, k, :], start=k == 0, stop=k == 1)
                if n in (0, 2):
                    for t in range(TT):
                        for k in range(2):
                            ins = mm(column[:, t:t + 1], squares[:, k, t * P:(t + 1) * P], ones,
                                     start=k == 0, stop=k == 1)
                ins.then_inc(sumsq_ready, 1)

            def attention(n, q, kpad, v, probs, probs_t, banks_free, before=None, between=None):
                def scores(h):
                    if before:
                        before(h)
                    if h >= 3 or n == 1:
                        pe.wait_ge(probs_ready, NH * n + max(h - 2, 0))
                    b = bank[h % 3]
                    mm(b[:, 0:P], q(h, 0), kpad(h)[:, 0:P], start=True, stop=False, skip_group_check=True)
                    mm(b[:, P:3 * P], q(h, 1), kpad(h), start=False, stop=False, skip_group_check=True)
                    mm(b[:, :].rearrange("p (a c) -> p a c", c=2 * P)[:, :, 0:P], ident_b[:, :],
                       mask_b[:, :].unsqueeze(1).to_broadcast([P, 2, P]), start=False, stop=True,
                       skip_group_check=True).then_inc(scores_ready, 1)

                def turn(h):
                    pe.wait_ge(probs_ready, NH * n + h + 1)
                    if h >= 2:
                        pe.wait_ge(probs_copied, NH * n + h - 1)
                    for j in range(3):
                        ins = nc.tensor.transpose(bank[3 + h % 2][:, j * P:(j + 1) * P],
                                                  probs[:, h % 3, j * P:(j + 1) * P], ident)
                    ins.then_inc(probs_turned, 1)

                def values(h):
                    pe.wait_ge(probs_copied, NH * n + h + 1)
                    g = h // 4
                    if h % 4 == 0 and g >= 2:
                        pe.wait_ge(o_read, 4 * n + g - 1)
                    b = bank[5 + g % 2]
                    pt = probs_t[:, h % 2, :]
                    at = (h % 4) * HD
                    mm(b[:, at:at + HD], pt[:, 0:P], v(h, 0), start=True, stop=True)
                    mm(b[:, S + at:S + at + HD], pt[:, P:2 * P], v(h, 0), start=True, stop=False)
                    mm(b[:, S + at:S + at + HD], pt[:, 2 * P:3 * P], v(h, 1), start=False,
                       stop=True).then_inc(pv_done, 1)

                for h in range(NH + 3):
                    if h < NH:
                        scores(h)
                    if h == 2:
                        banks_free()
                    if 2 <= h < NH + 2:
                        turn(h - 2)
                    if h >= 3:
                        values(h - 3)
                    if between:
                        between(h)

            def turn_output(n, o):
                flat = o.rearrange("p t h d -> p t (h d)")
                pe.wait_ge(probs_ready, NH * (n + 2))
                pe.wait_ge(probs_copied, NH * (n + 2))
                for p in range(DT // 2):
                    pe.wait_ge(o_read, 4 * (n + 1) + p + 1)
                    for m in (2 * p, 2 * p + 1):
                        for t in range(TT):
                            at = (m % 2) * S + t * P
                            ins = nc.tensor.transpose(bank[p][:, at:at + P], flat[:, t, m * P:(m + 1) * P], ident)
                    ins.then_inc(o_turned, 1)

            def turned(n):
                return lambda k: pe.wait_ge(r_low_ready, R_O[n] + k // 2 + 1) if k % 2 == 0 else None

            def feed_forward(n, acc_use):
                base, s0, blocks = BASE[f"ffn{n}"], FFN_STEP0[n], FFN_BLOCKS[n]

                def gate_and_up(j, c, turn=0, first=False):
                    for which in range(2):
                        chunk_here(c + which, turn)
                        for k in range(DT):
                            if first and which == 0 and k % 2 == 0:
                                pe.wait_ge(h_low_ready, H_N[2 * n + 1] + k // 2 + 1)
                            last = split_product(bank[2 * which + j % 2][:, 0:S], c + which, k * P,
                                                 h_high[:, k, :], h_low[:, k, :], k == 0, k == DT - 1)
                        last.then_inc(chunk_used, 1)
                        if first and which == 0:
                            norm_sums(2 * n + 1)

                def down(j, c, turn=0, more=0, first=False, last=False, sum_next=False):
                    pe.wait_ge(hid_low, s0 + j + more + 1)
                    chunk_here(c, turn)
                    row_chunk(c, r_high[:, j % 2, :], r_low[:, j % 2, :], first=first, last=last,
                              sum_next=sum_next)

                gate_and_up(0, base, first=True)
                gate_and_up(1, base + 2)
                pe.wait_ge(std_ready, 2 * n + 2)
                down(0, base + 4, first=True)
                turns = (blocks - 3) // 2
                with pe.Fori(0, turns) as i:
                    for q in range(2):
                        c = base + 5 + 3 * q
                        gate_and_up(2 + q, c, BODY * i)
                        down(1 + q, c + 2, BODY * i, more=2 * i)
                for j in range(2 + 2 * turns, blocks):
                    c = base + 3 * j - 1
                    gate_and_up(j, c)
                    down(j - 1, c + 2)
                down(blocks - 1, base + 3 * blocks - 1, last=True, sum_next=True)

            pe.wait_ge(norm_loaded, 16)
            column_tiles("kvc", h_high, h_low,
                         lambda k: pe.wait_ge(h_low_ready, H_N[0] + k // 2 + 1) if k % 2 == 0 else None,
                         after=lambda i: norm_sums(0) if i == 1 else None)
            column_tiles("rgate", h_high, h_low)
            pe.wait_ge(small_loaded, 16)
            pe.wait_ge(r_low_ready, R_CMP + 1)
            flat_high, flat_low = (r[:, :, :].rearrange("p k t -> p (k t)") for r in (r_high, r_low))
            for j in range(CL // 2):
                c = BASE["w1"] + j // 4
                if j % 4 == 0:
                    chunk_here(c)
                ins = moving_product(acc[2][0:WIN, 0:2 * P], c, (j % 4) * 2 * P, 2 * P,
                                     flat_high[:, j * WIN:(j + 1) * WIN], flat_low[:, j * WIN:(j + 1) * WIN],
                                     j == 0, j == CL // 2 - 1)
                if j % 4 == 3:
                    ins.then_inc(chunk_used, 1)

            def compression(i):
                if i == 1:
                    pe.wait_ge(cmp_ht_ready, 1)
                    nc.tensor.transpose(acc[3][:, 0:WIN], cmp_ht[0:WIN, :], ident[0:WIN, 0:WIN]).then_inc(cmp_ht_turned, 1)
                if i == 4:
                    pe.wait_ge(std_ready, 1)
                    pe.wait_ge(cmp_hv_ready, 1)
                    mm(acc[0][:, 0:60], par("w2k"), cmp_hid, start=True, stop=True)
                    for g in range(NKV):
                        ins = mm(acc[1][:, g * HD:(g + 1) * HD], cmp_hv[:, g, :, :].rearrange("p r c -> p (r c)"),
                                 par("w2v"), start=True, stop=True)
                    ins.then_inc(cmp_kv_ready, 1)
                if i == 6:
                    pe.wait_ge(cmp_sq_ready, 1)
                    mm(acc[2][0:60, 0:1], cmp_ksq, blk2[:, 0:1], start=True, stop=True).then_inc(cmp_sumsq_ready, 1)
                if i == 10:
                    pe.wait_ge(cmp_rstd_ready, 1)
                    mm(acc[3][:, 0:60], cmp_rstd[0:60, :].to_broadcast([60, P]), ident[0:60, 0:60],
                       start=True, stop=True).then_inc(cmp_spread, 1)

            column_tiles("rx", h_high, h_low, after=compression)
            for t, (gate, m, blocks) in enumerate(LRU_GROUPS):
                b = tile_bank(TILE0["lru"] + t)
                pe.wait_ge(r_low_ready, R_CONV + blocks[-1][1] + 1)
                for n, (at, k) in enumerate(blocks):
                    c = BASE["lru"] + at // 8
                    if at % 8 == 0:
                        chunk_here(c)
                    ins = split_product(b[:, 0:S], c, at % 8 * P, r_high[:, k, :], r_low[:, k, :],
                                        n == 0, n == len(blocks) - 1)
                    if at % 8 == 7 or at == len(GATES) - 1:
                        ins.then_inc(chunk_used, 1)
            def head_sums(e):
                pe.wait_ge(head_sq_ready, e + 1)
                if e == 0:
                    pe.wait_ge(head_normed, 1)
                for t in range(TT):
                    at = (t * 12 + e) * 2
                    ins = mm(acc[0][:, at:at + 2], head_sq[:, e % 2, t * P:(t + 1) * P], blk2,
                             start=True, stop=True)
                ins.then_inc(head_sumsq_done, 1)

            column_tiles("k", h_high, h_low, after=lambda i: head_sums(i - 1) if i else None)
            column_tiles("q", h_high, h_low, after=lambda i: head_sums(i + 3))
            for i in range(4):
                c = BASE["v"] + i
                chunk_here(c)
                for k in (2 * i, 2 * i + 1):
                    for t in range(TT):
                        ins = moving_product(acc[1 + t][:, :], c, (k % 2) * 512, 512, h_high[:, k, t * P:(t + 1) * P],
                                             h_low[:, k, t * P:(t + 1) * P], k == 0, k == DT - 1)
                ins.then_inc(chunk_used, 1)
                if i == 0:
                    head_sums(11)
            c = BASE["g"]
            chunk_here(c)
            for k in range(DT):
                for t in range(TT):
                    ins = moving_product(acc[3][:, t * 64:t * 64 + 3 * NH], c, k * P, 3 * NH,
                                         h_high[:, k, t * P:(t + 1) * P], h_low[:, k, t * P:(t + 1) * P],
                                         k == 0 and t == 0, k == DT - 1)
            ins.then_inc(chunk_used, 1)

            def spread_heads(e):
                if e == 0:
                    pe.wait_ge(head_rstd_ready, 1)
                if e >= TILE_BANKS:
                    pe.wait_ge(head_normed, 1 + e - TILE_BANKS + 1)
                for t in range(TT):
                    for j in range(2):
                        ins = mm(bank[e % TILE_BANKS][HD * j:HD * (j + 1), t * P:(t + 1) * P],
                                 head_rstd[:, t, e, j:j + 1].to_broadcast([P, HD]), ident, start=True, stop=True)
                ins.then_inc(head_spread, 1)

            tile_read(pe, "q", 7)
            pe.wait_ge(head_std_ready, 2)
            pe.wait_ge(acc_read, 4 * ACC_V + 4)
            for k in range(RT):
                chunk_here(BASE["yr"] + k)
                pe.wait_ge(r_low_ready, R_SCAN + k + 1)
                row_chunk(BASE["yr"] + k, r_high[:, k, :], r_low[:, k, :], first=k == 0, last=k == RT - 1)
                spread_heads(k)
            spread_heads(RT)

            def merge_gates(i, halves=(0, 1)):
                c = BASE["mg"] + i
                if 0 in halves:
                    chunk_here(c)
                    if i >= 4:
                        pe.wait_ge(mg_scaled, 2 if i == 4 else i)
                b = mg_bank(i)
                for half in halves:
                    for k in range(4 * half, 4 * half + 4):
                        ins = split_product(b, c, k * P, h_high[:, k, :], h_low[:, k, :], k == 0, k == DT - 1)
                if 1 in halves:
                    ins.then_inc(chunk_used, 1)

            pe.wait_ge(consts_ready, 1)
            pe.wait_ge(head_normed, 1 + 10)
            merge_gates(0)
            pe.wait_ge(head_normed, 1 + 12)
            for t in range(TT):
                for e in range(DT):
                    dst = bank[0][:, (t * NH + 2 * e) * 16:(t * NH + 2 * e + 2) * 16]
                    ins = mm(dst.rearrange("p (h c) -> p h c", h=2)[:, :, 0:NC], q0[:, e, t * P:(t + 1) * P],
                             cmp_k[:, :, e // 2:e // 2 + NKV * (NC - 1) + 1:NKV], start=True, stop=True)
            ins.then_inc(cmp_scores, 1)
            pe.wait_ge(acc_read, 4 * ACC_YR + 4)
            for i in (1, 2, 3):
                merge_gates(i)
            pe.wait_ge(cmp_probs, 1)
            pe.wait_ge(mg_scaled, 1)
            for i in range(8):
                ins = nc.tensor.transpose(bank[1 + i // 4][:, (i % 4) * P:(i % 4 + 1) * P],
                                          cmp_p[:, i // 4, 4 * (i % 4):4 * (i % 4) + 4, :]
                                          .rearrange("p h c -> p (h c)"), ident)
            ins.then_inc(cmp_turned, 1)
            merge_gates(4)
            pe.wait_ge(cmp_copied, 2)
            pe.wait_ge(mg_scaled, 4)
            for t in range(TT):
                for g in range(NKV):
                    ins = mm(bank[3 + 2 * t + g // 2][:, (g % 2) * 256:(g % 2 + 1) * 256],
                             cmp_pt[:, 4 * t + g, :], cmp_v[:, g, :], start=True, stop=True)
                ins.then_inc(cmp_pv, 1)
            merge_gates(5)

            def merge_between(h, n):
                h -= MG_START[n]
                if 0 <= h < 2 * MG_PER_BRANCH:
                    merge_gates(MG_EARLY + MG_PER_BRANCH * n + h // 2, (h % 2,))

            def banks_free_0():
                if n == 0:
                    pe.wait_ge(cmp_done, 4)
                else:
                    pe.wait_ge(probs_copied, NH)
                    pe.wait_ge(o_read, 4)

            for n in range(2):
                attention(n, lambda h, t: q0[:, h // 2, t * P:(t + 1) * P],
                          lambda h: k0[:, n, h % 2, h // 4, :],
                          lambda h, t: v0[:, n, t, (h // 4) * HD:(h // 4 + 1) * HD], probs0, probs_t0,
                          banks_free_0, between=lambda h: merge_between(h, n))
            pe.wait_ge(mg_scaled, 16)
            turn_output(0, o0)
            for k in range(0, DT, 2):
                turned(0)(k)
            column_tiles("ao", r_high, r_low)
            pe.wait_ge(acc_read, 4 * ACC_YR + 4)
            output_projection("wo", h_high, h_low, lambda k: pe.wait_ge(h_low_ready, H_Z + k + 1))
            feed_forward(0, ACC_FFN0)


            def values_all(stage, n_k, h0=0, before=None, after=None):
                for k in range(n_k):
                    c = BASE[stage] + k
                    chunk_here(c)
                    if before:
                        before(k)
                    for t in range(TT):
                        for half in range(2):
                            ins = moving_product(acc[2 * t + half][:, :], c, half * 512, 512,
                                                 h_high[:, h0 + k, t * P:(t + 1) * P], h_low[:, h0 + k, t * P:(t + 1) * P],
                                                 k == 0, k == n_k - 1)
                    ins.then_inc(chunk_used, 1)
                    if after:
                        after(k)

            pe.wait_ge(acc_read, 4 * ACC_FFN0 + 4)
            values_all("v1", DT, before=lambda k: pe.wait_ge(h_low_ready, H_N[2] + k // 2 + 1) if k % 2 == 0 else None,
                       after=lambda k: norm_sums(2) if k == 1 else None)
            pe.wait_ge(std_ready, 3)

            def turn_rope(e):
                if e == 0:
                    pe.wait_ge(acc_read, 4 * ACC_V1 + 4)
                tile_read(pe, "q1" if e < 8 else "k1", e % 8)
                if e >= 2:
                    pe.wait_ge(rope_done, e - 1)
                mm(acc[e % 2][:, 0:S], par("rot64"), rope_in[:, e % 2, :], start=True,
                   stop=True).then_inc(rope_turned, 1)

            column_tiles("q1", h_high, h_low, after=lambda i: turn_rope(i - 1) if i else None)
            column_tiles("k1", h_high, h_low, after=lambda i: turn_rope(i + 7))
            turn_rope(15)
            pe.wait_ge(zeros_ready, 2)
            tile_read(pe, "k1", 7)
            attention(2, lambda h, t: q1[:, h // 2, t * P:(t + 1) * P], lambda h: k1[:, h % 2, h // 2, :],
                      lambda h, t: v1[:, t, h * HD:(h + 1) * HD], probs1, probs_t1,
                      lambda: pe.wait_ge(rope_done, 16),
                      lambda h: pe.wait_ge(rope_done, 8 + h // 2 + 1))
            turn_output(1, o1)
            output_projection("wo1", r_high, r_low, turned(1))
            feed_forward(1, ACC_FFN1)

            column_tiles("c2", h_high, h_low,
                         lambda k: pe.wait_ge(h_low_ready, H_N[4] + k // 2 + 1) if k % 2 == 0 else None,
                         after=lambda i: norm_sums(4) if i == 1 else None)
            pe.wait_ge(std_ready, 5)
            pe.wait_ge(c_sq_ready, 1)
            for which, (a, b) in enumerate(((0, 3), (3, 5))):
                for t in range(TT):
                    for e in range(a, b):
                        ins = mm(acc[0][:, 2 * which + t:2 * which + t + 1], c_sq[:, e, t * P:(t + 1) * P], ones,
                                 start=e == a, stop=e == b - 1)
            ins.then_inc(c_sumsq, 1)
            pe.wait_ge(c_rstd_ready, 1)
            tile_read(pe, "c2", 5)
            for which in range(2):
                for t in range(TT):
                    ins = mm(spread_bank(which)[:, t * P:(t + 1) * P],
                             c_rstd[:, 2 * which + t:2 * which + t + 1].to_broadcast([P, P]), ident,
                             start=True, stop=True)
            ins.then_inc(c_spread, 1)
            values_all("uv", 2, h0=3, before=lambda k: pe.wait_ge(h_low_ready, H_C + k + 1))
            pe.wait_ge(c_normed, 5)
            for h in range(NH):
                b = tile_bank(TILE0["uq"] + h)
                for k in range(3):
                    n = 3 * h + k
                    c = BASE["uq"] + n // 8
                    if n % 8 == 0:
                        chunk_here(c)
                    if h == 0:
                        pe.wait_ge(h_low_ready, H_C + 2 + k + 1)
                    ins = split_product(b[:, 0:S], c, n % 8 * P, h_high[:, k, :], h_low[:, k, :], k == 0, k == 2)
                    if n % 8 == 7:
                        ins.then_inc(chunk_used, 1)
            for m in range(8):
                b = tile_bank(TILE0["uk"] + m)
                for k in range(2):
                    n = 2 * m + k
                    c = BASE["uk"] + n // 8
                    if n % 8 == 0:
                        chunk_here(c)
                    ins = split_product(b[:, 0:S], c, n % 8 * P, h_high[:, 3 + k, :], h_low[:, 3 + k, :],
                                        k == 0, k == 1)
                    if n % 8 == 7:
                        ins.then_inc(chunk_used, 1)
            pe.wait_ge(acc_read, 4 * ACC_V2 + 4)
            pe.wait_ge(k2_ready, 1)
            pe.wait_ge(zeros_ready, 3)

            def queries_and_keys(h):
                pe.wait_ge(rope_done, 16 + 1 + h // 2 + 1)
                if h < 2:
                    tile_read(pe, "uk", 4 + (h - TILE0["uk"]) % TILE_BANKS)
                elif h == 2:
                    tile_read(pe, "uk", 7)

            attention(3, lambda h, t: q2[:, h, t * P:(t + 1) * P], lambda h: k2[:, h, :],
                      lambda h, t: v2[:, t, h * HD:(h + 1) * HD], probs2, probs_t2,
                      lambda: None,
                      queries_and_keys)
            turn_output(2, o2)
            output_projection("wo2", r_high, r_low, turned(2))
            feed_forward(2, ACC_FFN2)
            norm_sums(6)

        @block.scalar
        def _(act):
            fn = nc.scalar.activation

            def split_high(c, i=None):
                if c >= N_CHUNKS:
                    return
                turn, turn_dma = (0, 0) if i is None else (BODY * i, 16 * (BODY // RAW) * i)
                act.wait_ge(chunk_loaded[c % RAW], turn_dma + 16 * (c // RAW + 1))
                if c >= RING:
                    act.wait_ge(chunk_used, turn + c - RING + 1)
                fn(w_high[:, c % RING, :], w_raw[:, c % RAW, :], ACT.Copy).then_inc(high_ready, 1)

            def stage(name, post, count=None):
                for i in range(count or SIZE[name]):
                    c = BASE[name] + i
                    act.wait_ge(chunk_used, c + 1)
                    post(i)
                    split_high(c + RING)

            def stage_behind(name, post):
                for i in range(SIZE[name]):
                    c = BASE[name] + i
                    split_high(c + RING)
                    post(i)

            def late_splits(end, count):
                for c in range(end - count, end):
                    split_high(c + RING)

            def tile(name, i):
                return bank[(TILE0[name] + i) % TILE_BANKS][:, 0:S]

            def freed(ins):
                ins.then_inc(tile_free["act"], 1)

            def read_acc(p, ap, scale=1.0):
                fn(ap, acc[p][:, :], ACT.Identity, scale=scale).then_inc(acc_read, 1)

            def norm(n):
                for p in range(4):
                    if n == 0:
                        act.wait_ge(x_loaded[p], 16)
                    if n:
                        act.wait_ge(acc_read, 4 * ACC_OF_NORM[n] + p + 1)
                    if n == 1 and p >= 2:
                        acc_bank_done(act, n, 3)
                    if n < 6:
                        for k in (2 * p, 2 * p + 1):
                            ins = fn(h_high[:, k, :], x[:, k, :], ACT.Identity, scale=par("norm", n * DT + k, 1))
                        ins.then_inc(h_high_ready, 1)
                    fn(pieces(squares, p), pieces(x, p), ACT.Square).then_inc(x_squared, 1)
                    if n == 0 and p == 2:
                        split_high(1)

            def roots(n):
                act.wait_ge(sumsq_ready, n + 1)
                every, column = sum_banks(n)
                ins = fn(rstd[:, :], every, ACT.Sqrt, bias=eps_col, scale=1.0 / D)
                if n in (0, 2):
                    ins = fn(std_col, column, ACT.Sqrt, bias=eps_col, scale=1.0 / D)
                ins.then_inc(std_ready, 1)

            def attention(n, probs, between=None):
                for h in range(NH + 3):
                    if h >= NH:
                        if between:
                            between(h)
                        continue
                    act.wait_ge(max_ready, NH * n + h + 1)
                    if h >= 3:
                        act.wait_ge(probs_turned, NH * n + h - 2)
                    b = bank[h % 3]
                    fn(probs[:, h % 3, 0:P], b[:, 0:P], ACT.Exp, bias=neg_max[:, h, 0:1],
                       accum_out=sums[:, 0, h:h + 1])
                    fn(probs[:, h % 3, P:3 * P], b[:, P:3 * P], ACT.Exp, bias=neg_max[:, h, 1:2],
                       accum_out=sums[:, 1, h:h + 1]).then_inc(probs_ready, 1)
                    if between:
                        between(h)

            def output_high(n):
                for p in range(DT // 2):
                    act.wait_ge(o_turned, DT // 2 * n + p + 1)
                    fn(pieces(r_high, p).rearrange("p k t -> p (k t)"), bank[p][:, :], ACT.Copy).then_inc(r_high_ready, 1)

            def feed_forward(n):
                base, s0, blocks, both = BASE[f"ffn{n}"], FFN_STEP0[n], FFN_BLOCKS[n], n == 0
                func = ACT.Gelu_apprx_tanh if both else ACT.Gelu

                def tap(name, row, j):
                    at = AT[name][0] + row * blocks
                    return small[:, at + j:at + j + 1] if isinstance(j, int) else small[:, bass.ds(j + at, 1)]

                def step(j, c, i=None):
                    turn, k = (0, 0) if i is None else (BODY * i, 2 * i)
                    act.wait_ge(chunk_used, turn + c + 1)
                    if i is None and j == 0:
                        roots(2 * n + 1)
                    if j:
                        split_high(c + RING, i)
                    act.wait_ge(g_scaled, k + (s0 + j + 1))
                    fn(taps_g[:, j % 2, :], scaled_g[:, j % 2, :], ACT.Identity, scale=tap(f"fcw{n}", 2, k + j),
                       bias=tap(f"fcb{n}", 0, k + j)).then_inc(tap_g, 1)
                    if 0 < j < blocks - 1:
                        split_high(c + 1 + RING, i)
                    if both:
                        act.wait_ge(v_scaled, k + (s0 + j + 1))
                        fn(taps_v[:, j % 2, :], scaled_v[:, j % 2, :], ACT.Identity,
                           scale=tap("fcw0", 5, k + j), bias=tap("fcb0", 1, k + j)).then_inc(tap_v, 1)
                    act.wait_ge(conv_g, k + (s0 + j + 1))
                    fn(gelu_g[:, j % 2, :], taps_g[:, j % 2, :], func).then_inc(gelu_ready, 1)
                    if 0 < j < blocks - 1:
                        split_high(c + 2 + RING, i)
                    act.wait_ge(hidden_ready, k + (s0 + j + 1))
                    fn(r_high[:, j % 2, :], hidden[:, j % 2, :], ACT.Copy).then_inc(hid_high, 1)
                    if j == 0:
                        split_high(c + RING)
                        split_high(c + 1 + RING)

                step(0, base)
                step(1, base + 2)
                turns = (blocks - 3) // 2 - (n == 2)
                with act.Fori(0, turns) as i:
                    for q in range(2):
                        step(2 + q, base + 5 + 3 * q, i)
                for j in range(2 + 2 * turns, blocks):
                    step(j, base + 3 * j - 1)

            act.dma_start(small[:, 0:N_FIRST], small_in[:, 0:N_FIRST]).then_inc(norm_loaded, 16)
            act.wait_ge(norm_loaded, 16)
            split_high(0)
            act.dma_start(small[:, N_FIRST:], small_in[:, N_FIRST:]).then_inc(small_loaded, 16)
            norm(0)
            for c in range(2, RING // 2):
                split_high(c)
            act.wait_ge(small_loaded, 16)
            fn(ident_b[:, :], ident, ACT.Copy)
            fn(mask_b[:, :], par("mask"), ACT.Copy).then_inc(consts_ready, 1)
            fn(lru_t[0], par("lam"), ACT.Abs).then_inc(act_step, 1)
            act.wait_ge(act_step, 1)
            fn(lru_t[1], lru_t[0], ACT.Exp, scale=-1.0).then_inc(act_step, 1)
            roots(0)
            for c in range(RING // 2, RING):
                split_high(c)

            def kvc(i):
                tile_read(act, "kvc", i)
                g = 4 * (i // 2) + 2 * (i % 2)
                for j in range(2):
                    rows = slice(HD * j, HD * (j + 1))
                    fn(kv2[0:HD, g + j, :], kv_scaled[rows, i, :], ACT.Copy)
                    ins = fn(kv2[HD:P, g + j, 0:S - 1], kv_scaled[rows, i, 1:S], ACT.Copy)
                ins.then_inc(kv2_ready, 1)

            stage_behind("kvc", kvc)

            def rgate(i):
                tile_read(act, "rgate", i)
                fn(gelu_gate[:, i, :], gelu_gate[:, i, :], ACT.Gelu_apprx_tanh)
                if i == 4:
                    act.wait_ge(windows_ready, 2)
                    fn(r_high[:, :, :].rearrange("p k t -> p (k t)")[:, 0:CL // 2 * WIN], windows,
                       ACT.Copy).then_inc(r_high_ready, 1)

            stage_behind("rgate", rgate)

            def hidden_cmp(i):
                if i < 3:
                    return
                fn(cmp_ht[0:HD, :], acc[2][0:HD, 0:P], ACT.Gelu_apprx_tanh)
                fn(cmp_ht[HD:WIN, :], acc[2][HD:WIN, P:2 * P], ACT.Gelu_apprx_tanh).then_inc(cmp_ht_ready, 1)

            stage("w1", hidden_cmp)

            def conv_high(i):
                act.wait_ge(conv_ready, i + 1)
                fn(r_high[:, i, :], conv[:, i, :], ACT.Copy).then_inc(r_high_ready, 1)

            def rx(i):
                tile_read(act, "rx", i)
                fn(conv[:, i, :], rx_scaled[:, i % 3, :], ACT.Identity, scale=par("rcw", 3 * RT + i, 1),
                   bias=par("rcb", i, 1)).then_inc(tap_ready, 1)
                if i >= 2:
                    conv_high(i - 2)
                if i == 2:
                    act.wait_ge(cmp_ht_turned, 1)
                    fn(cmp_hid, acc[3][:, 0:60], ACT.Copy)
                    act.wait_ge(zeros_ready, 1)
                    for r in range(4):
                        ins = fn(cmp_hv[:, :, r, 0:NC], acc[3][:, HD:HD + 60].rearrange("p (c g) -> p g c", g=NKV),
                                 ACT.Copy)
                    ins.then_inc(cmp_hv_ready, 1)
                if i == 5:
                    act.wait_ge(cmp_kv_ready, 1)
                    fn(cmp_kraw, acc[0][:, 0:60], ACT.Identity, scale=par("hg", 1, 1))
                    fn(cmp_ksq, acc[0][:, 0:60], ACT.Square).then_inc(cmp_sq_ready, 1)
                if i == 7:
                    act.wait_ge(cmp_sumsq_ready, 1)
                    fn(cmp_std[0:60, :], acc[2][0:60, 0:1], ACT.Sqrt, bias=eps_col[0:60, :],
                       scale=1.0 / HD).then_inc(cmp_std_ready, 1)

            stage_behind("rx", rx)
            conv_high(RT - 2)
            conv_high(RT - 1)

            def lru_gate(t, gate, m):
                dst, bias = ((r_gate, "rba"), (i_gate, "rbx"))[gate]
                freed(fn(dst[:, m, :], tile("lru", t), ACT.Sigmoid, bias=par(bias, m, 1)))

            lru_posts(act, split_high, lru_gate)
            def heads(e):
                act.wait_ge(heads_scaled, e + 1)
                fn(head_sq[:, e % 2, :], head_sq[:, e % 2, :], ACT.Square).then_inc(head_sq_ready, 1)
                if e < RT:
                    fn(decay[:, e, :], r_gate[:, e, :], ACT.Exp, scale=lru_k[:, e:e + 1])
                    fn(r_gate[:, e, :], r_gate[:, e, :], ACT.Tanh, scale=lru_kn[:, e:e + 1]).then_inc(decay_ready, 1)

            tile_read(act, "lru", 2 * RT - 1)
            stage_behind("k", heads)
            stage_behind("q", lambda i: heads(4 + i))
            head_sumsq = acc[0][:, 0:48].rearrange("p (t e j) -> p t e j", t=TT, j=2)
            for a, b in ((0, 4), (4, 8), (8, RT)):
                act.wait_ge(var_ready, b)
                fn(conv[:, a:b, :], conv[:, a:b, :], ACT.Sqrt).then_inc(scale_ready, 1)
            act.wait_ge(head_sumsq_done, 12)
            fn(head_std[:, :, 0:4, :], head_sumsq[:, :, 0:4, :], ACT.Sqrt, bias=eps_col,
               scale=1.0 / HD).then_inc(head_std_ready, 1)
            fn(head_std[:, :, 4:12, :], head_sumsq[:, :, 4:12, :], ACT.Sqrt, bias=eps64_col).then_inc(head_std_ready, 1)

            def scan_high(m):
                act.wait_ge(gated_ready, m + 1)
                fn(r_high[:, m, :], i_gate[:, m, :], ACT.Copy).then_inc(r_high_ready, 1)

            for i in range(5):
                if i == 3:
                    act.wait_ge(chunk_used, BASE["g"] + 1)
                    for t in range(TT):
                        read_acc(1 + t, v0[:, :, t, :], scale=rstd_col[:, t:t + 1])
                    for t in range(TT):
                        fn(stats[:, 200 + 48 * t:248 + 48 * t], acc[3][:, t * 64:t * 64 + 3 * NH],
                           ACT.Sigmoid, scale=rstd_col[:, t:t + 1]).then_inc(acc_read, 1)
                scan_high(2 * i)
                split_high(BASE["v"] + i + RING)
                scan_high(2 * i + 1)
            scan_high(RT - 1)
            stage("yr", lambda i: None, RT - 1)
            act.wait_ge(chunk_used, BASE["yr"] + RT)
            for p in range(4):
                read_acc(p, pieces(y_rnn, p).rearrange("p k t -> p (k t)"))
            split_high(BASE["yr"] + RT - 1 + RING)
            split_high(BASE["mg"] + RING)
            act.wait_ge(cmp_shifted, 1)
            fn(cmp_p[:, :, :, 0:NC], cmp_s, ACT.Exp).then_inc(cmp_probs, 1)
            for i in (1, 2, 3):
                split_high(BASE["mg"] + i + RING)
            act.wait_ge(cmp_turned, 1)
            fn(cmp_pt[:, 0:4, :], bank[1][:, :], ACT.Copy).then_inc(cmp_copied, 1)
            for i in (4, 5):
                split_high(BASE["mg"] + i + RING)

            def merge_gate(h, n):
                if mg_late(h, n) is not None:
                    split_high(BASE["mg"] + mg_late(h, n) + RING)

            for n in range(2):
                attention(n, probs0, lambda h: merge_gate(h, n))
            output_high(0)
            act.wait_ge(mg_scaled, 16)
            for i in range(4):
                fn(merge[:, 4 * i:4 * i + 4, :], merge[:, 4 * i:4 * i + 4, :], ACT.Sigmoid).then_inc(merge_gated, 1)

            def merged(i):
                act.wait_ge(z_ready, i + 1)
                fn(h_high[:, i, :], y_rnn[:, i, :], ACT.Copy).then_inc(h_high_ready, 1)

            stage_behind("ao", merged)
            stage("wo", lambda i: None, DT - LATE)
            norm(1)
            late_splits(BASE["ffn0"], LATE)
            feed_forward(0)

            norm(2)
            late_splits(BASE["v1"], 3)
            roots(2)

            stage("v1", lambda i: None, SIZE["v1"] - 1)
            act.wait_ge(chunk_used, BASE["v1"] + SIZE["v1"])
            for p in range(4):
                read_acc(p, v1[:, p // 2, (p % 2) * 512:(p % 2 + 1) * 512], scale=rstd_col[:, p // 2:p // 2 + 1])
            split_high(BASE["v1"] + SIZE["v1"] - 1 + RING)

            def rope_operand(e):
                if e >= 2:
                    act.wait_ge(rope_done, e - 1)
                freed(fn(rope_in[:, e % 2, :], tile("q1", e), ACT.Copy, scale=HD ** -0.5 if e < 8 else 1.0))

            stage("q1", rope_operand)
            stage("k1", lambda i: rope_operand(8 + i))
            attention(2, probs1)
            output_high(1)
            stage("wo1", lambda i: None, DT - LATE)
            norm(3)
            late_splits(BASE["ffn1"], LATE)
            feed_forward(1)

            norm(4)
            late_splits(BASE["c2"], 3)
            roots(4)

            def latents(e):
                tile_read(act, "c2", e)
                if e < 5:
                    ins = fn(c_sq[:, e, :], c_raw[:, e, :], ACT.Square)
                    if e == 4:
                        ins.then_inc(c_sq_ready, 1)

            stage_behind("c2", latents)
            act.wait_ge(c_sumsq, 1)
            for which, n in enumerate((QL, KVL)):
                ins = fn(c_std[:, 2 * which:2 * which + 2], acc[0][:, 2 * which:2 * which + 2], ACT.Sqrt,
                         bias=eps_col, scale=1.0 / n)
            ins.then_inc(c_std_ready, 1)
            for n, e in enumerate(LATENTS):
                act.wait_ge(c_normed, n + 1)
                fn(h_high[:, e, :], c_norm[:, e, :], ACT.Copy).then_inc(h_high_ready, 1)
            stage("uv", lambda i: None, SIZE["uv"] - 1)
            act.wait_ge(chunk_used, BASE["uv"] + SIZE["uv"])
            for p in range(4):
                read_acc(p, v2[:, p // 2, (p % 2) * 512:(p % 2 + 1) * 512])
            split_high(BASE["uv"] + SIZE["uv"] - 1 + RING)
            at = 0
            for q in range(SIZE["uq"]):
                act.wait_ge(chunk_used, BASE["uq"] + q + 1)
                while at < NH and (3 * at + 2) // 8 <= q:
                    freed(fn(q2[:, at, :], tile("uq", at), ACT.Copy, scale=(HD + ROPE) ** -0.5))
                    at += 1
                split_high(BASE["uq"] + q + RING)
            for q in range(SIZE["uk"]):
                act.wait_ge(chunk_used, BASE["uk"] + q + 1)
                for m in range(4 * q, 4 * q + 4):
                    for j in range(2):
                        ins = fn(k2[0:HD, 2 * m + j, :], tile("uk", m)[HD * j:HD * (j + 1), :], ACT.Copy)
                    freed(ins)
                if q == 0:
                    split_high(BASE["uk"] + RING)
            attention(3, probs2, lambda h: split_high(BASE["uk"] + 1 + RING) if h == 3 else None)
            output_high(2)
            stage("wo2", lambda i: None, DT - LATE)
            norm(5)
            late_splits(BASE["ffn2"], LATE)
            feed_forward(2)
            norm(6)
            roots(6)

        @block.vector
        def _(dve):
            v = nc.vector
            steps = [0]

            def mark(ins):
                ins.then_inc(dve_step, 1)
                steps[0] += 1
                return steps[0]

            def link(ins):
                dve.wait_ge(dve_step, mark(ins))

            def split_low(c, i=None):
                if c >= N_CHUNKS:
                    return
                dve.wait_ge(high_ready, (0 if i is None else BODY * i) + c + 1)
                v.tensor_tensor(w_low[:, c % RING, :], w_raw[:, c % RAW, :], f(w_high[:, c % RING, :]),
                                ALU.subtract).then_inc(low_ready, 1)

            def stage(name, post, wait=True, count=None, then=None):
                for i in range(count or SIZE[name]):
                    c = BASE[name] + i
                    if wait:
                        dve.wait_ge(chunk_used, c + 1)
                    post(i)
                    split_low(c + RING)
                    if then:
                        then(i)

            def late_splits(end, count):
                for c in range(end - count, end):
                    split_low(c + RING)

            def tile(name, i):
                return bank[(TILE0[name] + i) % TILE_BANKS][:, 0:S]

            def low(dst, src, high, ready, n, done):
                dve.wait_ge(ready, n)
                v.tensor_tensor(dst, src, f(high), ALU.subtract).then_inc(done, 1)

            def norm(n):
                for p in range(5):
                    if p < 4 and n:
                        acc_bank_done(dve, n, p)
                        v.tensor_tensor(pieces(x, p), acc[p][:, :].rearrange("p (k t) -> p k t", k=2), pieces(x, p),
                                        ALU.add).then_inc(acc_read, 1)
                    if p < 4 and n == 0:
                        dve.wait_ge(x_loaded[p], 16)
                    if p and n < 6:
                        dve.wait_ge(h_high_ready, H_N[n] + p)
                        for k in (2 * p - 2, 2 * p - 1):
                            ins = v.scalar_tensor_tensor(h_low[:, k, :], x[:, k, :], par("norm", n * DT + k, 1),
                                                         f(h_high[:, k, :]), ALU.mult, ALU.subtract)
                        ins.then_inc(h_low_ready, 1)
                if n == 0:
                    split_low(1)
                for p, count in ((0, 2), (2, 4)):
                    dve.wait_ge(x_squared, 4 * n + count)
                    ins = v.tensor_tensor(pieces(squares, p), pieces(squares, p), pieces(squares, p + 1), ALU.add)
                    link(ins)
                v.tensor_tensor(pieces(squares, 0), pieces(squares, 0), pieces(squares, 2),
                                ALU.add).then_inc(squares_ready, 1)

            def inverse_roots(n):
                dve.wait_ge(std_ready, n + 1)
                if n in (0, 2):
                    v.reciprocal(rstd_col, std_col)
                v.reciprocal(rstd[:, :], rstd[:, :]).then_inc(rstd_ready, 1)
                dve.wait_ge(rstd_ready, n + 1)

            def scaled(dst, name, i):
                dve.wait_ge(chunk_used, BASE[name] + i + 1)
                v.tensor_tensor(dst, tile(name, i), rstd[:, :], ALU.mult).then_inc(tile_free["dve"], 1)

            def attention(n, o, probs_t, branch=None, before=None, after=None):
                def row_max(h):
                    dve.wait_ge(scores_ready, NH * n + h + 1)
                    b = bank[h % 3]
                    v.tensor_reduce(neg_max[:, h, 0:1], b[:, 0:P], AX.X, ALU.max, negate=True)
                    v.tensor_reduce(neg_max[:, h, 1:2], b[:, P:3 * P], AX.X, ALU.max, negate=True).then_inc(max_ready, 1)

                def copy_turned(h):
                    dve.wait_ge(probs_turned, NH * n + h + 1)
                    if h >= 2:
                        dve.wait_ge(pv_done, NH * n + h - 1)
                    v.tensor_copy(probs_t[:, h % 2, :], bank[3 + h % 2][:, 0:3 * P]).then_inc(probs_copied, 1)

                def output(g):
                    dve.wait_ge(pv_done, NH * n + 4 * g + 4)
                    w = weights_o[:, :, 4 * g:4 * g + 4]
                    link(v.reciprocal(w, sums[:, :, 4 * g:4 * g + 4]))
                    if branch is not None:
                        link(v.tensor_tensor(w, w, nsa_gate[:, :, 4 * g:4 * g + 4, branch], ALU.mult))
                    dst = o[:, :, 4 * g:4 * g + 4, :]
                    src = bank[5 + g % 2][:, :].rearrange("p (t h d) -> p t h d", t=TT, h=4)
                    wide = w.unsqueeze(3).to_broadcast([P, TT, 4, HD])
                    if branch is None:
                        v.tensor_tensor(dst, src, wide, ALU.mult).then_inc(o_read, 1)
                    else:
                        link(v.tensor_tensor(o_part, src, wide, ALU.mult))
                        v.tensor_tensor(dst, dst, o_part, ALU.add).then_inc(o_read, 1)

                for h in range(NH + 3):
                    if before:
                        before(h)
                    if h < NH:
                        row_max(h)
                    if 2 <= h < NH + 2:
                        copy_turned(h - 2)
                    if after:
                        after(h)
                    if h >= 3 and h % 4 == 2:
                        output((h - 3) // 4)

            def output_low(n):
                for p in range(DT // 2):
                    low(pieces(r_low, p), bank[p][:, :].rearrange("p (k t) -> p k t", k=2), pieces(r_high, p),
                        r_high_ready, R_O[n] + p + 1, r_low_ready)

            def feed_forward(n):
                base, s0, blocks, both = BASE[f"ffn{n}"], FFN_STEP0[n], FFN_BLOCKS[n], n == 0

                def tap(row, j):
                    at = AT[f"fcw{n}"][0] + row * blocks
                    return small[:, at + j:at + j + 1] if isinstance(j, int) else small[:, bass.ds(j + at, 1)]

                def back(dst, src, tokens, row, j):
                    return v.scalar_tensor_tensor(dst[:, tokens:S], src[:, 0:S - tokens], tap(row, j), dst[:, tokens:S],
                                                  ALU.mult, ALU.add)

                def hidden_low(j, k):
                    low(r_low[:, j % 2, :], hidden[:, j % 2, :], r_high[:, j % 2, :], hid_high,
                        k + (s0 + j + 1), hid_low)

                def step(j, c, i=None):
                    turn, k = (0, 0) if i is None else (BODY * i, 2 * i)
                    count, slot, end = k + (s0 + j + 1), j % 2, j == blocks - 1
                    dve.wait_ge(chunk_used, turn + c + 1)
                    if i is None and j == 0:
                        inverse_roots(2 * n + 1)
                    v.tensor_tensor(scaled_g[:, slot, :], bank[slot][:, 0:S], rstd[:, :], ALU.mult).then_inc(g_scaled, 1)
                    if j > 1:
                        hidden_low(j - 1, k)
                    if j:
                        split_low(c + RING, i)
                    dve.wait_ge(tap_g, count)
                    back(taps_g[:, slot, :], scaled_g[:, slot, :], 1, 1, k + j).then_inc(tap_g2, 1)
                    dve.wait_ge(chunk_used, turn + c + 2)
                    v.tensor_tensor(scaled_v[:, slot, :], bank[2 + slot][:, 0:S], rstd[:, :],
                                    ALU.mult).then_inc(v_scaled, 1)
                    dve.wait_ge(tap_g2, count)
                    back(taps_g[:, slot, :], scaled_g[:, slot, :], 2, 0, k + j).then_inc(conv_g, 1)
                    if j and not end:
                        split_low(c + 1 + RING, i)
                    if both:
                        dve.wait_ge(tap_v, count)
                        back(taps_v[:, slot, :], scaled_v[:, slot, :], 1, 4, k + j).then_inc(tap_v2, 1)
                        dve.wait_ge(tap_v2, count)
                        back(taps_v[:, slot, :], scaled_v[:, slot, :], 2, 3, k + j).then_inc(conv_v, 1)
                        dve.wait_ge(conv_v, count)
                    else:
                        dve.wait_ge(v_scaled, count)
                    value = (taps_v if both else scaled_v)[:, slot, :]
                    dve.wait_ge(gelu_ready, count)
                    v.tensor_tensor(hidden[:, slot, :], gelu_g[:, slot, :], value, ALU.mult).then_inc(hidden_ready, 1)
                    if end or j == 0:
                        hidden_low(j, k)
                    if 0 < j and not end:
                        split_low(c + 2 + RING, i)
                    if j == 0:
                        split_low(c + RING)
                        split_low(c + 1 + RING)

                step(0, base)
                step(1, base + 2)
                turns = (blocks - 3) // 2 - (n == 2)
                with dve.Fori(0, turns) as i:
                    for q in range(2):
                        step(2 + q, base + 5 + 3 * q, i)
                for j in range(2 + 2 * turns, blocks):
                    step(j, base + 3 * j - 1)

            dve.wait_ge(norm_loaded, 16)
            split_low(0)
            norm(0)
            for c in range(2, RING // 2):
                split_low(c)
            inverse_roots(0)
            for c in range(RING // 2, RING):
                split_low(c)
            dve.wait_ge(small_loaded, 16)
            z, s, s2, t = lru_t[1], lru_t[0], lru_t[2], lru_t[3]
            dve.wait_ge(act_step, 2)
            link(v.tensor_scalar(s2, z, 2.0, None, ALU.add))
            link(v.reciprocal(s, s2))
            link(v.tensor_tensor(s, s, z, ALU.mult))
            link(v.tensor_tensor(s2, s, s, ALU.mult))
            link(v.tensor_scalar(t, s2, 1.0 / 17, None, ALU.mult))
            for n in range(7, 0, -1):
                link(v.scalar_tensor_tensor(t, t, 1.0 / (2 * n + 1), s2, ALU.add, ALU.mult))
            link(v.scalar_tensor_tensor(t, t, 1.0, s, ALU.add, ALU.mult))
            link(v.tensor_scalar(s, par("lam"), -1.0, 0.0, ALU.mult, ALU.max))
            link(v.scalar_tensor_tensor(t, t, 2.0, s, ALU.mult, ALU.add))
            v.tensor_scalar(lru_kn, t, LRU_C, None, ALU.mult)
            v.tensor_scalar(lru_k, t, -LRU_C, None, ALU.mult)
            v.memset(windows.rearrange("p (j n) -> p j n", n=WIN)[:, :, 60:HD], 0.0)
            stage("kvc", lambda i: scaled(kv_scaled[:, i, :], "kvc", i))

            def window(which):
                dve.wait_ge(kv2_ready, 2 * which + 2)
                dst = windows.rearrange("p (j n) -> p j n", n=WIN)[:, :, HD * which:HD * which + 60]
                dst = dst.rearrange("p j (c g) -> p g j c", g=NKV)
                pos = par(("pek", "pev")[which]).unsqueeze(2).to_broadcast([P, CL // 2, NC])
                for g in range(NKV):
                    pairs = kv2[:, 4 * which + g, :].rearrange("p (n j) -> p j n", j=2)[:, 0, :]
                    for half in range(2):
                        src = pairs[:, 8 * half:8 * half + 8 * NC].rearrange("p (c j) -> p j c", j=8)
                        at = slice(8 * half, 8 * half + 8)
                        ins = v.tensor_tensor(dst[:, g, at, :], src, pos[:, at, :], ALU.add)
                ins.then_inc(windows_ready, 1)

            def rgate(i):
                if i in (1, 2):
                    window(i - 1)
                if i == 6:
                    flat = [r[:, :, :].rearrange("p k t -> p (k t)")[:, 0:CL // 2 * WIN] for r in (r_low, r_high)]
                    low(flat[0], windows, flat[1], r_high_ready, 1, r_low_ready)

            stage("rgate", lambda i: scaled(gelu_gate[:, i, :], "rgate", i), then=rgate)

            stage("w1", lambda i: None)

            def conv_low(i):
                low(r_low[:, i, :], conv[:, i, :], r_high[:, i, :], r_high_ready, R_CONV + i + 1, r_low_ready)

            def conv_tap(i, back):
                if back > 1:
                    dve.wait_ge(dve_step, conv_taps[i, back - 1])
                ins = v.scalar_tensor_tensor(conv[:, i, back:S], rx_scaled[:, i % 3, 0:S - back],
                                             par("rcw", (3 - back) * RT + i, 1), conv[:, i, back:S], ALU.mult, ALU.add)
                if back < 3:
                    conv_taps[i, back] = mark(ins)
                else:
                    ins.then_inc(conv_ready, 1)

            conv_taps = {}

            def rx_scale(i):
                scaled(rx_scaled[:, i % 3, :], "rx", i)
                if i:
                    conv_tap(i - 1, 2)

            def rx(i):
                if i:
                    conv_tap(i - 1, 3)
                dve.wait_ge(tap_ready, i + 1)
                conv_tap(i, 1)
                if i >= 2:
                    conv_low(i - 2)
                if i == 5:
                    dve.wait_ge(cmp_kv_ready, 1)
                    for r in range(4):
                        v.tensor_copy(cmp_v[32 * r:32 * r + 32, :, r * HD:(r + 1) * HD],
                                      acc[1][32 * r:32 * r + 32, 0:4 * HD].rearrange("p (g d) -> p g d", g=NKV))
                if i == 8:
                    dve.wait_ge(cmp_std_ready, 1)
                    v.reciprocal(cmp_rstd[0:60, :], cmp_std[0:60, :]).then_inc(cmp_rstd_ready, 1)

            stage("rx", rx_scale, then=rx)
            conv_tap(RT - 1, 2)
            conv_low(RT - 2)
            conv_tap(RT - 1, 3)
            conv_low(RT - 1)
            dve.wait_ge(cmp_spread, 1)
            for j in range(2):
                rows = slice(HD * j, HD * (j + 1))
                ins = v.tensor_tensor(cmp_k[rows, j, :], cmp_kraw[rows, :], acc[3][rows, 0:60], ALU.mult)
            ins.then_inc(head_normed, 1)
            inputs_marked = [0]

            def lru_input(t, gate, m):
                if gate == 1:
                    tile_read(dve, "lru", t)
                    inputs_marked[0] = mark(v.tensor_tensor(i_gate[:, m, :], i_gate[:, m, :], conv[:, m, :], ALU.mult))

            lru_posts(dve, split_low, lru_input)
            squared = []

            def variance(m):
                dve.wait_ge(dve_step, squared[m])
                v.scalar_tensor_tensor(conv[:, m, :], conv[:, m, :], 1.0, r_gate[:, m, :], ALU.add,
                                       ALU.mult).then_inc(var_ready, 1)

            def lru_step(e):
                if e < RT:
                    dve.wait_ge(decay_ready, e + 1)
                    squared.append(mark(v.tensor_tensor(conv[:, e, :], decay[:, e, :], decay[:, e, :], ALU.mult)))
                if e >= 1:
                    variance(e - 1)

            def heads(e):
                if e >= 2:
                    dve.wait_ge(head_sumsq_done, e - 1)
                name, i = ("k", e) if e < 4 else ("q", e - 4)
                scaled(head_sq[:, e % 2, :], name, i)
                tile_read(dve, name, i)
                if e < 4:
                    if e == 0:
                        dve.wait_ge(zeros_ready, 1)
                    branch, g = e // 2, 2 * (e % 2)
                    for j in range(2):
                        rows = slice(HD * j, HD * (j + 1))
                        ins = v.tensor_scalar(k0[rows, branch, j, g + j, :], head_sq[rows, e % 2, :],
                                              par("hg", 2 + branch, 1)[rows, :], None, ALU.mult)
                else:
                    ins = v.tensor_scalar(q0[:, e - 4, :], head_sq[:, e % 2, :], par("hg", 0, 1), None, ALU.mult)
                ins.then_inc(heads_scaled, 1)

            stage("k", heads, then=lru_step)
            stage("q", lambda i: heads(4 + i), then=lambda i: lru_step(4 + i))
            dve.wait_ge(dve_step, inputs_marked[0])
            driven, scanned = [], []
            for m in range(RT + 3):
                if m == 3:
                    dve.wait_ge(head_std_ready, 2)
                    v.reciprocal(stats[:, 148:196], stats[:, 100:148]).then_inc(head_rstd_ready, 1)
                if m < RT:
                    dve.wait_ge(scale_ready, m // 4 + 1)
                    driven.append(mark(v.tensor_tensor(conv[:, m, :], conv[:, m, :], i_gate[:, m, :], ALU.mult)))
                if 1 <= m <= RT:
                    dve.wait_ge(dve_step, driven[m - 1])
                    v.tensor_tensor_scan(r_gate[:, m - 1, :], decay[:, m - 1, :], conv[:, m - 1, :], 0.0, ALU.mult,
                                         ALU.add).then_inc(scan_ready, 1)
                if 2 <= m <= RT + 1:
                    dve.wait_ge(scan_ready, m - 1)
                    v.tensor_tensor(i_gate[:, m - 2, :], r_gate[:, m - 2, :], gelu_gate[:, m - 2, :],
                                    ALU.mult).then_inc(gated_ready, 1)
                if m >= 3:
                    low(r_low[:, m - 3, :], i_gate[:, m - 3, :], r_high[:, m - 3, :], r_high_ready,
                        R_SCAN + m - 2, r_low_ready)
                    if m % 2 and m < RT + 2:
                        c = BASE["v"] + (m - 3) // 2
                        split_low(c + RING)
            v.memset(cmp_p[:, :, :, :], 0.0)

            def normed_heads(e):
                dve.wait_ge(head_spread, e + 1)
                b = bank[e % TILE_BANKS][:, 0:S]
                if e >= 4:
                    ins = v.tensor_tensor(q0[:, e - 4, :], q0[:, e - 4, :], b, ALU.mult)
                else:
                    branch, g = e // 2, 2 * (e % 2)
                    for j in range(2):
                        own, other = slice(HD * j, HD * (j + 1)), slice(HD * (1 - j), HD * (2 - j))
                        v.tensor_tensor(k0[other, branch, 1 - j, g + j, :], k0[own, branch, j, g + j, :], b[own, :],
                                        ALU.mult)
                        ins = v.tensor_tensor(k0[own, branch, j, g + j, :], k0[own, branch, j, g + j, :], b[own, :],
                                              ALU.mult)
                ins.then_inc(head_normed, 1)

            stage("yr", normed_heads, wait=False)
            normed_heads(RT)

            def merge_scaled(i):
                dve.wait_ge(chunk_used, BASE["mg"] + i + 1)
                v.tensor_tensor(merge[:, i, :], mg_bank(i), rstd[:, :], ALU.mult).then_inc(mg_scaled, 1)

            merge_scaled(0)
            dve.wait_ge(cmp_scores, 1)
            src = bank[0][:, :].rearrange("p (t h c) -> p t h c", t=TT, h=NH)
            masks = par("cmpmask").rearrange("p (t c) -> p t c", t=TT)
            for t in range(TT):
                ins = v.tensor_tensor(cmp_s[:, t, :, :], src[:, t, :, 0:NC],
                                      masks[:, t, :].unsqueeze(1).to_broadcast([P, NH, NC]), ALU.add)
            link(ins)
            link(v.tensor_reduce(cmp_max, cmp_s, AX.X, ALU.max))
            for t in range(TT):
                ins = v.tensor_tensor(cmp_s[:, t, :, :], cmp_s[:, t, :, :],
                                      cmp_max[:, t, :].unsqueeze(2).to_broadcast([P, NH, NC]), ALU.subtract)
            ins.then_inc(cmp_shifted, 1)
            split_low(BASE["mg"] + RING)
            for i in (1, 2, 3):
                merge_scaled(i)
                split_low(BASE["mg"] + i + RING)
            dve.wait_ge(cmp_probs, 1)
            link(v.tensor_reduce(cmp_sum, cmp_p[:, :, :, 0:NC], AX.X, ALU.add))
            dve.wait_ge(cmp_turned, 1)
            v.tensor_copy(cmp_pt[:, 4:8, :], bank[2][:, :].rearrange("p (a b) -> p a b", a=4)).then_inc(cmp_copied, 1)
            link(v.reciprocal(cmp_max, cmp_sum))
            for t in range(TT):
                ins = v.scalar_tensor_tensor(weights_o[:, t, :], cmp_max[:, t, :], par("rowok", t, 1),
                                             nsa_gate[:, t, :, 0], ALU.mult, ALU.mult)
            link(ins)
            merge_scaled(4)
            split_low(BASE["mg"] + 4 + RING)
            for t in range(TT):
                dve.wait_ge(cmp_pv, t + 1)
                for half in range(2):
                    v.tensor_tensor(o0[:, t, 8 * half:8 * half + 8, :],
                                    bank[3 + 2 * t + half][:, :].rearrange("p (h d) -> p h d", h=8),
                                    weights_o[:, t, 8 * half:8 * half + 8].unsqueeze(2).to_broadcast([P, 8, HD]),
                                    ALU.mult).then_inc(cmp_done, 1)
            merge_scaled(5)
            split_low(BASE["mg"] + 5 + RING)
            dve.wait_ge(cmp_done, 4)

            def merge_gate(h, n):
                if mg_late(h, n) is not None:
                    merge_scaled(mg_late(h, n))

            def merge_split(h, n):
                if mg_late(h, n) is not None:
                    split_low(BASE["mg"] + mg_late(h, n) + RING)

            for n in range(2):
                if n:
                    dve.wait_ge(o_read, 4)
                attention(n, o0, probs_t0, branch=1 + n, before=lambda h: merge_gate(h, n),
                          after=lambda h: merge_split(h, n))
            output_low(0)

            def merge_low(i):
                low(h_low[:, i, :], y_rnn[:, i, :], h_high[:, i, :], h_high_ready, H_Z + i + 1, h_low_ready)

            def merged(i):
                dve.wait_ge(merge_gated, 3 + i // 4)
                v.tensor_tensor(merge[:, 8 + i, :], merge[:, 8 + i, :], tile("ao", i), ALU.mult).then_inc(tile_free["dve"], 1)
                link(v.tensor_tensor(merge[:, i, :], merge[:, i, :], y_rnn[:, i, :], ALU.mult))
                v.tensor_tensor(y_rnn[:, i, :], merge[:, i, :], merge[:, 8 + i, :], ALU.add).then_inc(z_ready, 1)
                if i:
                    merge_low(i - 1)

            stage("ao", merged)
            merge_low(DT - 1)
            stage("wo", lambda i: None, count=DT - LATE)
            norm(1)
            late_splits(BASE["ffn0"], LATE)
            feed_forward(0)

            norm(2)
            late_splits(BASE["v1"], 3)
            inverse_roots(2)
            v.tensor_tensor(c64r, par("c64"), rstd[:, :], ALU.mult)
            link(v.tensor_tensor(s64r, par("s64"), rstd[:, :], ALU.mult))
            stage("v1", lambda i: None)

            def rope(e):
                name, i = ("q1", e) if e < 8 else ("k1", e - 8)
                tile_read(dve, name, i)
                a, b = rope_a[:, e % 2, :], rope_b[:, e % 2, :]
                v.tensor_tensor(a, rope_in[:, e % 2, :], c64r, ALU.mult)
                dve.wait_ge(rope_turned, e + 1)
                link(v.tensor_tensor(b, acc[e % 2][:, 0:S], s64r, ALU.mult))
                if e < 8:
                    ins = v.tensor_tensor(q1[:, i, :], a, b, ALU.add)
                else:
                    for j in range(2):
                        rows = slice(HD * j, HD * (j + 1))
                        ins = v.tensor_tensor(k1[rows, j, i, :], a[rows, :], b[rows, :], ALU.add)
                ins.then_inc(rope_done, 1)

            stage("q1", lambda i: rope(i - 1) if i else None)
            stage("k1", lambda i: rope(i + 7))
            rope(15)
            attention(2, o1, probs_t1)
            output_low(1)
            stage("wo1", lambda i: None, count=DT - LATE)
            norm(3)
            late_splits(BASE["ffn1"], LATE)
            feed_forward(1)

            norm(4)
            late_splits(BASE["c2"], 3)
            inverse_roots(4)
            stage("c2", lambda i: scaled(c_raw[:, i, :], "c2", i))
            dve.wait_ge(c_std_ready, 1)
            v.reciprocal(c_rstd, c_std).then_inc(c_rstd_ready, 1)
            dve.wait_ge(c_spread, 1)
            for n in range(6):
                if n < 5:
                    e = LATENTS[n]
                    v.scalar_tensor_tensor(c_norm[:, e, :], c_raw[:, e, :], par("ln2", e, 1),
                                           spread_bank(int(e >= 3))[:, 0:S], ALU.mult, ALU.mult).then_inc(c_normed, 1)
                if n:
                    e = LATENTS[n - 1]
                    low(h_low[:, e, :], c_norm[:, e, :], h_high[:, e, :], h_high_ready, H_C + n, h_low_ready)
            stage("uv", lambda i: None)
            rows, other = slice(HD, HD + ROPE), slice(HD + ROPE, P)
            tile_read(dve, "c2", 5)
            v.tensor_tensor(rope_a2[rows, 0, 0:S], c_raw[rows, 5, :], par("c32")[rows, :], ALU.mult)
            link(v.tensor_tensor(rope_b2[rows, 0, 0:S], c_raw[other, 5, :], par("s32")[other, :], ALU.mult))
            v.tensor_tensor(c_raw[rows, 5, :], rope_a2[rows, 0, 0:S], rope_b2[rows, 0, 0:S], ALU.add).then_inc(rope_done, 1)

            def query_rope(e):
                a = rope_a2[rows, e % 2, :].rearrange("p (h t) -> p h t", h=2)
                b = rope_b2[rows, e % 2, :].rearrange("p (h t) -> p h t", h=2)
                tile_read(dve, "uq", 2 * e + 1)
                if e != 1:
                    dve.wait_ge(rope_done, 17 if e == 0 else 16 + e)
                v.tensor_tensor(a, q2[rows, 2 * e:2 * e + 2, :],
                                par("c32")[rows, :].unsqueeze(1).to_broadcast([ROPE, 2, S]), ALU.mult)
                link(v.tensor_tensor(b, q2[other, 2 * e:2 * e + 2, :],
                                     par("s32")[other, :].unsqueeze(1).to_broadcast([ROPE, 2, S]), ALU.mult))
                v.tensor_tensor(q2[rows, 2 * e:2 * e + 2, :], a, b, ALU.add).then_inc(rope_done, 1)

            ROPED_BEFORE = 5
            roped = 0
            for i in range(SIZE["uq"]):
                dve.wait_ge(chunk_used, BASE["uq"] + i + 1)
                split_low(BASE["uq"] + i + RING)
                while (3 * (2 * roped + 1) + 2) // 8 <= i and roped < ROPED_BEFORE:
                    query_rope(roped)
                    roped += 1

            def behind_maxima(h):
                if h % 2 == 1 and h // 2 + ROPED_BEFORE < 8:
                    query_rope(h // 2 + ROPED_BEFORE)
                elif h in (9, 11):
                    split_low(BASE["uk"] + (h - 9) // 2 + RING)

            attention(3, o2, probs_t2, after=behind_maxima)
            output_low(2)
            stage("wo2", lambda i: None, count=DT - LATE)
            norm(5)
            late_splits(BASE["ffn2"], LATE)
            feed_forward(2)
            norm(6)
            inverse_roots(6)
            for k in range(DT):
                ins = v.scalar_tensor_tensor(x_norm[:, k, :], x[:, k, :], par("norm", 6 * DT + k, 1), rstd[:, :],
                                             ALU.mult, ALU.mult)
                if k % 2:
                    ins.then_inc(norm_ready, 1)


def column_chunks(w, width=P):
    k, n = w.shape
    padded = np.zeros((k, -(-n // width) * width), w.dtype)
    padded[:, :n] = w
    return padded.reshape(k // P, P, -1, width).transpose(2, 1, 0, 3).reshape(-1, P, k // P * width)


def row_chunks(w):
    n, m = w.shape
    padded = np.zeros((-(-n // P) * P, m), w.dtype)
    padded[:n] = w
    return padded.reshape(-1, P, m)


def block_chunks(blocks):
    out = np.zeros((-(-len(blocks) // 8), P, 8, P), blocks[0].dtype)
    for n, b in enumerate(blocks):
        out[n // 8, :b.shape[0], n % 8, :b.shape[1]] = b
    return out.reshape(-1, P, D)


def ffn_chunks(gate, up, down):
    g, u, d = column_chunks(gate), column_chunks(up), row_chunks(down)
    order = [g[0], u[0]]
    for j in range(1, len(g)):
        order += [g[j], u[j], d[j - 1]]
    return np.stack(order + [d[-1]])


def lay_out_weights(a):
    w_in = a["w_in"]
    sizes = [D_RNN, D_RNN, NH * HD] + [KVW] * 6 + [3 * NH, D, D]
    cut = np.concatenate([[0], np.cumsum(sizes)])
    rx, rg, q, kc, vc, ks, vs, kw, vw, g, mr, ma = (w_in[:, cut[i]:cut[i + 1]] for i in range(12))
    full = []
    for w in (a["rg_w_a"], a["rg_w_x"]):
        band = np.zeros((RT * P, RT * P), w.dtype)
        for n in range(RNN_BLOCKS):
            band[n * BW:(n + 1) * BW, n * BW:(n + 1) * BW] = w[n]
        full.append(band)
    gates = [full[gate][k * P:(k + 1) * P, m * P:(m + 1) * P] for gate, m, k in GATES]
    qkv = a["a_w_qkv_2"][0]
    c2 = a["b_w_in_2"][0]
    uq = a["b_w_uq_2"][0].reshape(QL, NH, HD + ROPE)
    ukv = a["b_w_ukv_2"][0].reshape(KVL, NH, 2, HD)
    uk = ukv[:, :, 0, :].reshape(KVL, D)
    uv = ukv[:, :, 1, :].reshape(KVL, D)
    d0 = FF0
    swap = np.roll(np.arange(ROPE), ROPE // 2)
    parts = {
        "kvc": column_chunks(np.concatenate([kc, vc], 1)), "rgate": column_chunks(rg),
        "w1": np.stack([a[n].reshape(4, 4, P, P).transpose(0, 2, 1, 3) for n in ("cmp_w1_k", "cmp_w1_v")],
                       3).reshape(4, P, D),
        "rx": column_chunks(rx), "lru": block_chunks(gates),
        "v": np.concatenate([vs, vw], 1).reshape(4, 2, P, 512).transpose(0, 2, 1, 3).reshape(4, P, D),
        "g": column_chunks(g), "k": column_chunks(np.concatenate([ks, kw], 1)), "q": column_chunks(q),
        "yr": row_chunks(a["w_rnn_out"]), "mg": column_chunks(np.concatenate([mr, ma], 1)),
        "ao": column_chunks(a["w_attn_out"]), "wo": row_chunks(a["w_out"]),
        "ffn0": ffn_chunks(a["w_up"][:, :d0], a["w_up"][:, d0:], a["w_down"]),
        "q1": column_chunks(qkv[:, :D]), "k1": column_chunks(qkv[:, D:2 * D]), "v1": row_chunks(qkv[:, 2 * D:]),
        "wo1": row_chunks(a["a_w_o_2"][0]),
        "ffn1": ffn_chunks(a["ffn_w_gate_2"][0], a["ffn_w_up_2"][0], a["ffn_w_down_2"][0]),
        "c2": np.concatenate([column_chunks(c2[:, :QL + KVL]),
                              column_chunks(np.concatenate([c2[:, QL + KVL - HD:], c2[:, QL + KVL:][:, swap]], 1))]),
        "uq": block_chunks([np.concatenate([uq[k * P:(k + 1) * P, h], uq[k * P:(k + 1) * P, h, HD:][:, swap]], 1)
                            for h in range(NH) for k in range(3)]),
        "uk": block_chunks([uk[k * P:(k + 1) * P, m * P:(m + 1) * P] for m in range(8) for k in range(2)]),
        "uv": row_chunks(uv), "wo2": row_chunks(a["b_w_o_2"][0]),
        "ffn2": ffn_chunks(a["ffn_w_gate_2"][1], a["ffn_w_up_2"][1], a["ffn_w_down_2"][1]),
    }
    for name, n in STAGES:
        assert parts[name].shape == (n, P, D), (name, parts[name].shape)
    return np.concatenate([parts[name] for name, _ in STAGES])


def feature_tiles(v):
    padded = np.zeros(-(-v.shape[0] // P) * P, v.dtype)
    padded[:v.shape[0]] = v
    return padded.reshape(-1, P).T


def lay_out_small(a):
    out = np.zeros((P, N_SMALL), np.float32)

    def put(name, value):
        at, n = AT[name]
        out[:, at:at + n] = np.asarray(value).reshape(P, n)

    token, row = np.arange(S), np.arange(P)
    put("ident", np.eye(P))
    put("mask", np.where(row[None, :] <= row[:, None], 0.0, NEG))
    end = np.arange(NC) * CS + CL - 1
    t = np.arange(TT)[None, :] * P + row[:, None]
    put("cmpmask", np.where(end <= t[:, :, None], 0.0, NEG))
    put("rowok", t >= CL - 1)
    put("blk2", row[:, None] // HD == np.arange(2))
    put("ones", np.ones((P, 2)))
    put("eps", np.tile([EPS, HD * EPS], (P, 1)))
    for name, dim in (("64", HD), ("32", ROPE)):
        inv = (np.float32(10000.0) ** (-np.arange(0, dim, 2, dtype=np.float32) / np.float32(dim))).astype(np.float32)
        angle = (token.astype(np.float32)[None, :] * inv[:, None]).astype(np.float32)
        table = np.tile(angle, (P // (dim // 2), 1))
        put("c" + name, np.cos(table))
        put("s" + name, np.sin(table))
    half = ROPE // 2
    sines = out[:, AT["s32"][0]:AT["s32"][0] + S]
    sines[HD + ROPE:HD + ROPE + half] *= -1.0
    rot = np.zeros((P, P))
    for at in range(0, P, HD):
        for j in range(HD // 2):
            rot[at + HD // 2 + j, at + j] = -1.0
            rot[at + j, at + HD // 2 + j] = 1.0
    put("rot64", rot)
    norms = [a["norm1_g"], a["norm2_g"], a["norm_mix_2"][0], a["norm_ffn_2"][0], a["norm_mix_2"][1],
             a["norm_ffn_2"][1], a["norm_final_2"]]
    put("norm", np.concatenate([feature_tiles(g) for g in norms], 1))
    put("rcw", np.concatenate([feature_tiles(w) for w in a["rnn_conv_w"]], 1))
    for name, key in (("rcb", "rnn_conv_b"), ("rba", "rg_b_a"), ("rbx", "rg_b_x"), ("lam", "lru_lambda")):
        put(name, feature_tiles(a[key]))
    put("hg", np.stack([np.tile(a[n], 2) for n in ("q_norm_g", "k_cmp_norm_g", "k_slc_norm_g", "k_win_norm_g")], 1))
    for name, key in (("pek", "cmp_pe_k"), ("pev", "cmp_pe_v")):
        put(name, a[key].reshape(CL // 2, P).T)
    put("w2k", np.tile(a["cmp_w2_k"], (1, 2)))
    put("w2v", a["cmp_w2_v"])
    put("fcw0", np.concatenate([feature_tiles(w) for half in (slice(0, FF0), slice(FF0, None))
                                for w in a["ffn_conv_w"][:, half]], 1))
    put("fcb0", np.concatenate([feature_tiles(a["ffn_conv_b"][half]) for half in (slice(0, FF0), slice(FF0, None))], 1))
    for n in (1, 2):
        put(f"fcw{n}", np.concatenate([feature_tiles(w) for w in a["ffn_conv_w_2"][n - 1]], 1))
        put(f"fcb{n}", feature_tiles(a["ffn_conv_b_2"][n - 1]))
    put("ln2", np.concatenate([feature_tiles(a["b_q_norm_2"][0]), feature_tiles(a["b_kv_norm_2"][0])], 1))
    return out


def kernel(**inputs):
    import concourse.bacc as bacc
    from concourse.bass_utils import run_bass_kernel_spmd

    a = {name: np.asarray(value) for name, value in inputs.items()}
    arrays = {
        "weight_stream": lay_out_weights(a),
        "small_in": lay_out_small(a),
        "x_in": np.ascontiguousarray(a["x"][0].T.reshape(DT, P, S).transpose(1, 0, 2)),
    }
    nc = bacc.Bacc("TRN2", target_bir_lowering=False, num_devices=1)
    args = [nc.dram_tensor(n, v.shape, mybir.dt.from_np(v.dtype), kind="ExternalInput").ap() for n, v in arrays.items()]
    out = nc.dram_tensor("out", (P, DT, S), F32, kind="ExternalOutput").ap()
    build(nc, *args, out)
    r = run_bass_kernel_spmd(nc, [arrays], core_ids=[0])
    y = r.results[0]["out"]
    return np.ascontiguousarray(y.transpose(2, 1, 0).reshape(1, S, D))
```
